# Optimizing a Trainium2 kernel written in Bass

```python
import math
import jax, jax.numpy as jnp
from jax import lax
import numpy as np

D_MODEL = 1024
BATCH = 1
SEQ = 256
DEPTH = 2
DEC_BATCH = 8
DEC_SEQ = 1
PAST_LEN = 2048
PAGE_SIZE = 128

N_MIXERS = 2
N_GDN = (DEPTH + 1) // 2
N_SCONV = DEPTH // 2
GDN_DK = 128
GDN_DV = 128
GDN_HEADS = D_MODEL // GDN_DK
GDN_KEY_DIM = GDN_HEADS * GDN_DK
GDN_VAL_DIM = GDN_HEADS * GDN_DV
GDN_CONV_DIM = 2 * GDN_KEY_DIM + GDN_VAL_DIM
GDN_CONV_K = 4
GDN_CHUNK = 64
GDN_IN_DIM = GDN_CONV_DIM + GDN_VAL_DIM + 2 * GDN_HEADS
SC_WIDTH = 3
MOE_GROUPS = 4
MOE_PER_GROUP = 8
MOE_EXPERTS = MOE_GROUPS * MOE_PER_GROUP
MOE_TOPK = 2
MOE_FF = D_MODEL // 4
NORM_EPS = 1e-6
L2_EPS = 1e-6

kernel_name = 'hybrid_gdn_shortconv_hiermoe_step'

def rms_norm(x, g):
    xf = x.astype(jnp.float32)
    y = xf * lax.rsqrt(jnp.mean(xf * xf, axis=-1, keepdims=True) + NORM_EPS)
    return (y * g.astype(jnp.float32)).astype(x.dtype)

def l2_normalize(x):
    xf = x.astype(jnp.float32)
    return xf * lax.rsqrt(jnp.sum(xf * xf, axis=-1, keepdims=True) + L2_EPS)

def modulation(c, w_ada, b_ada):
    m = jax.nn.silu(c) @ w_ada + b_ada
    return jnp.split(m[:, None, :], 6, axis=-1)

def causal_depthwise_conv(x, buf, w):
    K = w.shape[0]
    L = x.shape[1]
    xp = jnp.concatenate([buf.astype(x.dtype), x], axis=1)
    y = xp[:, 0:L] * w[0]
    for j in range(1, K):
        y = y + xp[:, j:j + L] * w[j]
    return y, xp[:, L:]

def gated_delta_chunked(q, k, v, g, beta, s0):
    B, L, H, DK = k.shape
    DV = v.shape[-1]
    C = min(GDN_CHUNK, L)
    N = L // C

    def to_chunks(t):
        return jnp.moveaxis(t.reshape((B, N, C) + t.shape[2:]), 3, 2)

    qc, kc, vc = to_chunks(q), to_chunks(k), to_chunks(v)
    gc = jnp.cumsum(to_chunks(g), axis=-1)
    bc = to_chunks(beta)
    causal = jnp.tril(jnp.ones((C, C), dtype=bool))
    strict = jnp.tril(jnp.ones((C, C), dtype=bool), -1)
    diff = gc[..., :, None] - gc[..., None, :]
    decay = jnp.exp(jnp.where(causal, diff, -jnp.inf))
    kb = kc * bc[..., None]
    a_low = jnp.where(strict, jnp.einsum('bnhid,bnhjd->bnhij', kb, kc) * decay, 0.0)
    t_mat = a_low + jnp.eye(C, dtype=a_low.dtype)
    rhs = jnp.concatenate([vc * bc[..., None], kb * jnp.exp(gc)[..., None]], axis=-1)
    sol = lax.linalg.triangular_solve(t_mat, rhs, left_side=True, lower=True, unit_diagonal=True)
    u, w = sol[..., :DV], sol[..., DV:]
    attn_intra = jnp.einsum('bnhid,bnhjd->bnhij', qc, kc) * decay

    def step(S, inp):
        q_i, k_i, u_i, w_i, g_i, a_i = inp
        v_new = u_i - jnp.einsum('bhcd,bhde->bhce', w_i, S)
        o = (jnp.einsum('bhcd,bhde->bhce', q_i * jnp.exp(g_i)[..., None], S)
             + jnp.einsum('bhij,bhje->bhie', a_i, v_new))
        g_last = g_i[..., -1:]
        S = (S * jnp.exp(g_last)[..., None]
             + jnp.einsum('bhcd,bhce->bhde', k_i * jnp.exp(g_last - g_i)[..., None], v_new))
        return S, o

    xs = tuple(jnp.moveaxis(t, 1, 0) for t in (qc, kc, u, w, gc, attn_intra))
    S, o = lax.scan(step, s0.astype(jnp.float32), xs)
    o = jnp.moveaxis(jnp.moveaxis(o, 0, 1), 2, 3).reshape(B, L, H, DV)
    return o, S

def gated_delta_recurrent(q, k, v, g, beta, s0):
    def step(S, inp):
        q_t, k_t, v_t, g_t, b_t = inp
        S = S * jnp.exp(g_t)[..., None, None]
        v_err = v_t - jnp.einsum('bhd,bhde->bhe', k_t, S)
        S = S + jnp.einsum('bhd,bhe->bhde', k_t, v_err * b_t[..., None])
        o = jnp.einsum('bhd,bhde->bhe', q_t, S)
        return S, o

    xs = tuple(jnp.moveaxis(t, 1, 0) for t in (q, k, v, g, beta))
    S, o = lax.scan(step, s0.astype(jnp.float32), xs)
    return jnp.moveaxis(o, 0, 1), S

def gdn_mixer(h, conv_buf, s0, w_in, conv_w, a_log, dt_bias, norm_g, w_out, chunked):
    B, L, _ = h.shape
    proj = h @ w_in
    splits = [GDN_CONV_DIM, GDN_CONV_DIM + GDN_VAL_DIM, GDN_CONV_DIM + GDN_VAL_DIM + GDN_HEADS]
    qkv, z, b_raw, a_raw = jnp.split(proj, splits, axis=-1)
    qkv, new_buf = causal_depthwise_conv(qkv, conv_buf, conv_w)
    qkv = jax.nn.silu(qkv)
    q, k, v = jnp.split(qkv, [GDN_KEY_DIM, 2 * GDN_KEY_DIM], axis=-1)
    q = l2_normalize(q.reshape(B, L, GDN_HEADS, GDN_DK)) * (GDN_DK ** -0.5)
    k = l2_normalize(k.reshape(B, L, GDN_HEADS, GDN_DK))
    v = v.reshape(B, L, GDN_HEADS, GDN_DV).astype(jnp.float32)
    beta = jax.nn.sigmoid(b_raw.astype(jnp.float32))
    g = -jnp.exp(a_log.astype(jnp.float32)) * jax.nn.softplus(a_raw.astype(jnp.float32) + dt_bias.astype(jnp.float32))
    if chunked:
        o, S = gated_delta_chunked(q, k, v, g, beta, s0)
    else:
        o, S = gated_delta_recurrent(q, k, v, g, beta, s0)
    o = rms_norm(o, norm_g) * jax.nn.silu(z.reshape(B, L, GDN_HEADS, GDN_DV).astype(jnp.float32))
    o = o.reshape(B, L, GDN_VAL_DIM).astype(h.dtype)
    return o @ w_out, new_buf, S.astype(s0.dtype)

def sconv_mixer(h, conv_buf, w_in, conv_w, w_out):
    gate_b, gate_c, xv = jnp.split(h @ w_in, 3, axis=-1)
    y, new_buf = causal_depthwise_conv(gate_c * xv, conv_buf, conv_w)
    return (gate_b * y) @ w_out, new_buf

def hier_moe(h, w_group, b_group, w_router, b_router, w_gate, w_up, w_down):
    B, L, D = h.shape
    t = h.reshape(-1, D)
    grp_prob = jax.nn.softmax((t @ w_group + b_group).astype(jnp.float32), axis=-1)
    grp_p, grp_idx = lax.top_k(grp_prob, 1)
    exp_logits = (t @ w_router + b_router).astype(jnp.float32).reshape(-1, MOE_GROUPS, MOE_PER_GROUP)
    sel_logits = jnp.einsum('tge,tg->te', exp_logits, jax.nn.one_hot(grp_idx[:, 0], MOE_GROUPS, dtype=jnp.float32))
    top_p, top_idx = lax.top_k(jax.nn.softmax(sel_logits, axis=-1), MOE_TOPK)
    top_p = top_p / jnp.sum(top_p, axis=-1, keepdims=True)
    weights = grp_p * top_p
    flat_idx = grp_idx * MOE_PER_GROUP + top_idx
    combine = jnp.einsum('tk,tke->te', weights, jax.nn.one_hot(flat_idx, MOE_EXPERTS, dtype=jnp.float32))
    hid = jax.nn.silu(jnp.einsum('td,edf->tef', t, w_gate)) * jnp.einsum('td,edf->tef', t, w_up)
    hid = hid * combine[:, :, None].astype(hid.dtype)
    y = jnp.einsum('tef,efd->td', hid, w_down)
    return y.reshape(B, L, D)

def run_trunk(x, c, gdn_S, gdn_buf, sc_buf, W, chunked):
    new_S, new_gbuf, new_sbuf = [], [], []
    for i in range(DEPTH):
        sh_m, sc_m, gt_m, sh_f, sc_f, gt_f = modulation(c, W['w_ada'][i], W['b_ada'][i])
        h = rms_norm(x, W['norm_mix_g'][i]) * (1.0 + sc_m) + sh_m
        j = i // N_MIXERS
        if i % N_MIXERS == 0:
            y, buf, S = gdn_mixer(h, gdn_buf[j], gdn_S[j], W['gdn_w_in'][j], W['gdn_conv_w'][j],
                                  W['gdn_A_log'][j], W['gdn_dt_bias'][j], W['gdn_norm_g'][j],
                                  W['gdn_w_out'][j], chunked)
            new_gbuf.append(buf)
            new_S.append(S)
        else:
            y, buf = sconv_mixer(h, sc_buf[j], W['sc_w_in'][j], W['sc_conv_w'][j], W['sc_w_out'][j])
            new_sbuf.append(buf)
        x = x + gt_m * y
        h = rms_norm(x, W['norm_ffn_g'][i]) * (1.0 + sc_f) + sh_f
        x = x + gt_f * hier_moe(h, W['moe_w_group'][i], W['moe_b_group'][i], W['moe_w_router'][i],
                                W['moe_b_router'][i], W['moe_w_gate'][i], W['moe_w_up'][i], W['moe_w_down'][i])
    x = rms_norm(x, W['norm_final_g'])
    return x, jnp.stack(new_S), jnp.stack(new_gbuf), jnp.stack(new_sbuf)

def setup_inputs(seed: int = 0) -> dict:
    key = jax.random.key(seed)
    ks = jax.random.split(key, 32)
    f32 = jnp.float32
    D = D_MODEL

    def nrm(k, shape, scale):
        return jax.random.normal(k, shape, f32) * scale

    A = jax.random.uniform(ks[14], (N_GDN, GDN_HEADS), f32, 1.0, 16.0)
    dt = jnp.exp(jax.random.uniform(ks[15], (N_GDN, GDN_HEADS), f32, math.log(1e-3), math.log(1e-1)))
    return {
        'x_prompt': nrm(ks[0], (BATCH, SEQ, D), 1.0),
        'x_sample': nrm(ks[1], (DEC_BATCH, DEC_SEQ, D), 1.0),
        'state_gdn_S': nrm(ks[2], (N_GDN, DEC_BATCH, GDN_HEADS, GDN_DK, GDN_DV), GDN_DK ** -0.5),
        'state_gdn_conv': nrm(ks[3], (N_GDN, DEC_BATCH, GDN_CONV_K - 1, GDN_CONV_DIM), 1.0),
        'state_sconv': nrm(ks[4], (N_SCONV, DEC_BATCH, SC_WIDTH - 1, D), 1.0),
        'c_prompt': nrm(ks[5], (BATCH, D), 1.0),
        'c_sample': nrm(ks[6], (DEC_BATCH, D), 1.0),
        'norm_mix_g': 1.0 + nrm(ks[7], (DEPTH, D), 0.05),
        'norm_ffn_g': 1.0 + nrm(ks[8], (DEPTH, D), 0.05),
        'norm_final_g': 1.0 + nrm(ks[9], (D,), 0.05),
        'w_ada': nrm(ks[10], (DEPTH, D, 6 * D), 0.5 * D ** -0.5),
        'b_ada': nrm(ks[11], (DEPTH, 6 * D), 0.01),
        'gdn_w_in': nrm(ks[12], (N_GDN, D, GDN_IN_DIM), D ** -0.5),
        'gdn_conv_w': nrm(ks[13], (N_GDN, GDN_CONV_K, GDN_CONV_DIM), GDN_CONV_K ** -0.5),
        'gdn_A_log': jnp.log(A),
        'gdn_dt_bias': dt + jnp.log(-jnp.expm1(-dt)),
        'gdn_norm_g': 1.0 + nrm(ks[16], (N_GDN, GDN_DV), 0.05),
        'gdn_w_out': nrm(ks[17], (N_GDN, GDN_VAL_DIM, D), GDN_VAL_DIM ** -0.5),
        'sc_w_in': nrm(ks[18], (N_SCONV, D, 3 * D), D ** -0.5),
        'sc_conv_w': nrm(ks[19], (N_SCONV, SC_WIDTH, D), SC_WIDTH ** -0.5),
        'sc_w_out': nrm(ks[20], (N_SCONV, D, D), D ** -0.5),
        'moe_w_group': nrm(ks[21], (DEPTH, D, MOE_GROUPS), D ** -0.5),
        'moe_b_group': nrm(ks[22], (DEPTH, MOE_GROUPS), 0.01),
        'moe_w_router': nrm(ks[23], (DEPTH, D, MOE_EXPERTS), D ** -0.5),
        'moe_b_router': nrm(ks[24], (DEPTH, MOE_EXPERTS), 0.01),
        'moe_w_gate': nrm(ks[25], (DEPTH, MOE_EXPERTS, D, MOE_FF), D ** -0.5),
        'moe_w_up': nrm(ks[26], (DEPTH, MOE_EXPERTS, D, MOE_FF), D ** -0.5),
        'moe_w_down': nrm(ks[27], (DEPTH, MOE_EXPERTS, MOE_FF, D), MOE_FF ** -0.5),
    }

def reference(x_prompt, x_sample, state_gdn_S, state_gdn_conv, state_sconv, c_prompt, c_sample,
              norm_mix_g, norm_ffn_g, norm_final_g, w_ada, b_ada,
              gdn_w_in, gdn_conv_w, gdn_A_log, gdn_dt_bias, gdn_norm_g, gdn_w_out,
              sc_w_in, sc_conv_w, sc_w_out,
              moe_w_group, moe_b_group, moe_w_router, moe_b_router, moe_w_gate, moe_w_up, moe_w_down):
    W = {
        'norm_mix_g': norm_mix_g, 'norm_ffn_g': norm_ffn_g, 'norm_final_g': norm_final_g,
        'w_ada': w_ada, 'b_ada': b_ada,
        'gdn_w_in': gdn_w_in, 'gdn_conv_w': gdn_conv_w, 'gdn_A_log': gdn_A_log,
        'gdn_dt_bias': gdn_dt_bias, 'gdn_norm_g': gdn_norm_g, 'gdn_w_out': gdn_w_out,
        'sc_w_in': sc_w_in, 'sc_conv_w': sc_conv_w, 'sc_w_out': sc_w_out,
        'moe_w_group': moe_w_group, 'moe_b_group': moe_b_group, 'moe_w_router': moe_w_router,
        'moe_b_router': moe_b_router, 'moe_w_gate': moe_w_gate, 'moe_w_up': moe_w_up,
        'moe_w_down': moe_w_down,
    }
    B = x_prompt.shape[0]
    s0_p = jnp.zeros((N_GDN, B, GDN_HEADS, GDN_DK, GDN_DV), state_gdn_S.dtype)
    gbuf0_p = jnp.zeros((N_GDN, B, GDN_CONV_K - 1, GDN_CONV_DIM), state_gdn_conv.dtype)
    sbuf0_p = jnp.zeros((N_SCONV, B, SC_WIDTH - 1, D_MODEL), state_sconv.dtype)
    y_prompt, gdn_S_prompt, gdn_conv_prompt, sconv_prompt = run_trunk(
        x_prompt, c_prompt, s0_p, gbuf0_p, sbuf0_p, W, True)
    y_sample, gdn_S_sample, gdn_conv_sample, sconv_sample = run_trunk(
        x_sample, c_sample, state_gdn_S, state_gdn_conv, state_sconv, W, False)
    return (y_prompt, y_sample, gdn_S_prompt, gdn_conv_prompt, sconv_prompt,
            gdn_S_sample, gdn_conv_sample, sconv_sample)


_drawn_inputs = setup_inputs


def setup_inputs(seed=0):
    import zlib

    import numpy as np

    out = dict(_drawn_inputs(seed))
    spreads = {}
    factors = {'gdn_norm_g': 3.124, 'moe_b_group': 5.567, 'moe_b_router': 8.0}
    for name, (base, spread) in spreads.items():
        noise = np.random.default_rng([zlib.crc32(name.encode()), seed]).standard_normal(out[name].shape)
        drawn = base * np.exp(spread * noise) if base else spread * noise
        out[name] = __import__('jax').numpy.asarray(drawn.astype(out[name].dtype))
    for name, factor in factors.items():
        out[name] = (out[name] * factor).astype(out[name].dtype)
    return out
```

```python
from contextlib import ExitStack

import concourse.bass as bass
from concourse import mybir

F32 = mybir.dt.float32
I32 = mybir.dt.int32
U32 = mybir.dt.uint32
ALU = mybir.AluOpType
ACT = mybir.ActivationFunctionType
AX = mybir.AxisListType

P = 128


def hybrid_step(nc, A, O):
    (y_prompt, y_sample, S_prompt_out, conv_prompt_out, sconv_prompt_out,
     S_sample_out, conv_sample_out, sconv_sample_out) = O
    SEQ, D = A["x_prompt"].shape[1:]
    NB = A["x_sample"].shape[0]
    DT = D // P
    H = A["state_gdn_S"].shape[2]
    QT = A["gdn_conv_w"].shape[2] // P
    NCH = SEQ // P
    TOK = SEQ + NB
    MODS = 1 + NB
    KC = A["gdn_conv_w"].shape[1]
    KS = A["sc_conv_w"].shape[1]
    NG = A["moe_w_group"].shape[2]
    NE = A["moe_w_router"].shape[2]
    PG = NE // NG
    FF = A["moe_w_gate"].shape[3]
    ADA = 6 * D // 512
    CAP = P
    HALF = CAP // 2
    MAXPASS = -(-TOK // CAP)
    EPS = 1e-6
    NM = NCH * H
    NQ = NM // 4
    LEVELS = P.bit_length() - 1
    PART = {"sh_m": 0, "sc_m": 1, "gt_m": 2, "sh_f": 3, "sc_f": 4, "gt_f": 5}

    with ExitStack() as ctx:
        def sb(name, shape, dt=F32):
            return ctx.enter_context(nc.sbuf_tensor(name, shape, dt))

        sems = {}

        def S(name):
            if name not in sems:
                sems[name] = ctx.enter_context(nc.semaphore(name))
            return sems[name]

        class Link:

            def __init__(self, eng, name):
                self.eng, self.sem, self.n = eng, S(name), 0

            def __call__(self, ins):
                self.n += 1
                ins.then_inc(self.sem, 1)
                self.eng.wait_ge(self.sem, self.n)

        xT = sb("xT", [P, DT, TOK])
        hT = sb("hT", [P, DT, TOK])
        ident = sb("ident", [P, P])
        ones = sb("ones", [P, P])
        causal = sb("causal", [P, P])
        strict = sb("strict", [P, P])
        slot_iota = sb("slot_iota", [P, P])
        vecT = sb("vecT", [P, 3, P])
        cT = sb("cT", [P, DT, 32])
        mT = sb("mT", [P, 2, 6 * DT, MODS])
        gain = sb("gain", [P, DT, MODS])
        w_route = sb("w_route", [P, 2, DT, NG + NE])
        b_route = sb("b_route", [P, 2, NG + NE])
        w_ba = sb("w_ba", [P, DT, 40])
        decay_w = sb("decay_w", [P, 4])
        epsc = sb("epsc", [P, 4])
        rstd = sb("rstd", [P, TOK])
        sc_state = sb("sc_state", [P, DT, 2 * NB])
        x_new = sb("x_new", [P, DT, NB])
        passes = sb("passes", [P, 2], I32)
        small_i = sb("small_i", [P, 2, MAXPASS * NG], I32)
        small_f = sb("small_f", [P, MAXPASS, NG])
        count = sb("count", [P, NG])
        upper = sb("upper", [P, P])
        ada_row = sb("ada_row", [P, 512])
        ada_sum = sb("ada_sum", [P, 4, MODS])
        NSTAT, NRING = 3, 6
        ring_lo = sb("ring_lo", [P, NSTAT, DT * 512])
        ARENA = 28992
        arena = sb("arena", [P, ARENA])
        slots = [ring_lo[:, s, :] for s in range(NSTAT)] + \
                [arena[:, s * 4096:(s + 1) * 4096] for s in range(NRING - NSTAT)]

        class Area:

            def __init__(self, at):
                self.at = at

            def take(self, *dims):
                n = 1
                for d in dims:
                    n *= d
                v = arena[:, self.at:self.at + n]
                self.at += n
                assert self.at <= ARENA, self.at
                if len(dims) == 1:
                    return v
                names = "abcd"[:len(dims)]
                return v.rearrange(f"p ({' '.join(names)}) -> p {' '.join(names)}",
                                   **{k: d for k, d in zip(names[1:], dims[1:])})

        g = Area(0)
        cv = g.take(QT, TOK)
        zs = g.take(H, TOK)
        AT = g.take(NM, P)
        intraT = g.take(NM, P)
        eg = g.take(H, P + NB)
        vb = g.take(NM, P)
        kdec = g.take(NM, P)
        kbg = g.take(H, P)
        vnew = g.take(H, P)
        S1 = g.take(H, P)
        work = g.at
        X = g.take(NM, P)
        PX = g.take(NM, P)
        BT = g.take(NM, P)
        XT = g.take(NM, P)
        g = Area(work)
        pre = g.take(QT, KC - 1 + SEQ)
        preS = g.take(QT, NB, KC)
        g = Area(work)
        decM = g.take(NCH, H, P)
        decB = g.take(NCH, H, P)
        g = Area(work)
        Ss = g.take(NB * H, P)
        wT = AT[:, 0:H, :]
        vnew1 = AT[:, H:NM, :]
        S2 = kbg
        levels = sb("levels", [P, LEVELS, P])
        small_iota = levels[:, 0:NG, :]
        e = Area(QT * TOK + H * TOK)
        x_rows = e.take(NCH, D)
        xs_rows = e.take(D)
        c_rows = e.take(D)
        vec_rows = e.take(3, P)
        sc_rows = e.take(D)
        cs_rows = e.take(QT * P)
        convtmp = e.take(QT, NB, KC)
        assert e.at <= work
        e = Area(QT * TOK + H * TOK)
        sqb = e.take(4, TOK)
        rno = e.take(H, TOK)
        e = Area(work)
        rnb = e.take(2 * H, TOK)
        e = Area(QT * TOK + H * TOK)
        slots += [e.take(DT * 512) for _ in range(2)]
        tail = e.take(QT, 3 + NB)
        e2 = Area(QT * TOK + H * TOK + 2 * NM * P + H * (P + NB) + 2 * NM * P)
        tail_rows = e2.take(QT * P)
        smT = sb("smT", [40, TOK])
        ba = sb("ba", [40, TOK])
        bb = sb("bb", [40, TOK])
        bc = sb("bc", [40, TOK])
        colv = sb("colv", [P, NCH, 40])
        lastg = sb("lastg", [P, H, NCH])
        kd = sb("kd", [P, NCH, H])
        kb1 = sb("kb1", [P, H])
        betaS = sb("betaS", [P, H, NB])
        Rs = vb[:, 0, :].rearrange("p (r c) -> p r c", c=2)
        kS = vb[:, 1, 0:NB * H].rearrange("p (h b) -> p h b", h=H)
        qkS = vb[:, 1, NB * H:2 * NB * H].rearrange("p (h b) -> p h b", h=H)
        verr = vb[:, 2, 0:NB * H].rearrange("p (h b) -> p h b", h=H)
        k_rows = vb[:, 3, :]
        v_rows = vb[:, 4, :]
        spread = vb[:, 8:16, :].rearrange("p (t r) c -> p t r c", t=2)

        m = Area((NRING - NSTAT) * 4096)
        hg = m.take(DT, NG * CAP)
        sqx = hg[:, 0:DT, 0:TOK]
        hcur = m.take(DT, CAP)
        ysb = m.take(NG, D)
        htok = m.take(3, D)
        Pm = m.take(3, NG, CAP)
        sg = m.take(2, FF)
        hid = m.take(2, FF)
        hidT = m.take(2, 2, CAP)
        PT = m.take(NG, TOK)
        lg = sb("lg", [NG + NE, 3 * P])
        lt = sb("lt", [P, 3, NG + NE])
        r4 = sb("r4", [P, 3, NG])
        oh = sb("oh", [P, 3, NG])
        r8 = sb("r8", [P, 3, 4, PG])
        mx8 = sb("mx8", [P, 3, 8])
        ix8 = sb("ix8", [P, 3, 8], U32)
        ixf = sb("ixf", [P, 3, 8])
        r1 = sb("r1", [P, 8, 3])
        cmb = sb("cmb", [P, NG * PG])
        ccur = sb("ccur", [P, PG])
        c = Area((NRING - NSTAT) * 4096)
        gateb = c.take(DT, TOK)
        gatec = c.take(DT, TOK)
        up = c.take(DT, KS - 1 + SEQ)
        upS = c.take(DT, NB, KS)
        uptmp = c.take(DT, NB, KS)
        tail2 = c.take(DT, 2 + NB)
        tail2_rows = c.take(D)
        c = Area(0)
        y_rows = c.take(NCH, D)
        ys_rows = c.take(D)

        banks = [ctx.enter_context(nc.psum_tensor(f"bank{i}", [P, 512], F32)) for i in range(8)]

        order = []

        def tiles(*names, by):
            order.extend((n, by) for n in names)

        tiles("c", by="A")
        tiles("xs", "x0", "x1", "x2", "x3", by="D")
        tiles("vec", by="A")
        tiles("cs0", "cs1", "sc", by="D")

        ada_first = [(0, i) for i in range(2 * DT * P // 512)]
        ada_later = [(l, i) for l in range(2) for i in range(ADA) if (l, i) not in ada_first]
        WIN = (QT + H) // 4
        ada_after = [ada_later[len(ada_later) * j // WIN:len(ada_later) * (j + 1) // WIN] for j in range(WIN)]

        def ada_tiles(pieces):
            for n, (l, i) in enumerate(pieces):
                tiles(f"ada{l}_{i}", by="A")
                if n:
                    tiles("adaT%d_%d" % pieces[n - 1], by="D")
            tiles("adaT%d_%d" % pieces[-1], by="D")

        ada_tiles(ada_first)
        tiles("ss0", by="A")
        tiles("ba", by="D")
        for j in range(WIN):
            tiles(*[f"in{i}" for i in range(4 * j, 4 * j + 4)], by="A")
            ada_tiles(ada_after[j])
        tiles(*[f"cb{i}" for i in range(QT // 4)], by="A")
        tiles(*[f"l2_{i}" for i in range(2 * H)], by="A")
        tiles("smx", by="D")
        tiles(*[f"gr{h}" for h in range(H)], by="D")
        tiles(*[f"br{h}" for h in range(H)], by="D")
        tiles(*[f"kk{q}" for q in range(NQ)], by="D")
        tiles(*[f"qk{q}" for q in range(NQ)], by="D")
        tiles(*[f"vt{q}" for q in range(NQ)], by="D")
        tiles(*[f"kt{q}" for q in range(NQ)], by="D")
        tiles(*[f"xt{q}" for q in range(NQ)], by="A")
        for L in range(1, LEVELS):
            tiles(*[f"P{L}_{q}" for q in range(NQ)], by="A")
            for q in range(NQ):
                tiles(f"T{L}_{q}", by="D")
                if L < LEVELS - 1:
                    tiles(f"Q{L}_{q}", by="D")
        for q in range(2):
            tiles(f"u0_{q}", by="A")
        for q in range(2):
            tiles(f"s1_{q}", by="D")
        for q in range(2):
            tiles(f"o0_{q}", by="A")
        for q in range(2):
            tiles(f"w_{q}", by="A")
        for q in range(2):
            tiles(f"u1_{q}", by="A")
        for q in range(2):
            tiles(f"o1_{q}", by="A")
        for q in range(2):
            tiles(f"s2_{q}", by="D")
        tiles("R", "qkS", by="D")
        tiles("rw", by="A")
        tiles(*[f"ou{t}" for t in range(NB * H // 4)], by="D")
        tiles(*[f"on{h}" for h in range(H)], by="A")
        tiles(*[f"wo{i}" for i in range(DT)], by="D")
        for l in range(2):
            if l == 1:
                tiles("ss2", by="A")
                tiles(*[f"sg{i}" for i in range(2 * DT)], by="A")
                tiles(*[f"sg{i}" for i in range(2 * DT, 3 * DT)], by="D")
                tiles(*[f"st{i}" for i in range(DT // 4)], by="A")
                tiles(*[f"so{i}" for i in range(DT)], by="D")
            tiles(f"ss{2 * l + 1}", by="A")
            tiles(f"lg{l}", f"lgT{l}", f"cum{l}", by="D")
            tiles(*[f"ht{l}_{i}" for i in range(6)], by="A")
        tiles("ss4", by="A")
        tiles(*[f"y{i}" for i in range(6)], by="A")

        place = {n: i for i, (n, _) in enumerate(order)}
        upto = {e: [0] for e in "AD"}
        for _, by in order:
            for e_ in "AD":
                upto[e_].append(upto[e_][-1] + (e_ in by))
        emptied = {"A": S("bank_emptied_by_scalar"), "D": S("bank_emptied_by_vector")}
        bank_full = S("bank_full")

        def bank_of(name):
            return banks[place[name] % 8]

        def scatter_bank(l, t):
            return banks[(place[f"ss{2 * l + 2}"] + t) % 8]

        def claim(pe, name):
            i = place[name]
            if i >= 8:
                for e_ in order[i - 8][1]:
                    pe.wait_ge(emptied[e_], upto[e_][i - 7])
            return banks[i % 8]

        def full(eng, name):
            eng.wait_ge(bank_full, place[name] + 1)
            return bank_of(name)

        wa, wi = A["w_ada"], A["gdn_w_in"]
        col512 = lambda w, c_: w[:, c_ * 512:(c_ + 1) * 512].rearrange("(t p) n -> p t n", p=P)
        stream = [(f"ada{l}", i, col512(wa[l], i)) for l, i in ada_first]
        for j in range(WIN):
            stream += [("win", j, col512(wi[0], j))] + [(f"ada{l}", i, col512(wa[l], i)) for l, i in ada_after[j]]
        stream += [("wout", i, col512(A["gdn_w_out"][0], i)) for i in range(D // 512)]
        early = len(stream)
        stream += [("scin", i, col512(A["sc_w_in"][0], i)) for i in range(3 * D // 512)]
        stream += [("scout", i, col512(A["sc_w_out"][0], i)) for i in range(D // 512)]
        EARLY_SLOTS = [0, 1, 2, NRING, NRING + 1]
        FIRST_SLOT = [NSTAT, NSTAT, (NSTAT + len(stream) - early) % NRING]
        moe_slot = lambda l, f: (f + FIRST_SLOT[2 * l]) % NRING
        where, uses = {}, [0] * len(slots)
        for n, (kind, i, _) in enumerate(stream):
            if kind == "wout":
                s = i
            elif n < early:
                s = EARLY_SLOTS[n % len(EARLY_SLOTS)]
            else:
                s = (n - early + FIRST_SLOT[1]) % NRING
            where[kind, i] = (s, uses[s])
            uses[s] += 1
        release, in_slot = {}, {}
        for n, (kind, i, _) in enumerate(stream):
            if kind.startswith("ada"):
                release[kind, i] = (bank_full, place[f"{kind}_{i}"] + 1)
            else:
                last_tile = {"win": "in", "wout": "wo", "scin": "sg", "scout": "so"}[kind]
                release[kind, i] = (bank_full, place[f"{last_tile}{4 * i + 3}"] + 1)
            in_slot[where[kind, i]] = (kind, i)
        last_early = [max(n for n in range(early) if where[stream[n][0:2]][0] == s) for s in range(NSTAT)]
        filled = [S(f"slot_filled{s}") for s in range(len(slots))]
        moe_filled = [[S(f"moe_filled{l}_{s}") for s in range(NRING)] for l in range(2)]

        def slot_of(pe, kind, i):
            s, u = where[kind, i]
            pe.wait_ge(filled[s], 32 * (u + 1))
            return slots[s].rearrange("p (t n) -> p t n", n=512)

        block = ctx.enter_context(nc.Block())

        @block.sync
        def _(sp):
            def fill(n):
                kind, i, src = stream[n]
                s, u = where[kind, i]
                if u:
                    sp.wait_ge(*release[in_slot[s, u - 1]])
                elif s >= NRING:
                    sp.wait_ge(bank_full, place["sc"] + 1)
                dst = slots[s].rearrange("p (t n) -> p t n", n=512)
                for half in range(2):
                    sp.dma_start(dst[:, 4 * half:4 * half + 4, :], src[:, 4 * half:4 * half + 4, :]) \
                        .then_inc(filled[s], 16)

            sp.wait_ge(S("rows_loaded"), 13 * 16)
            for n in range(early):
                fill(n)

            def wait_moe_fill(l, groups, f):
                pair, part = divmod(f, 3)
                if part < 2:
                    sp.wait_ge(S(f"gu_full{l}"), groups * PG + 2 * pair + part + 1)
                else:
                    sp.wait_ge(S(f"dn_done{l}"), groups * PG + 2 * pair + 2)

            def moe_fills(l, gi, g_):
                for f in range(12):
                    s = moe_slot(l, f)
                    if f < NRING:
                        wait_moe_fill(l, gi, f + NRING)
                    else:
                        wait_moe_fill(l, gi + 1, f - NRING)
                    pair, part = f // 3, f % 3
                    if part < 2:
                        dst = slots[s].rearrange("p (t n) -> p t n", n=512)
                        e_ = bass.ds(g_ * PG + 2 * pair + part, 1)
                        for half, w in enumerate((A["moe_w_gate"], A["moe_w_up"])):
                            sp.dma_start(dst[:, :, half * FF:(half + 1) * FF],
                                         w[l, e_, :, :].rearrange("e (t p) n -> p (e t) n", p=P)) \
                                .then_inc(moe_filled[l][s], 16)
                    else:
                        dst = slots[s].rearrange("p (e t n) -> p e t n", e=2, t=2)
                        for half in range(2):
                            e_ = bass.ds(g_ * PG + 2 * pair + half, 1)
                            sp.dma_start(dst[:, half, :, :],
                                         A["moe_w_down"][l, e_, :, :].rearrange("e (t p) n -> p (e t) n", p=P)) \
                                .then_inc(moe_filled[l][s], 16)

            for l in range(2):
                if l == 0:
                    for s in range(NSTAT):
                        sp.wait_ge(*release[stream[last_early[s]][0:2]])
                    sp.wait_ge(S("oT_gated"), H)
                else:
                    for s in range(NRING):
                        sp.wait_ge(*release[in_slot[s, uses[s] - 1]])
                sp.sem_inc(S(f"gu_full{l}"), PG)
                sp.sem_inc(S(f"dn_done{l}"), PG)
                with sp.Fori(0, NG) as g_:
                    moe_fills(l, g_, g_)
                sp.wait_ge(S(f"passes_known{l}"), 1)
                n_pass = sp.value_load(passes[0:1, l:l + 1], min_val=1, max_val=MAXPASS)
                with sp.If(n_pass > 1):
                    with sp.Fori(1, n_pass) as p_:
                        with sp.Fori(0, NG) as g_:
                            moe_fills(l, p_ * NG + g_, g_)
                if l == 0:
                    for n in range(early, len(stream)):
                        if n - early < NRING:
                            wait_moe_fill(l, n_pass * NG, n - early + NRING)
                        fill(n)
            for n in range(NCH):
                sp.wait_ge(S("y_ready"), 2 * (n + 1))
                sp.dma_start(y_prompt[0, n * P:(n + 1) * P, :], y_rows[:, n, :]).then_inc(S("y_out"), 16)
            sp.wait_ge(S("y_ready"), 6)
            sp.dma_start(y_sample.rearrange("b s d -> (b s) d"), ys_rows[0:NB, :]).then_inc(S("y_out"), 16)
            sp.wait_ge(S("y_out"), 16 * (NCH + 1))
            sp.wait_ge(S("state_copied"), 32)
            sp.wait_ge(S("state_out"), 48)
            sp.wait_ge(S("conv_rows_out"), 32)
            sp.wait_ge(S("sconv_rows_out"), 32)

        @block.gpsimd
        def _(pool):
            link = Link(pool, "pool_link")
            pool.memset(ident[:, :], 0.0)
            pool.memset(ones[:, :], 1.0)
            pool.memset(causal[:, :], 1.0)
            pool.memset(strict[:, :], 1.0)
            pool.memset(levels[:, :, :], 0.0)
            pool.memset(cT[:, :, :], 0.0)
            pool.memset(epsc[:, 0:1], EPS)
            pool.memset(epsc[:, 1:2], 0.0)
            link(pool.memset(epsc[:, 2:3], 1.0))
            for L in range(LEVELS):
                s = 1 << L
                half = levels[:, L, :].rearrange("p (b h c) -> p b h c", h=2, c=s)[:, :, 1, :]
                last = pool.memset(half, 1.0)
            link(last)
            pool.affine_select(out=ident[:, :], in_=ident[:, :], compare_op=ALU.not_equal, fill=1.0, base=0,
                               pattern=[[-1, P]], channel_multiplier=1)
            pool.affine_select(out=causal[:, :], in_=causal[:, :], compare_op=ALU.is_ge, fill=0.0, base=0,
                               pattern=[[1, P]], channel_multiplier=-1)
            pool.affine_select(out=strict[:, :], in_=strict[:, :], compare_op=ALU.is_gt, fill=0.0, base=0,
                               pattern=[[1, P]], channel_multiplier=-1)
            pool.iota(slot_iota[:, :], pattern=[[1, P]], base=0, channel_multiplier=0,
                      allow_small_or_imprecise_dtypes=True)
            for L in range(LEVELS):
                s = 1 << L
                half = levels[:, L, :].rearrange("p (b h c) -> p b h c", h=2, c=s)[:, :, 1, :]
                last = pool.affine_select(out=half, in_=half, compare_op=ALU.is_ge, fill=0.0, base=0,
                                          pattern=[[-2 * s, P // (2 * s)], [0, s]], channel_multiplier=1)
            pool.memset(upper[:, 0:HALF], 0.0)
            last = pool.memset(upper[:, HALF:], float(HALF))
            link(last)
            for L in range(LEVELS):
                s = 1 << L
                half = levels[:, L, :].rearrange("p (b h c) -> p b h c", h=2, c=s)[:, :, 1, :]
                last = pool.affine_select(out=half, in_=half, compare_op=ALU.is_ge, fill=0.0, base=s - 1,
                                          pattern=[[2 * s, P // (2 * s)], [0, s]], channel_multiplier=-1)
            last.then_inc(S("consts"), 1)
            pool.memset(pre[:, :, 0:KC - 1], 0.0).then_inc(S("pre_zeroed"), 1)
            pool.wait_ge(S("pre_ready"), QT)
            pool.tensor_copy(tail[:, :, 0:KC - 1], pre[:, :, SEQ:SEQ + KC - 1])
            pool.tensor_copy(tail[:, :, KC - 1:], preS[:, :, :, KC - 1]).then_inc(S("tail_ready"), 1)
            pool.wait_ge(S("cv_ready"), QT + 1)
            for i in range(2 * H):
                if i >= 4:
                    pool.wait_ge(bank_full, place[f"l2_{i - 4}"] + 1)
                pool.tensor_tensor(sqb[:, i % 4, :], cv[:, i, :], cv[:, i, :], ALU.mult).then_inc(S("sq_ready"), 1)
            for h in range(H):
                pool.wait_ge(S("dec_exp"), h + 1)
                pool.tensor_tensor(decM[:, :, h, :], decM[:, :, h, :],
                                   causal[:, :].unsqueeze(1).broadcast_to([P, NCH, P]), ALU.mult) \
                    .then_inc(S("dec_masked"), 1)
            for q in range(NQ):
                pool.wait_ge(S("AT_raw"), q + 1)
                pool.tensor_tensor(AT[:, 4 * q:4 * q + 4, :], AT[:, 4 * q:4 * q + 4, :],
                                   strict[:, :].unsqueeze(1).broadcast_to([P, 4, P]), ALU.mult) \
                    .then_inc(S("AT_ready"), 1)
            for L in range(LEVELS):
                for q in range(NQ):
                    if L == 0:
                        pool.wait_ge(S("AT_ready"), q + 1)
                        pool.wait_ge(S("decays_used"), 1)
                    elif L >= 2:
                        pool.wait_ge(bank_full, place[f"P{L - 1}_{q}"] + 1)
                    else:
                        pool.wait_ge(S("XT_ready"), q + 1)
                    pool.tensor_tensor(BT[:, 4 * q:4 * q + 4, :], AT[:, 4 * q:4 * q + 4, :],
                                       levels[:, L, :].unsqueeze(1).broadcast_to([P, 4, P]), ALU.mult) \
                        .then_inc(S("BT_ready"), 1)
            pool.wait_ge(bank_full, place["u1_1"] + 1)
            pool.memset(k_rows[NB * H:96, :], 0.0)
            pool.memset(spread[NB * H:96, :, :, :], 0.0)
            pool.wait_ge(S("rows_ready"), 2)
            for t in range(0, NB * H // 4, 2):
                if t >= 2:
                    pool.wait_ge(bank_full, place[f"ou{t - 2}"] + 1)
                pool.tensor_tensor(spread[0:NB * H, 0, :, :],
                                   v_rows[0:NB * H, :].unsqueeze(1).broadcast_to([NB * H, 4, P]),
                                   ident[0:NB * H, 4 * t:4 * t + 4].unsqueeze(2).broadcast_to([NB * H, 4, P]),
                                   ALU.mult).then_inc(S("spread_even"), 1)
            pool.wait_ge(S("oT_ready"), 5)
            for h in range(H):
                if h >= 4:
                    pool.wait_ge(bank_full, place[f"on{h - 4}"] + 1)
                pool.tensor_tensor(sqb[:, h % 4, :], hT[:, h, :], hT[:, h, :], ALU.mult).then_inc(S("osq_ready"), 1)
            pool.wait_ge(S("state_out"), 48)
            pool.memset(htok[:, 2, :], 0.0)
            pool.memset(Pm[:, 2, :, :], 0.0).then_inc(S("pads_zeroed"), 1)
            pool.wait_ge(S("up_ready"), DT)
            pool.tensor_copy(tail2[:, :, 0:KS - 1], up[:, :, SEQ:SEQ + KS - 1])
            pool.tensor_copy(tail2[:, :, KS - 1:], upS[:, :, :, KS - 1]).then_inc(S("tail2_ready"), 1)

        @block.scalar
        def _(act):
            link = Link(act, "act_link")
            ld = S("rows_loaded")
            act.dma_start(c_rows[0:1, :], A["c_prompt"]).then_inc(ld, 16)
            act.dma_start(c_rows[1:1 + NB, :], A["c_sample"]).then_inc(ld, 16)
            act.dma_start(vec_rows[0:96, 0, :], A["b_ada"].rearrange("l (t p) -> (l t) p", p=P)).then_inc(ld, 16)
            act.dma_start(vec_rows[0:96, 1, :], A["gdn_conv_w"].rearrange("o k (t p) -> (o k t) p", p=P)).then_inc(ld, 16)
            act.dma_start(vec_rows[0:16, 2, :], A["norm_mix_g"].rearrange("l (t p) -> (l t) p", p=P)).then_inc(ld, 16)
            act.dma_start(vec_rows[16:32, 2, :], A["norm_ffn_g"].rearrange("l (t p) -> (l t) p", p=P)).then_inc(ld, 16)
            act.dma_start(vec_rows[32:40, 2, :], A["norm_final_g"].rearrange("(t p) -> t p", p=P)).then_inc(ld, 16)
            act.dma_start(vec_rows[40:41, 2, :], A["gdn_norm_g"]).then_inc(ld, 16)
            act.dma_start(vec_rows[41:65, 2, :], A["sc_conv_w"].rearrange("o k (t p) -> (o k t) p", p=P)).then_inc(ld, 16)
            act.dma_start(xs_rows[0:NB, :], A["x_sample"].rearrange("b s d -> (b s) d")).then_inc(ld, 16)
            act.dma_start(x_rows, A["x_prompt"][0].rearrange("(n p) d -> p n d", p=P)).then_inc(ld, 16)
            act.dma_start(cs_rows[0:NB * (KC - 1), :], A["state_gdn_conv"][0].rearrange("b k c -> (b k) c")).then_inc(ld, 16)
            act.dma_start(sc_rows[0:NB * (KS - 1), :], A["state_sconv"][0].rearrange("b k c -> (b k) c")).then_inc(ld, 16)
            wl = S("small_weights")
            with nc.allow_non_contiguous_dma(reason="narrow weights, once"):
                act.dma_start(decay_w[32:40, 0:1], A["gdn_A_log"].rearrange("o h -> h o")).then_inc(wl, 16)
                act.dma_start(decay_w[32:40, 1:2], A["gdn_dt_bias"].rearrange("o h -> h o")).then_inc(wl, 16)
                act.wait_ge(S("w_ba_zeroed"), 1)
                narrow = A["gdn_w_in"][0].rearrange("(t p) n -> p t n", p=P)
                act.dma_start(w_ba[:, :, 0:H], narrow[:, :, 4 * D:4 * D + H]).then_inc(wl, 16)
                act.dma_start(w_ba[:, :, 32:32 + H], narrow[:, :, 4 * D + H:4 * D + 2 * H]).then_inc(wl, 16)
                for l in range(2):
                    act.dma_start(w_route[:, l, :, 0:NG], A["moe_w_group"][l].rearrange("(t p) n -> p t n", p=P)).then_inc(wl, 16)
                    act.dma_start(w_route[:, l, :, NG:], A["moe_w_router"][l].rearrange("(t p) n -> p t n", p=P)).then_inc(wl, 16)
                    act.dma_start(b_route[:, l, 0:NG], A["moe_b_group"][l:l + 1, :].to_broadcast([P, NG])).then_inc(wl, 16)
                    act.dma_start(b_route[:, l, NG:], A["moe_b_router"][l:l + 1, :].to_broadcast([P, NE])).then_inc(wl, 16)
            act.dma_start(conv_sample_out[0, :, 0:KC - 2, :], A["state_gdn_conv"][0, :, 1:KC - 1, :]).then_inc(S("state_copied"), 16)
            act.dma_start(sconv_sample_out[0, :, 0:KS - 2, :], A["state_sconv"][0, :, 1:KS - 1, :]).then_inc(S("state_copied"), 16)

            b = full(act, "c")
            act.wait_ge(S("consts"), 1)
            act.activation(cT[:, :, 0:MODS], b[:, 0:DT * MODS].rearrange("p (t c) -> p t c", c=MODS), ACT.Silu) \
                .then_inc(emptied["A"], 1)
            b = full(act, "vec")
            act.activation(vecT[:, 0, 0:96], b[:, 0:96], ACT.Copy)
            act.activation(vecT[:, 1, 0:96], b[:, P:P + 96], ACT.Copy)
            act.activation(vecT[:, 2, 0:65], b[:, 2 * P:2 * P + 65], ACT.Copy).then_inc(emptied["A"], 1)

            def ada(pieces):
                for l, i in pieces:
                    b = full(act, f"ada{l}_{i}")
                    n = (ada_first + ada_later).index((l, i))
                    if n:
                        full(act, "adaT%d_%d" % (ada_first + ada_later)[n - 1])
                    act.activation(ada_row[:, :], b[:, :], ACT.Copy).then_inc(emptied["A"], 1)

            def norm(k, ready, n, squares=hT):
                for t in range(DT):
                    act.wait_ge(ready, n(t))
                    act.activation(squares[:, t, :], xT[:, t, :], ACT.Square).then_inc(S("sq_x"), 1)
                b = full(act, f"ss{k}")
                act.activation(rstd[:, :], b[:, 0:TOK], ACT.Ln, bias=epsc[:, 0:1], scale=1.0 / D).then_inc(emptied["A"], 1)
                act.wait_ge(emptied["A"], upto["A"][place[f"ss{k}"] + 1])
                act.activation(rstd[:, :], rstd[:, :], ACT.Exp, scale=-0.5).then_inc(S("rstd_ready"), 1)
                if k < 4:
                    shift = mT[:, k // 2, PART["sh_m" if k % 2 == 0 else "sh_f"] * DT:, :]
                    for t in range(DT):
                        act.wait_ge(S("h_scaled"), k * DT + t + 1)
                        act.activation(hT[:, t, 0:SEQ], hT[:, t, 0:SEQ], ACT.Identity, bias=shift[:, t, 0:1]) \
                            .then_inc(S("h_tiles"), 1)

            ada(ada_first)
            norm(0, emptied["D"], lambda t: upto["D"][place["x3"] + 1])

            for i in range(QT + H):
                if i < QT:
                    b = full(act, f"in{i}")
                    act.activation(pre[:, i, KC - 1:], b[:, 0:SEQ], ACT.Copy)
                    act.activation(preS[:, i, :, KC - 1], b[:, SEQ:TOK], ACT.Copy).then_inc(emptied["A"], 1)
                    act.wait_ge(emptied["A"], upto["A"][place[f"in{i}"] + 1])
                    act.sem_inc(S("pre_ready"), 1)
                elif i < QT + H:
                    b = full(act, f"in{i}")
                    act.activation(zs[:, i - QT, :], b[:, 0:TOK], ACT.Silu).then_inc(emptied["A"], 1)
                if 2 <= i < QT + 2:
                    act.wait_ge(S("conv_done"), i - 1)
                    act.activation(cv[:, i - 2, 0:SEQ], cv[:, i - 2, 0:SEQ], ACT.Silu).then_inc(S("cv_ready"), 1)
                if i % 4 == 3:
                    ada(ada_after[i // 4])
            act.wait_ge(S("conv_done"), QT + 1)
            act.activation(cv[:, :, SEQ:TOK], cv[:, :, SEQ:TOK], ACT.Silu).then_inc(S("cv_ready"), 1)
            for i in range(QT // 4):
                b = full(act, f"cb{i}")
                act.activation(tail_rows[0:3 + NB, i * 512:(i + 1) * 512], b[0:3 + NB, :], ACT.Copy).then_inc(emptied["A"], 1)
            act.wait_ge(emptied["A"], upto["A"][place[f"cb{QT // 4 - 1}"] + 1])
            act.dma_start(conv_prompt_out[0, 0], tail_rows[0:3, :]).then_inc(S("conv_rows_out"), 16)
            act.dma_start(conv_sample_out[0, :, KC - 2, :], tail_rows[3:3 + NB, :]).then_inc(S("conv_rows_out"), 16)

            act.wait_ge(emptied["D"], upto["D"][place["ba"] + 1])
            act.activation(bb[0:8, :], ba[0:8, :], ACT.Exp, scale=-1.0).then_inc(S("beta_exp"), 1)
            act.activation(decay_w[32:40, 2:3], decay_w[32:40, 0:1], ACT.Exp).then_inc(S("beta_exp"), 1)
            act.wait_ge(S("abs_a"), 1)
            link(act.activation(bb[32:40, :], bb[32:40, :], ACT.Exp, scale=-1.0))
            act.activation(bb[32:40, :], bb[32:40, :], ACT.Ln, bias=epsc[32:40, 2:3]).then_inc(S("softplus_ln"), 1)

            act.wait_ge(S("tail_ready"), 1)
            for i in range(2 * H):
                b = full(act, f"l2_{i}")
                act.activation(rnb[:, i, :], b[:, 0:TOK], ACT.Ln, bias=epsc[:, 0:1]).then_inc(emptied["A"], 1)
                if i % H == H - 1:
                    act.wait_ge(emptied["A"], upto["A"][place[f"l2_{i}"] + 1])
                    act.activation(rnb[:, i - H + 1:i + 1, :], rnb[:, i - H + 1:i + 1, :], ACT.Exp, scale=-0.5) \
                        .then_inc(S("qk_rn"), 1)
            for h in range(H):
                act.wait_ge(S("dec_raw"), h + 1)
                act.activation(eg[:, h, :], eg[:, h, :], ACT.Exp)
                act.activation(decM[:, :, h, :], decM[:, :, h, :], ACT.Exp).then_inc(S("dec_exp"), 1)
            act.wait_ge(S("kd_raw"), 1)
            act.activation(kd[:, :, :], kd[:, :, :], ACT.Exp).then_inc(S("kd_exp"), 1)
            act.activation(kb1[:, :], colv[:, 1, 32:32 + H], ACT.Exp).then_inc(S("kd_exp"), 1)

            for q in range(NQ):
                b = full(act, f"xt{q}")
                act.activation(X[:, 4 * q:4 * q + 4, :], b[:, :].rearrange("p (a c) -> p a c", a=4), ACT.Copy).then_inc(emptied["A"], 1)
            for L in range(1, LEVELS):
                for q in range(NQ):
                    b = full(act, f"P{L}_{q}")
                    act.activation(PX[:, 4 * q:4 * q + 4, :], b[:, :].rearrange("p (a c) -> p a c", a=4), ACT.Copy).then_inc(emptied["A"], 1)

            def four(dst, name):
                b = full(act, name)
                return act.activation(dst, b[:, :].rearrange("p (a c) -> p a c", a=4), ACT.Copy).then_inc(emptied["A"], 1)

            act.wait_ge(bank_full, place[f"T{LEVELS - 1}_{NQ - 1}"] + 1)
            S_in = A["state_gdn_S"][0].rearrange("b h k v -> k (b h) v")
            cut = 3 * NM
            act.dma_start(Ss[:, 0:cut, :], S_in[:, 0:cut, :]).then_inc(S("states_in"), 16)
            act.wait_ge(S("conv_rows_out"), 32)
            for q in range(2):
                four(vnew[:, 4 * q:4 * q + 4, :], f"u0_{q}")
            for q in range(2):
                four(hT[:, 4 * q:4 * q + 4, 0:P], f"o0_{q}")
            act.wait_ge(emptied["A"], upto["A"][place["o0_1"] + 1])
            act.sem_inc(S("oT_ready"), 1)
            for q in range(2):
                four(wT[:, 4 * q:4 * q + 4, :], f"w_{q}")
            for q in range(2):
                four(vnew1[:, 4 * q:4 * q + 4, :], f"u1_{q}")
            act.dma_start(Ss[:, cut:, :], S_in[:, cut:, :]).then_inc(S("states_in"), 16)
            for q in range(2):
                four(hT[:, 4 * q:4 * q + 4, P:SEQ], f"o1_{q}")
            act.wait_ge(emptied["A"], upto["A"][place["o1_1"] + 1])
            act.sem_inc(S("oT_ready"), 3)

            act.wait_ge(S("S2_ready"), 1)
            act.dma_start(S_prompt_out[0, 0].rearrange("h k v -> k h v"), S2).then_inc(S("state_out"), 16)
            b = full(act, "rw")
            act.activation(k_rows[0:NB * H, :], b[0:NB * H, 0:P], ACT.Copy).then_inc(S("rows_ready"), 1)
            act.activation(v_rows[0:NB * H, :], b[0:NB * H, P:2 * P], ACT.Copy).then_inc(emptied["A"], 1)
            act.wait_ge(emptied["A"], upto["A"][place["rw"] + 1])
            act.sem_inc(S("rows_ready"), 1)
            for t in range(1, NB * H // 4, 2):
                if t >= 2:
                    act.wait_ge(bank_full, place[f"ou{t - 2}"] + 1)
                for a in range(4):
                    last = act.activation(spread[0:NB * H, 1, a, :], v_rows[0:NB * H, :], ACT.Copy,
                                          scale=ident[0:NB * H, 4 * t + a:4 * t + a + 1])
                last.then_inc(S("spread_odd"), 1)
            for h in range(H):
                b = full(act, f"on{h}")
                act.activation(rno[:, h, :], b[:, 0:TOK], ACT.Ln, bias=epsc[:, 0:1], scale=1.0 / P).then_inc(emptied["A"], 1)
            act.wait_ge(emptied["A"], upto["A"][place[f"on{H - 1}"] + 1])
            act.activation(rno, rno, ACT.Exp, scale=-0.5).then_inc(S("o_rn"), 1)
            act.wait_ge(S("states_new"), NB * H // 4)
            half = NB * H // 2
            S_out = S_sample_out[0].rearrange("b h k v -> k (b h) v")
            for i in range(2):
                act.dma_start(S_out[:, i * half:(i + 1) * half, :], Ss[:, i * half:(i + 1) * half, :]).then_inc(S("state_out"), 16)

            def moe(l):
                norm(2 * l + 1, S("x_mixed"), lambda t: l * DT + t + 1, squares=sqx if l == 0 else hT)
                act.wait_ge(S(f"gexp_raw{l}"), 1)
                act.activation(r4[:, :, :], r4[:, :, :], ACT.Exp).then_inc(S(f"gexp{l}"), 1)
                act.wait_ge(S(f"e2_raw{l}"), 1)
                act.activation(r1[:, 2, :], r1[:, 2, :], ACT.Exp).then_inc(S(f"e2_exp{l}"), 1)
                act.wait_ge(S("state_out"), 48)
                act.wait_ge(S("pads_zeroed"), 1)
                for i in range(6):
                    n, j = i // 2, i % 2
                    rows = P if n < 2 else NB
                    b = full(act, f"ht{l}_{i}")
                    act.activation(htok[0:rows, n, j * 512:(j + 1) * 512], b[0:rows, :], ACT.Copy).then_inc(emptied["A"], 1)
                act.wait_ge(S(f"passes_known{l}"), 1)
                n_pass = act.value_load(passes[0:1, l:l + 1], min_val=1, max_val=MAXPASS)
                act.sem_inc(S(f"y_emptied{l}"), 1)
                with act.Fori(0, n_pass) as p_:
                    for g_ in range(NG):
                        act.wait_ge(S(f"PT_full{l}"), p_ * NG + g_ + 1)
                        act.activation(PT[:, g_, :], banks[g_][:, 0:TOK], ACT.Copy).then_inc(S(f"PT_ready{l}"), 1)
                    for k in range(DT):
                        act.wait_ge(S(f"gathered{l}"), p_ * DT + k + 1)
                        act.activation(hg[:, k, :], banks[(5 + k) % 8][:, :], ACT.Copy).then_inc(S(f"hg_ready{l}"), 1)
                    with act.Fori(0, NG) as g_:
                        gi = p_ * NG + g_

                        def experts(c_):
                            for u in range(PG // c_ + 1):
                                if u < PG // c_:
                                    act.wait_ge(S(f"gu_full{l}"), gi * PG + (u + 1) * c_ + PG)
                                    if u >= 2:
                                        act.wait_ge(S(f"hid_done{l}"), gi * PG + (u - 1) * c_ + PG)
                                    act.activation(sg[:, u % 2, :], banks[u % 2][:, 0:FF], ACT.Silu) \
                                        .then_inc(S(f"sg_ready{l}"), c_)
                                if u >= 1:
                                    v = u - 1
                                    act.wait_ge(S(f"tr_full{l}"), gi * PG + (v + 1) * c_)
                                    if v >= 2:
                                        act.wait_ge(S(f"dn_done{l}"), gi * PG + (v - 1) * c_ + PG)
                                    act.activation(hidT[:, v % 2, :, :],
                                                   banks[2 + v % 2][:, 0:2 * P].rearrange("p (a c) -> p a c", a=2),
                                                   ACT.Copy).then_inc(S(f"hidT_ready{l}"), c_)

                        is_small = act.value_load(small_i[0:1, l, bass.ds(gi, 1)], min_val=0, max_val=1)
                        with act.If(is_small > 0):
                            experts(2)
                        with act.Else():
                            experts(1)
                        act.wait_ge(S(f"dn_done{l}"), gi * PG + 2 * PG)
                        act.activation(ysb[:, bass.ds(g_, 1), 0:512], banks[4][:, :].unsqueeze(1), ACT.Copy)
                        act.activation(ysb[:, bass.ds(g_, 1), 512:1024], banks[5][:, :].unsqueeze(1), ACT.Copy) \
                            .then_inc(S(f"y_emptied{l}"), 1)
                return n_pass

            np0 = moe(0)
            norm(2, S("x_moe0"), lambda t: np0 * DT + t + 1)
            for i in range(2 * DT):
                b = full(act, f"sg{i}")
                dst = gateb[:, i, :] if i < DT else gatec[:, i - DT, :]
                act.activation(dst, b[:, 0:TOK], ACT.Copy).then_inc(emptied["A"], 1)
            for i in range(DT // 4):
                b = full(act, f"st{i}")
                act.activation(tail2_rows[0:2 + NB, i * 512:(i + 1) * 512], b[0:2 + NB, :], ACT.Copy).then_inc(emptied["A"], 1)
            act.wait_ge(emptied["A"], upto["A"][place[f"st{DT // 4 - 1}"] + 1])
            act.dma_start(sconv_prompt_out[0, 0], tail2_rows[0:2, :]).then_inc(S("sconv_rows_out"), 16)
            act.dma_start(sconv_sample_out[0, :, KS - 2, :], tail2_rows[2:2 + NB, :]).then_inc(S("sconv_rows_out"), 16)
            act.wait_ge(S("sconv_rows_out"), 32)
            np1 = moe(1)
            norm(4, S("x_moe1"), lambda t: np1 * DT + t + 1)
            for i in range(6):
                n, j = i // 2, i % 2
                b = full(act, f"y{i}")
                dst = y_rows[:, n, j * 512:(j + 1) * 512] if n < 2 else ys_rows[0:NB, j * 512:(j + 1) * 512]
                act.activation(dst, b[0:(P if n < 2 else NB), :], ACT.Copy).then_inc(S("y_ready"), 1)

        @block.tensor
        def _(pe):
            pe.wait_ge(S("consts"), 1)
            pe.wait_ge(S("rows_loaded"), 13 * 16)
            b = claim(pe, "c")
            for t in range(DT):
                last = pe.transpose(b[:, t * MODS:(t + 1) * MODS], c_rows[0:MODS, t * P:(t + 1) * P], ident[0:MODS, 0:MODS])
            last.then_inc(bank_full, 1)
            b = claim(pe, "xs")
            for t in range(DT):
                last = pe.transpose(b[:, t * NB:(t + 1) * NB], xs_rows[0:NB, t * P:(t + 1) * P], ident[0:NB, 0:NB])
            last.then_inc(bank_full, 1)
            for i in range(4):
                n, j = i // 2, i % 2
                b = claim(pe, f"x{i}")
                for t in range(4):
                    last = pe.transpose(b[:, t * P:(t + 1) * P], x_rows[:, n, (4 * j + t) * P:(4 * j + t + 1) * P], ident[:, :])
                last.then_inc(bank_full, 1)
            b = claim(pe, "vec")
            pe.transpose(b[:, 0:96], vec_rows[0:96, 0, :], ident[0:96, 0:96])
            pe.transpose(b[:, P:P + 96], vec_rows[0:96, 1, :], ident[0:96, 0:96])
            pe.transpose(b[:, 2 * P:2 * P + 65], vec_rows[0:65, 2, :], ident[0:65, 0:65]).then_inc(bank_full, 1)
            R = NB * (KC - 1)
            for name, lo, hi in (("cs0", 0, 16), ("cs1", 16, QT)):
                b = claim(pe, name)
                for t in range(lo, hi):
                    last = pe.transpose(b[:, (t - lo) * R:(t - lo + 1) * R], cs_rows[0:R, t * P:(t + 1) * P], ident[0:R, 0:R])
                last.then_inc(bank_full, 1)
            b = claim(pe, "sc")
            R = NB * (KS - 1)
            for t in range(DT):
                last = pe.transpose(b[:, t * R:(t + 1) * R], sc_rows[0:R, t * P:(t + 1) * P], ident[0:R, 0:R])
            last.then_inc(bank_full, 1)

            def ada(pieces):
                def turn(l, i):
                    b = claim(pe, f"adaT{l}_{i}")
                    pe.wait_ge(emptied["A"], upto["A"][place[f"ada{l}_{i}"] + 1])
                    for c_ in range(4):
                        last = pe.transpose(b[:, c_ * P:(c_ + 1) * P], ada_row[:, c_ * P:(c_ + 1) * P], ident[:, :])
                    last.then_inc(bank_full, 1)

                for n, (l, i) in enumerate(pieces):
                    w = slot_of(pe, f"ada{l}", i)
                    b = claim(pe, f"ada{l}_{i}")
                    for k in range(DT // 4):
                        for j in range(4):
                            last = pe.matmul(b[32 * j:32 * j + 32, :], cT[:, 4 * k + j, :], w[:, 4 * k + j, :],
                                             start=(k == 0), stop=(k == DT // 4 - 1), skip_group_check=True)
                    last.then_inc(bank_full, 1)
                    if n:
                        turn(*pieces[n - 1])
                turn(*pieces[-1])

            def norm(k, squares=hT):
                b = claim(pe, f"ss{k}")
                for t in range(DT):
                    pe.wait_ge(S("sq_x"), k * DT + t + 1)
                    last = pe.matmul(b[:, 0:TOK], ones[:, :], squares[:, t, :], start=(t == 0), stop=(t == DT - 1))
                last.then_inc(bank_full, 1)

            def h_tile(k, t):
                if t == 0:
                    pe.wait_ge(S("h_samples"), k + 1)
                pe.wait_ge(S("h_tiles"), k * DT + t + 1)

            def project(kind, names, x, ready=None):
                for i, name in enumerate(names):
                    c_, j = i // 4, i % 4
                    if j == 0:
                        w = slot_of(pe, kind, c_)
                    b = claim(pe, name)
                    for k in range(DT):
                        if i == 0 and ready:
                            ready(k)
                        last = pe.matmul(b[:, 0:TOK], w[:, k, j * P:(j + 1) * P], x[:, k, :],
                                         start=(k == 0), stop=(k == DT - 1))
                    last.then_inc(bank_full, 1)
                    if kind == "win" and j == 3:
                        ada(ada_after[c_])

            pe.wait_ge(emptied["A"], upto["A"][place["c"] + 1])
            ada(ada_first)
            norm(0)
            pe.wait_ge(S("small_weights"), 12 * 16)
            b = claim(pe, "ba")
            for k in range(DT):
                h_tile(0, k)
                last = pe.matmul(b[0:40, 0:TOK], w_ba[:, k, :], hT[:, k, :], start=(k == 0), stop=(k == DT - 1))
            last.then_inc(bank_full, 1)
            project("win", [f"in{i}" for i in range(QT + H)], hT)
            pe.wait_ge(S("tail_ready"), 1)
            for i in range(QT // 4):
                b = claim(pe, f"cb{i}")
                for t in range(4):
                    last = pe.transpose(b[0:3 + NB, t * P:(t + 1) * P], tail[:, 4 * i + t, :], ident[:, :])
                last.then_inc(bank_full, 1)
            for i in range(2 * H):
                b = claim(pe, f"l2_{i}")
                pe.wait_ge(S("sq_ready"), i + 1)
                pe.matmul(b[:, 0:TOK], ones[:, :], sqb[:, i % 4, :], start=True, stop=True).then_inc(bank_full, 1)
            b = claim(pe, "smx")
            pe.wait_ge(S("smT_ready"), 1)
            for n in range(NCH):
                last = pe.transpose(b[:, n * 40:(n + 1) * 40], smT[:, n * P:(n + 1) * P], ident[0:40, 0:40])
            last.then_inc(bank_full, 1)
            for h in range(H):
                b = claim(pe, f"gr{h}")
                pe.matmul(b[:, 0:TOK], ident[0:40, 32 + h:33 + h].to_broadcast([40, P]), smT[:, :], start=True, stop=True) \
                    .then_inc(bank_full, 1)
            for h in range(H):
                b = claim(pe, f"br{h}")
                pe.matmul(b[:, 0:TOK], ident[0:40, h:h + 1].to_broadcast([40, P]), smT[:, :], start=True, stop=True) \
                    .then_inc(bank_full, 1)
            pe.wait_ge(S("qk_normed"), 2 * H)
            for name, other in (("kk", H), ("qk", 0)):
                for q in range(NQ):
                    b = claim(pe, f"{name}{q}")
                    for a in range(4):
                        n, h = divmod(4 * q + a, H)
                        last = pe.matmul(b[:, a * P:(a + 1) * P], cv[:, H + h, n * P:(n + 1) * P],
                                         cv[:, other + h, n * P:(n + 1) * P], start=True, stop=True)
                    last.then_inc(bank_full, 1)
            for name, base in (("vt", 2 * H), ("kt", H)):
                for q in range(NQ):
                    b = claim(pe, f"{name}{q}")
                    for a in range(4):
                        n, h = divmod(4 * q + a, H)
                        last = pe.transpose(b[:, a * P:(a + 1) * P], cv[:, base + h, n * P:(n + 1) * P], ident[:, :])
                    last.then_inc(bank_full, 1)
            for q in range(NQ):
                b = claim(pe, f"xt{q}")
                pe.wait_ge(S("XT_ready"), q + 1)
                for a in range(4):
                    last = pe.transpose(b[:, a * P:(a + 1) * P], XT[:, 4 * q + a, :], ident[:, :])
                last.then_inc(bank_full, 1)
            for L in range(1, LEVELS):
                for q in range(NQ):
                    b = claim(pe, f"P{L}_{q}")
                    pe.wait_ge(S("BT_ready"), L * NQ + q + 1)
                    if L == 1:
                        pe.wait_ge(emptied["A"], upto["A"][place[f"xt{q}"] + 1])
                    else:
                        pe.wait_ge(emptied["D"], upto["D"][place[f"Q{L - 1}_{q}"] + 1])
                    for a in range(4):
                        last = pe.matmul(b[:, a * P:(a + 1) * P], BT[:, 4 * q + a, :], X[:, 4 * q + a, :], start=True, stop=True)
                    last.then_inc(bank_full, 1)
                for q in range(NQ):
                    b = claim(pe, f"T{L}_{q}")
                    pe.wait_ge(emptied["A"], upto["A"][place[f"P{L}_{q}"] + 1])
                    for a in range(4):
                        last = pe.matmul(b[:, a * P:(a + 1) * P], PX[:, 4 * q + a, :], XT[:, 4 * q + a, :], start=True, stop=True)
                    last.then_inc(bank_full, 1)
                    if L < LEVELS - 1:
                        b = claim(pe, f"Q{L}_{q}")
                        for a in range(4):
                            last = pe.matmul(b[:, a * P:(a + 1) * P], XT[:, 4 * q + a, :], PX[:, 4 * q + a, :], start=True, stop=True)
                        last.then_inc(bank_full, 1)

            def four(name, terms):
                b = claim(pe, name)
                q = int(name[-1])
                for a in range(4):
                    h = 4 * q + a
                    ts = terms(h)
                    for i, (l_, r_) in enumerate(ts):
                        last = pe.matmul(b[:, a * P:(a + 1) * P], l_, r_, start=(i == 0), stop=(i == len(ts) - 1))
                last.then_inc(bank_full, 1)

            def got(e_, name):
                pe.wait_ge(emptied[e_], upto[e_][place[name] + 1])

            got("D", f"T{LEVELS - 1}_{NQ - 1}")
            for q in range(2):
                four(f"u0_{q}", lambda h: [(XT[:, h, :], vb[:, h, :])])
            for q in range(2):
                got("A", f"u0_{q}")
                four(f"s1_{q}", lambda h: [(kdec[:, h, :], vnew[:, h, :])])
            for q in range(2):
                four(f"o0_{q}", lambda h: [(vnew[:, h, :], intraT[:, h, :])])
            for q in range(2):
                four(f"w_{q}", lambda h: [(kbg[:, h, :], XT[:, H + h, :])])
            for q in range(2):
                got("A", f"w_{q}")
                got("D", f"s1_{q}")
                four(f"u1_{q}", lambda h: [(XT[:, H + h, :], vb[:, H + h, :]), (wT[:, h, :], S1[:, h, :])])
            pe.wait_ge(S("qg_ready"), 1)
            for q in range(2):
                got("A", f"u1_{q}")
                four(f"o1_{q}", lambda h: [(vnew1[:, h, :], intraT[:, H + h, :]), (S1[:, h, :], cv[:, h, P:SEQ])])
            for q in range(2):
                four(f"s2_{q}", lambda h: [(kdec[:, H + h, :], vnew1[:, h, :])])
            b = claim(pe, "R")
            pe.wait_ge(S("states_in"), 32)
            cvqk = cv[:, 0:2 * H, :].rearrange("p (c h) t -> p c h t", c=2)
            for h in range(H):
                for s in range(NB):
                    r = h * NB + s
                    last = pe.matmul(b[:, 2 * r:2 * r + 2], Ss[:, s * H + h, :], cvqk[:, :, h, SEQ + s], start=True, stop=True)
            last.then_inc(bank_full, 1)
            b = claim(pe, "qkS")
            pe.wait_ge(S("qk_prod"), 1)
            pe.matmul(b[:, 0:NB * H], ones[:, :], qkS.rearrange("p h b -> p (h b)"), start=True, stop=True).then_inc(bank_full, 1)
            b = claim(pe, "rw")
            pe.wait_ge(S("verr_ready"), 1)
            pe.transpose(b[0:NB * H, 0:P], kS.rearrange("p h b -> p (h b)"), ident[:, :])
            pe.transpose(b[0:NB * H, P:2 * P], verr.rearrange("p h b -> p (h b)"), ident[:, :]).then_inc(bank_full, 1)
            pe.wait_ge(S("rows_ready"), 2)
            for t in range(NB * H // 4):
                b = claim(pe, f"ou{t}")
                pe.wait_ge(S("spread_odd" if t % 2 else "spread_even"), t // 2 + 1)
                pe.matmul(b[:, :], k_rows[0:96, :], spread[0:96, t % 2, :, :].rearrange("p r c -> p (r c)"),
                          start=True, stop=True).then_inc(bank_full, 1)
            for h in range(H):
                b = claim(pe, f"on{h}")
                pe.wait_ge(S("osq_ready"), h + 1)
                pe.matmul(b[:, 0:TOK], ones[:, :], sqb[:, h % 4, :], start=True, stop=True).then_inc(bank_full, 1)
            pe.wait_ge(S("oT_gated"), H)
            project("wout", [f"wo{i}" for i in range(DT)], hT)

            def moe(l):
                norm(2 * l + 1, squares=sqx if l == 0 else hT)
                b = claim(pe, f"lg{l}")
                for k in range(DT):
                    h_tile(2 * l + 1, k)
                    last = pe.matmul(b[0:NG + NE, 0:TOK], w_route[:, l, k, :], hT[:, k, :], start=(k == 0), stop=(k == DT - 1))
                last.then_inc(bank_full, 1)
                b = claim(pe, f"lgT{l}")
                pe.wait_ge(emptied["D"], upto["D"][place[f"lg{l}"] + 1])
                for n in range(3):
                    last = pe.transpose(b[:, n * (NG + NE):(n + 1) * (NG + NE)], lg[:, n * P:(n + 1) * P],
                                        ident[0:NG + NE, 0:NG + NE])
                last.then_inc(bank_full, 1)
                b = claim(pe, f"cum{l}")
                pe.wait_ge(S(f"oh_ready{l}"), 1)
                for n in range(4):
                    for n2 in range(min(n, 2) + 1):
                        rows = P if n2 < 2 else NB
                        diag = n2 == n
                        last = pe.matmul(b[:, n * NG:(n + 1) * NG], (strict if diag else ones)[0:rows, :],
                                         oh[0:rows, n2, :], start=(n2 == 0), stop=(n2 == min(n, 2)))
                last.then_inc(bank_full, 1)
                for i in range(6):
                    n, j = i // 2, i % 2
                    b = claim(pe, f"ht{l}_{i}")
                    rows = P if n < 2 else NB
                    for t in range(4):
                        last = pe.transpose(b[0:rows, t * P:(t + 1) * P], hT[:, 4 * j + t, n * P:n * P + rows], ident[:, :])
                    last.then_inc(bank_full, 1)
                got("A", f"ht{l}_5")
                got("D", f"cum{l}")
                pe.wait_ge(S(f"passes_known{l}"), 1)
                n_pass = pe.value_load(passes[0:1, l:l + 1], min_val=1, max_val=MAXPASS)
                with pe.Fori(0, n_pass) as p_:
                    pe.wait_ge(S(f"Pm_ready{l}"), p_ + 1)
                    for g_ in range(NG):
                        for n in range(3):
                            rows = P if n < 2 else NB
                            last = pe.transpose(banks[g_][:, n * P:n * P + rows], Pm[0:rows, n, g_, :], ident[0:rows, 0:rows])
                        last.then_inc(S(f"PT_full{l}"), 1)
                    for g_ in range(NG):
                        for n in range(3):
                            rows = P if n < 2 else NB
                            last = pe.matmul(banks[4][:, g_ * PG:(g_ + 1) * PG], Pm[0:rows, n, g_, :], r8[0:rows, n, 0, :],
                                             start=(n == 0), stop=(n == 2))
                    last.then_inc(S(f"cmb_full{l}"), 1)
                    for k in range(DT):
                        bk = (5 + k) % 8
                        if bk < 4:
                            pe.wait_ge(S(f"PT_ready{l}"), p_ * NG + bk + 1)
                        if bk == 4:
                            pe.wait_ge(S(f"cmb_ready{l}"), p_ + 1)
                        for n in range(3):
                            last = pe.matmul(banks[bk][:, :], htok[:, n, k * P:(k + 1) * P],
                                             Pm[:, n, :, :].rearrange("p g c -> p (g c)"), start=(n == 0), stop=(n == 2))
                        last.then_inc(S(f"gathered{l}"), 1)
                    with pe.Fori(0, NG) as g_:
                        gi = p_ * NG + g_
                        pe.wait_ge(S(f"hcur_ready{l}"), gi + 1)

                        def filled_by(f):
                            s = moe_slot(l, f)
                            pe.wait_ge(moe_filled[l][s], (gi * 2 + f // NRING + 1) * 32)
                            return slots[s]

                        def experts(c_):
                            M = CAP // c_

                            def turn(u):
                                pe.wait_ge(S(f"hid_done{l}"), gi * PG + (u + 1) * c_ + PG)
                                if u >= 2:
                                    pe.wait_ge(S(f"hidT_ready{l}"), gi * PG + (u - 1) * c_)
                                for f in range(2):
                                    last = pe.transpose(banks[2 + u % 2][:, f * P:(f + 1) * P],
                                                        hid[:, u % 2, f * P:(f + 1) * P], ident[:, :])
                                last.then_inc(S(f"tr_full{l}"), c_)

                            def gate_up(u):
                                w = [filled_by(3 * (j // 2) + j % 2).rearrange("p (t n) -> p t n", n=512)
                                     for j in range(u * c_, (u + 1) * c_)]
                                if u >= 2:
                                    pe.wait_ge(S(f"hid_done{l}"), gi * PG + (u - 1) * c_ + PG)
                                for k in range(DT):
                                    if k == DT // 2 and u >= 1:
                                        turn(u - 1)
                                    for x in range(c_):
                                        last = pe.matmul(banks[u % 2][x * M:(x + 1) * M, :], hcur[:, k, x * M:(x + 1) * M],
                                                         w[x][:, k, :], start=(k == 0), stop=(k == DT - 1),
                                                         skip_group_check=True)
                                last.then_inc(S(f"gu_full{l}"), c_)

                            def down(u):
                                w = filled_by(3 * (u * c_ // 2) + 2).rearrange("p (e t n) -> p e t n", e=2, t=2)
                                pe.wait_ge(S(f"hidT_ready{l}"), gi * PG + (u + 1) * c_)
                                for f in range(2):
                                    for d in range(2):
                                        for x in range(c_):
                                            last = pe.matmul(banks[4 + d][x * M:(x + 1) * M, :],
                                                             hidT[:, u % 2, f, x * M:(x + 1) * M],
                                                             w[:, (u * c_ + x) % 2, f, d * 512:(d + 1) * 512],
                                                             start=(u == 0 and f == 0), stop=(u == PG // c_ - 1 and f == 1),
                                                             skip_group_check=True)
                                last.then_inc(S(f"dn_done{l}"), c_)

                            for u in range(PG // c_):
                                gate_up(u)
                                if u == 1:
                                    pe.wait_ge(S(f"y_emptied{l}"), gi + 1)
                                if u >= 1:
                                    down(u - 1)
                            turn(PG // c_ - 1)
                            down(PG // c_ - 1)

                        is_small = pe.value_load(small_i[0:1, l, bass.ds(gi, 1)], min_val=0, max_val=1)
                        with pe.If(is_small > 0):
                            experts(2)
                        with pe.Else():
                            experts(1)
                    pe.wait_ge(S(f"y_emptied{l}"), (p_ + 1) * NG + 1)
                    for t in range(DT):
                        for g_ in range(NG):
                            last = pe.matmul(scatter_bank(l, t)[:, 0:TOK], ysb[:, g_, t * P:(t + 1) * P], PT[:, g_, :],
                                             start=(g_ == 0), stop=(g_ == NG - 1))
                        last.then_inc(S(f"scattered{l}"), 1)
                return n_pass

            np0 = moe(0)
            pe.wait_ge(S("samples_gated0"), np0 * DT + 1)
            norm(2)
            project("scin", [f"sg{i}" for i in range(3 * DT)], hT, ready=lambda k: h_tile(2, k))
            pe.wait_ge(S("tail2_ready"), 1)
            for i in range(DT // 4):
                b = claim(pe, f"st{i}")
                for t in range(4):
                    last = pe.transpose(b[0:2 + NB, t * P:(t + 1) * P], tail2[:, 4 * i + t, :], ident[:, :])
                last.then_inc(bank_full, 1)
            pe.wait_ge(S("sconv_y"), DT)
            project("scout", [f"so{i}" for i in range(DT)], gatec)
            np1 = moe(1)
            pe.wait_ge(S("samples_gated1"), np1 * DT + 1)
            norm(4)
            for i in range(6):
                n, j = i // 2, i % 2
                b = claim(pe, f"y{i}")
                rows = P if n < 2 else NB
                for t in range(4):
                    if n == 0:
                        pe.wait_ge(S("h_tiles"), 4 * DT + 4 * j + t + 1)
                    last = pe.transpose(b[0:rows, t * P:(t + 1) * P], hT[:, 4 * j + t, n * P:n * P + rows], ident[:, :])
                last.then_inc(bank_full, 1)

        @block.vector
        def _(dve):
            link = Link(dve, "dve_link")
            stt, tt, ts = dve.scalar_tensor_tensor, dve.tensor_tensor, dve.tensor_scalar
            dve.memset(w_ba[:, :, :], 0.0).then_inc(S("w_ba_zeroed"), 1)
            dve.memset(smT[:, :], 0.0)
            link(dve.memset(lg[:, :], 0.0))
            b = full(dve, "xs")
            dve.tensor_copy(xT[:, :, SEQ:TOK], b[:, 0:DT * NB].rearrange("p (t c) -> p t c", c=NB)).then_inc(emptied["D"], 1)
            for i in range(4):
                n, j = i // 2, i % 2
                b = full(dve, f"x{i}")
                dve.tensor_copy(xT[:, 4 * j:4 * j + 4, n * P:(n + 1) * P], b[:, :].rearrange("p (t c) -> p t c", t=4)) \
                    .then_inc(emptied["D"], 1)
            for name, lo, hi in (("cs0", 0, 16), ("cs1", 16, QT)):
                b = full(dve, name)
                for t in range(lo, hi):
                    last = dve.tensor_copy(preS[:, t, :, 0:KC - 1],
                                           b[:, (t - lo) * NB * (KC - 1):(t - lo + 1) * NB * (KC - 1)].rearrange("p (b k) -> p b k", b=NB))
                last.then_inc(emptied["D"], 1)
            b = full(dve, "sc")
            dve.tensor_copy(sc_state[:, :, :], b[:, 0:DT * NB * (KS - 1)].rearrange("p (t r) -> p t r", t=DT)).then_inc(emptied["D"], 1)

            def ada(pieces):
                for l, i in pieces:
                    b = full(dve, f"adaT{l}_{i}")
                    v = b[:, :].rearrange("p (t j r) -> p t r j", t=4, j=4)[:, :, 0:MODS, :]
                    link(dve.tensor_reduce(ada_sum[:, :, :], v, AX.X, ALU.add))
                    bias = vecT[:, 0, l * 6 * DT + 4 * i:l * 6 * DT + 4 * i + 4].unsqueeze(2).broadcast_to([P, 4, MODS])
                    tt(mT[:, l, 4 * i:4 * i + 4, :], ada_sum[:, :, :], bias, ALU.add).then_inc(emptied["D"], 1)
                    dve.wait_ge(emptied["D"], upto["D"][place[f"adaT{l}_{i}"] + 1])

            def mod(l, part):
                t = PART[part] * DT
                return mT[:, l, t:t + DT, :]

            def norm(k, l, which):
                at = (l * DT if which == "m" else 2 * DT + l * DT)
                dve.wait_ge(emptied["A"], upto["A"][place["vec"] + 1])
                gv = vecT[:, 2, at:at + DT].unsqueeze(2).broadcast_to([P, DT, MODS])
                link(stt(gain[:, :, :], mod(l, "sc_" + which), 1.0, gv, ALU.add, ALU.mult))
                dve.wait_ge(S("rstd_ready"), k + 1)
                hS = hT[:, :, SEQ:TOK]
                link(tt(hS, xT[:, :, SEQ:TOK], rstd[:, SEQ:TOK].unsqueeze(1).broadcast_to([P, DT, NB]), ALU.mult))
                link(tt(hS, hS, gain[:, :, 1:MODS], ALU.mult))
                tt(hS, hS, mod(l, "sh_" + which)[:, :, 1:MODS], ALU.add).then_inc(S("h_samples"), 1)
                for t in range(DT):
                    stt(hT[:, t, 0:SEQ], xT[:, t, 0:SEQ], gain[:, t, 0:1], rstd[:, 0:SEQ], ALU.mult, ALU.mult) \
                        .then_inc(S("h_scaled"), 1)

            def residual(l, part, t, b):
                gt = mod(l, part)
                stt(xT[:, t, 0:SEQ], b[:, 0:SEQ], gt[:, t, 0:1], xT[:, t, 0:SEQ], ALU.mult, ALU.add)
                return tt(x_new[:, t, :], b[:, SEQ:TOK], gt[:, t, 1:MODS], ALU.mult)

            def residual_samples(t):
                return tt(xT[:, t, SEQ:TOK], xT[:, t, SEQ:TOK], x_new[:, t, :], ALU.add)

            dve.wait_ge(emptied["A"], upto["A"][place["vec"] + 1])
            ada(ada_first)
            norm(0, 0, "m")
            b = full(dve, "ba")
            dve.tensor_copy(ba[:, :], b[0:40, 0:TOK]).then_inc(emptied["D"], 1)

            dve.wait_ge(S("pre_zeroed"), 1)
            for i in range(QT):
                if i and i % 4 == 0:
                    ada(ada_after[i // 4 - 1])
                dve.wait_ge(S("pre_ready"), i + 1)
                w = lambda k: vecT[:, 1, k * QT + i:k * QT + i + 1]
                link(ts(cv[:, i, 0:SEQ], pre[:, i, 0:SEQ], w(0), None, ALU.mult))
                for k in range(1, KC - 1):
                    link(stt(cv[:, i, 0:SEQ], pre[:, i, k:k + SEQ], w(k), cv[:, i, 0:SEQ], ALU.mult, ALU.add))
                stt(cv[:, i, 0:SEQ], pre[:, i, KC - 1:KC - 1 + SEQ], w(KC - 1), cv[:, i, 0:SEQ], ALU.mult, ALU.add) \
                    .then_inc(S("conv_done"), 1)
            for k in range(KC):
                wk = vecT[:, 1, k * QT:(k + 1) * QT].unsqueeze(2).broadcast_to([P, QT, NB])
                last = tt(convtmp[:, :, :, k], preS[:, :, :, k], wk, ALU.mult)
            link(last)
            link(tt(convtmp[:, :, :, 0], convtmp[:, :, :, 0], convtmp[:, :, :, 1], ALU.add))
            link(tt(convtmp[:, :, :, 0], convtmp[:, :, :, 0], convtmp[:, :, :, 2], ALU.add))
            tt(cv[:, :, SEQ:TOK], convtmp[:, :, :, 0], convtmp[:, :, :, 3], ALU.add).then_inc(S("conv_done"), 1)
            for j in range(QT // 4 - 1, WIN):
                ada(ada_after[j])

            link(ts(bc[32:40, :], ba[32:40, :], decay_w[32:40, 1:2], None, ALU.add))
            dve.wait_ge(S("beta_exp"), 2)
            link(ts(bb[32:40, :], bc[32:40, :], -1.0, None, ALU.mult))
            tt(bb[32:40, :], bb[32:40, :], bc[32:40, :], ALU.max).then_inc(S("abs_a"), 1)
            link(ts(bb[0:8, :], bb[0:8, :], 1.0, None, ALU.add))
            link(dve.reciprocal(smT[0:8, :], bb[0:8, :]))
            dve.wait_ge(S("softplus_ln"), 1)
            link(stt(bc[32:40, :], bc[32:40, :], 0.0, bb[32:40, :], ALU.max, ALU.add))
            link(ts(bc[32:40, :], bc[32:40, :], decay_w[32:40, 2:3], -1.0, ALU.mult, ALU.mult))
            for n in range(NCH):
                dve.tensor_tensor_scan(smT[32:40, n * P:(n + 1) * P], ones[32:40, :], bc[32:40, n * P:(n + 1) * P],
                                       0.0, ALU.mult, ALU.add)
            dve.tensor_copy(smT[32:40, SEQ:TOK], bc[32:40, SEQ:TOK]).then_inc(S("smT_ready"), 1)
            for i in range(2 * H):
                dve.wait_ge(S("qk_rn"), i // H + 1)
                stt(cv[:, i, :], cv[:, i, :], float(P) ** -0.5 if i < H else 1.0, rnb[:, i, :], ALU.mult, ALU.mult) \
                    .then_inc(S("qk_normed"), 1)
            dve.wait_ge(S("qk_normed"), 2 * H)
            b = full(dve, "smx")
            dve.tensor_copy(colv[:, :, :], b[:, 0:NCH * 40].rearrange("p (n c) -> p n c", n=NCH)).then_inc(emptied["D"], 1)
            dve.wait_ge(emptied["D"], upto["D"][place["smx"] + 1])
            dve.wait_ge(S("conv_done"), QT + 1)
            dve.wait_ge(S("tail_ready"), 1)
            for h in range(H):
                b = full(dve, f"gr{h}")
                for n in range(NCH):
                    ts(decM[:, n, h, :], b[:, n * P:(n + 1) * P], colv[:, n, 32 + h:33 + h], 0.0, ALU.subtract, ALU.min)
                dve.tensor_copy(eg[:, h, :], b[:, P:TOK])
                dve.tensor_copy(lastg[:, h, :], b[:, P - 1:SEQ:P]).then_inc(emptied["D"], 1)
                dve.wait_ge(emptied["D"], upto["D"][place[f"gr{h}"] + 1])
                dve.sem_inc(S("dec_raw"), 1)
            for h in range(H):
                b = full(dve, f"br{h}")
                dve.wait_ge(S("dec_masked"), h + 1)
                tt(decB[:, :, h, :], decM[:, :, h, :], b[:, 0:SEQ].rearrange("p (n c) -> p n c", n=NCH), ALU.mult)
                dve.tensor_copy(betaS[:, h, :], b[:, SEQ:TOK]).then_inc(emptied["D"], 1)
            tt(kd[:, :, :], lastg[:, :, :].rearrange("p h n -> p n h"), colv[:, :, 32:32 + H], ALU.subtract).then_inc(S("kd_raw"), 1)
            flat = lambda v: v.rearrange("p n h c -> p (n h) c")
            b4 = lambda b_: b_[:, :].rearrange("p (a c) -> p a c", a=4)
            dve.wait_ge(emptied["D"], upto["D"][place[f"br{H - 1}"] + 1])
            for q in range(NQ):
                b = full(dve, f"kk{q}")
                tt(AT[:, 4 * q:4 * q + 4, :], b4(b), flat(decB)[:, 4 * q:4 * q + 4, :], ALU.mult).then_inc(emptied["D"], 1)
                dve.wait_ge(emptied["D"], upto["D"][place[f"kk{q}"] + 1])
                dve.sem_inc(S("AT_raw"), 1)
            for q in range(NQ):
                b = full(dve, f"qk{q}")
                tt(intraT[:, 4 * q:4 * q + 4, :], b4(b), flat(decM)[:, 4 * q:4 * q + 4, :], ALU.mult).then_inc(emptied["D"], 1)
            dve.wait_ge(emptied["D"], upto["D"][place[f"qk{NQ - 1}"] + 1])
            dve.sem_inc(S("decays_used"), 1)
            beta_col = lambda q: colv[:, (4 * q) // H, (4 * q) % H:(4 * q) % H + 4].unsqueeze(2).broadcast_to([P, 4, P])
            for q in range(NQ):
                b = full(dve, f"vt{q}")
                tt(vb[:, 4 * q:4 * q + 4, :], b4(b), beta_col(q), ALU.mult).then_inc(emptied["D"], 1)
            dve.wait_ge(S("kd_exp"), 2)
            link(stt(kb1[:, :], kb1[:, :], -1.0, colv[:, 1, 0:H], ALU.mult, ALU.mult))
            kdf = kd[:, :, :].rearrange("p n h -> p (n h)")
            dve.wait_ge(S("conv_rows_out"), 32)
            for q in range(NQ):
                b = full(dve, f"kt{q}")
                last = tt(kdec[:, 4 * q:4 * q + 4, :], b4(b), kdf[:, 4 * q:4 * q + 4].unsqueeze(2).broadcast_to([P, 4, P]), ALU.mult)
                if 4 * q >= H:
                    last = tt(kbg[:, 4 * q - H:4 * q - H + 4, :], b4(b),
                              kb1[:, 4 * q - H:4 * q - H + 4].unsqueeze(2).broadcast_to([P, 4, P]), ALU.mult)
                last.then_inc(emptied["D"], 1)
            for q in range(NQ):
                dve.wait_ge(S("BT_ready"), q + 1)
                tt(XT[:, 4 * q:4 * q + 4, :], ident[:, :].unsqueeze(1).broadcast_to([P, 4, P]), BT[:, 4 * q:4 * q + 4, :], ALU.subtract) \
                    .then_inc(S("XT_ready"), 1)
            dve.wait_ge(S("XT_ready"), NQ)
            for L in range(1, LEVELS):
                for q in range(NQ):
                    b = full(dve, f"T{L}_{q}")
                    if L < LEVELS - 1:
                        b2 = full(dve, f"Q{L}_{q}")
                    if L > 1:
                        dve.wait_ge(emptied["D"], upto["D"][place[f"T{L}_{q}"]])
                    v = XT[:, 4 * q:4 * q + 4, :]
                    tt(v, v, b4(b), ALU.subtract).then_inc(emptied["D"], 1)
                    if L < LEVELS - 1:
                        v = X[:, 4 * q:4 * q + 4, :]
                        tt(v, v, b4(b2), ALU.subtract).then_inc(emptied["D"], 1)
            for q in range(2):
                b = full(dve, f"s1_{q}")
                dve.tensor_copy(S1[:, 4 * q:4 * q + 4, :], b4(b)).then_inc(emptied["D"], 1)
            dve.wait_ge(emptied["D"], upto["D"][place["s1_1"] + 1])
            tt(cv[:, 0:H, P:SEQ], cv[:, 0:H, P:SEQ], eg[:, :, 0:P], ALU.mult).then_inc(S("qg_ready"), 1)
            for q in range(2):
                b = full(dve, f"s2_{q}")
                for a in range(4):
                    h = 4 * q + a
                    last = stt(S2[:, h, :], S1[:, h, :], eg[:, h, P - 1:P], b[:, a * P:(a + 1) * P], ALU.mult, ALU.add)
                last.then_inc(emptied["D"], 1)
            dve.wait_ge(emptied["D"], upto["D"][place["s2_1"] + 1])
            dve.sem_inc(S("S2_ready"), 1)

            qv = cv[:, 0:H, SEQ:TOK]
            kv = cv[:, H:2 * H, SEQ:TOK]
            dve.tensor_copy(kS, kv)
            tt(qkS, qv, kv, ALU.mult).then_inc(S("qk_prod"), 1)
            b = full(dve, "R")
            egs = eg[:, :, P:P + NB]
            Rv = Rs.rearrange("p (h b) c -> p h b c", h=H)
            bv = b[:, 0:2 * NB * H].rearrange("p (h b c) -> p h b c", h=H, c=2)
            tt(Rv[:, :, :, 0], bv[:, :, :, 0], egs, ALU.mult)
            tt(Rv[:, :, :, 1], bv[:, :, :, 1], egs, ALU.mult).then_inc(emptied["D"], 1)
            dve.wait_ge(emptied["D"], upto["D"][place["R"] + 1])
            link(tt(verr, cv[:, 2 * H:3 * H, SEQ:TOK], Rv[:, :, :, 1], ALU.subtract))
            tt(verr, verr, betaS[:, :, :], ALU.mult).then_inc(S("verr_ready"), 1)
            dve.wait_ge(S("verr_ready"), 1)
            b = full(dve, "qkS")
            tt(qkS, b[:, 0:NB * H].rearrange("p (h b) -> p h b", h=H), verr, ALU.mult).then_inc(emptied["D"], 1)
            dve.wait_ge(emptied["D"], upto["D"][place["qkS"] + 1])
            tt(hT[:, :, SEQ:TOK], Rv[:, :, :, 0], qkS, ALU.add).then_inc(S("oT_ready"), 1)
            SsV = Ss.rearrange("p (b h) c -> p b h c", h=H)
            for t in range(NB * H // 4):
                h, b0 = t // 2, 4 * (t % 2)
                b = full(dve, f"ou{t}")
                for a in range(4):
                    v = SsV[:, b0 + a, h, :]
                    last = stt(v, v, eg[:, h, P + b0 + a:P + b0 + a + 1], b[:, a * P:(a + 1) * P], ALU.mult, ALU.add)
                last.then_inc(emptied["D"], 1)
            dve.wait_ge(emptied["D"], upto["D"][place[f"ou{NB * H // 4 - 1}"] + 1])
            dve.sem_inc(S("states_new"), NB * H // 4)
            for h in range(H):
                dve.wait_ge(S("o_rn"), 1)
                link(tt(hT[:, h, :], hT[:, h, :], rno[:, h, :], ALU.mult))
                stt(hT[:, h, :], hT[:, h, :], vecT[:, 2, 40:41], zs[:, h, :], ALU.mult, ALU.mult).then_inc(S("oT_gated"), 1)

            def mixed(l, names):
                for t in range(DT):
                    b = full(dve, f"{names}{t}")
                    residual(l, "gt_m", t, b).then_inc(emptied["D"], 1)
                    if t:
                        dve.wait_ge(emptied["D"], upto["D"][place[f"{names}{t - 1}"] + 1])
                        residual_samples(t - 1).then_inc(S("x_mixed"), 1)
                dve.wait_ge(emptied["D"], upto["D"][place[f"{names}{DT - 1}"] + 1])
                residual_samples(DT - 1).then_inc(S("x_mixed"), 1)

            def moe(l):
                norm(2 * l + 1, l, "f")
                b = full(dve, f"lg{l}")
                dve.tensor_copy(lg[:, 0:TOK], b[0:NG + NE, 0:TOK]).then_inc(emptied["D"], 1)
                b = full(dve, f"lgT{l}")
                v = b[:, 0:3 * (NG + NE)].rearrange("p (n c) -> p n c", n=3)
                tt(lt[:, :, :], v, b_route[:, l, :].unsqueeze(1).broadcast_to([P, 3, NG + NE]), ALU.add).then_inc(emptied["D"], 1)
                dve.wait_ge(emptied["D"], upto["D"][place[f"lgT{l}"] + 1])
                gl = lt[:, :, 0:NG]
                link(dve.tensor_reduce(r1[:, 0, :], gl, AX.X, ALU.max))
                gmax = r1[:, 0, :].unsqueeze(2).broadcast_to([P, 3, NG])
                tt(r4[:, :, :], gl, gmax, ALU.subtract).then_inc(S(f"gexp_raw{l}"), 1)
                link(tt(oh[:, :, :], gl, gmax, ALU.is_ge))
                link(dve.tensor_copy(r1[:, 1, :], oh[:, :, 0]))
                for q in range(1, NG):
                    link(tt(r1[:, 3, :], r1[:, 1, :], oh[:, :, q], ALU.max))
                    link(tt(oh[:, :, q], oh[:, :, q], r1[:, 1, :], ALU.is_gt))
                    link(dve.tensor_copy(r1[:, 1, :], r1[:, 3, :]))
                dve.sem_inc(S(f"oh_ready{l}"), 1)
                ev = lt[:, :, NG:].rearrange("p n (g e) -> p n g e", g=NG)
                for n in range(3):
                    last = tt(r8[:, n, :, :], ev[:, n, :, :], oh[:, n, :].unsqueeze(2).broadcast_to([P, NG, PG]), ALU.mult)
                link(last)
                link(tt(r8[:, :, 0, :], r8[:, :, 0, :], r8[:, :, 1, :], ALU.add))
                link(tt(r8[:, :, 2, :], r8[:, :, 2, :], r8[:, :, 3, :], ALU.add))
                link(tt(r8[:, :, 0, :], r8[:, :, 0, :], r8[:, :, 2, :], ALU.add))
                for n in range(3):
                    last = dve.max(mx8[:, n, :], r8[:, n, 0, :])
                link(last)
                for n in range(3):
                    last = dve.max_index(ix8[:, n, :], mx8[:, n, :], r8[:, n, 0, :])
                link(last)
                link(dve.tensor_copy(ixf[:, :, :], ix8[:, :, :]))
                tt(r1[:, 2, :], mx8[:, :, 1], mx8[:, :, 0], ALU.subtract).then_inc(S(f"e2_raw{l}"), 1)
                dve.wait_ge(S(f"gexp{l}"), 1)
                link(dve.tensor_reduce(r1[:, 4, :], r4[:, :, :], AX.X, ALU.add))
                dve.wait_ge(S(f"e2_exp{l}"), 1)
                link(ts(r1[:, 5, :], r1[:, 2, :], 1.0, None, ALU.add))
                link(tt(r1[:, 5, :], r1[:, 5, :], r1[:, 4, :], ALU.mult))
                link(dve.reciprocal(r1[:, 5, :], r1[:, 5, :]))
                link(tt(r1[:, 6, :], r1[:, 5, :], r1[:, 2, :], ALU.mult))
                io = slot_iota[:, 0:PG].unsqueeze(1).broadcast_to([P, 3, PG])
                for c_, w_ in ((0, 5), (1, 6)):
                    link(tt(r8[:, :, 2 + c_, :], io, ixf[:, :, c_:c_ + 1].broadcast_to([P, 3, PG]), ALU.is_equal))
                    link(tt(r8[:, :, 2 + c_, :], r8[:, :, 2 + c_, :], r1[:, w_, :].unsqueeze(2).broadcast_to([P, 3, PG]), ALU.mult))
                link(tt(r8[:, :, 0, :], r8[:, :, 2, :], r8[:, :, 3, :], ALU.add))
                b = full(dve, f"cum{l}")
                link(tt(r4[:, :, :], b[:, 0:3 * NG].rearrange("p (n g) -> p n g", n=3), oh[:, :, :], ALU.mult))
                link(dve.tensor_reduce(r1[:, 7, :], r4[:, :, :], AX.X, ALU.add))
                link(dve.tensor_reduce(r1[:, 0, 0:1], b[:, 3 * NG:4 * NG], AX.X, ALU.max))
                link(ts(r1[:, 0, 1:2], r1[:, 0, 0:1], float(CAP), 1.0, ALU.is_gt, ALU.add))
                link(ts(r1[:, 0, 2:3], r1[:, 0, 0:1], float(2 * CAP), None, ALU.is_gt))
                for p_ in range(MAXPASS):
                    last = ts(small_f[:, p_, :], b[:, 3 * NG:4 * NG], float(CAP * p_ + HALF), None, ALU.is_le)
                link(last)
                dve.tensor_copy(small_i[:, l, :], small_f[:, :, :].rearrange("p n g -> p (n g)"))
                dve.tensor_copy(count[:, :], b[:, 3 * NG:4 * NG])
                tt(r1[:, 0, 1:2], r1[:, 0, 1:2], r1[:, 0, 2:3], ALU.add).then_inc(emptied["D"], 1)
                dve.wait_ge(emptied["D"], upto["D"][place[f"cum{l}"] + 1])
                dve.tensor_copy(passes[:, l:l + 1], r1[:, 0, 1:2]).then_inc(S(f"passes_known{l}"), 1)
                dve.wait_ge(S(f"passes_known{l}"), 1)
                n_pass = dve.value_load(passes[0:1, l:l + 1], min_val=1, max_val=MAXPASS)
                dve.wait_ge(S("state_out"), 48)
                dve.wait_ge(S("pads_zeroed"), 1)
                dve.sem_inc(S(f"hid_done{l}"), PG)
                dve.sem_inc(S(f"x_moe{l}"), DT)
                dve.sem_inc(S(f"samples_gated{l}"), DT)
                with dve.Fori(0, n_pass) as p_:
                    ts(small_f[:, 0, :], count[:, :], float(HALF), -1.0, ALU.is_le, ALU.mult).then_inc(S(f"small_sign{l}"), 1)
                    dve.wait_ge(S(f"small_sign{l}"), p_ + 1)
                    for g_ in range(NG):
                        last = stt(small_iota[:, g_, :], upper[:, :], small_f[:, 0, g_:g_ + 1], slot_iota[:, :], ALU.mult, ALU.add)
                    last.then_inc(S(f"slots_numbered{l}"), 1)
                    dve.wait_ge(S(f"slots_numbered{l}"), p_ + 1)
                    for n in range(3):
                        rows = P if n < 2 else NB
                        for g_ in range(NG):
                            last = ts(Pm[0:rows, n, g_, :], small_iota[0:rows, g_, :], r1[0:rows, 7, n:n + 1],
                                      oh[0:rows, n, g_:g_ + 1], ALU.is_equal, ALU.mult)
                    last.then_inc(S(f"Pm_ready{l}"), 1)
                    dve.wait_ge(S(f"cmb_full{l}"), p_ + 1)
                    dve.tensor_copy(cmb[:, :], banks[4][:, 0:NG * PG]).then_inc(S(f"cmb_ready{l}"), 1)
                    dve.wait_ge(S(f"hg_ready{l}"), (p_ + 1) * DT)
                    ts(count[:, :], count[:, :], float(CAP), None, ALU.subtract)
                    ts(r1[:, 7, :], r1[:, 7, :], float(CAP), None, ALU.subtract)
                    with dve.Fori(0, NG) as g_:
                        gi = p_ * NG + g_
                        dve.wait_ge(S(f"gu_full{l}"), gi * PG + PG)
                        dve.tensor_copy(hcur, hg[:, :, bass.ds(g_ * CAP, CAP)]).then_inc(S(f"hcur_ready{l}"), 1)
                        dve.wait_ge(S(f"hid_done{l}"), gi * PG + PG)

                        def experts(c_):
                            for u in range(PG // c_):
                                dve.wait_ge(S(f"sg_ready{l}"), gi * PG + (u + 1) * c_)
                                if u >= 2:
                                    dve.wait_ge(S(f"tr_full{l}"), gi * PG + (u - 1) * c_)
                                stt(hid[:, u % 2, :], banks[u % 2][:, FF:2 * FF], ccur[:, u:u + 1], sg[:, u % 2, :],
                                    ALU.mult, ALU.mult).then_inc(S(f"hid_done{l}"), c_)

                        is_small = dve.value_load(small_i[0:1, l, bass.ds(gi, 1)], min_val=0, max_val=1)
                        with dve.If(is_small > 0):
                            cp = cmb[:, bass.ds(g_ * PG, PG)].rearrange("p (u x) -> p u x", x=2)
                            dve.tensor_copy(ccur[0:HALF, 0:PG // 2], cp[0:HALF, :, 0])
                            dve.tensor_copy(ccur[HALF:CAP, 0:PG // 2], cp[HALF:CAP, :, 1]).then_inc(S(f"ccur_ready{l}"), 1)
                            dve.wait_ge(S(f"ccur_ready{l}"), gi + 1)
                            experts(2)
                        with dve.Else():
                            dve.tensor_copy(ccur[:, :], cmb[:, bass.ds(g_ * PG, PG)]).then_inc(S(f"ccur_ready{l}"), 1)
                            dve.wait_ge(S(f"ccur_ready{l}"), gi + 1)
                            experts(1)
                    for t in range(DT):
                        dve.wait_ge(S(f"scattered{l}"), p_ * DT + t + 1)
                        residual(l, "gt_f", t, scatter_bank(l, t)).then_inc(S(f"samples_gated{l}"), 1)
                        if t:
                            dve.wait_ge(S(f"samples_gated{l}"), (p_ + 1) * DT + t)
                            residual_samples(t - 1).then_inc(S(f"x_moe{l}"), 1)
                    dve.wait_ge(S(f"samples_gated{l}"), (p_ + 2) * DT)
                    residual_samples(DT - 1).then_inc(S(f"x_moe{l}"), 1)

            mixed(0, "wo")
            moe(0)
            norm(2, 1, "m")
            dve.memset(up[:, :, 0:KS - 1], 0.0)
            dve.tensor_copy(upS[:, :, :, 0:KS - 1], sc_state[:, :, :].rearrange("p t (b k) -> p t b k", b=NB))
            for t in range(DT):
                b = full(dve, f"sg{2 * DT + t}")
                tt(up[:, t, KS - 1:], b[:, 0:SEQ], gatec[:, t, 0:SEQ], ALU.mult)
                tt(upS[:, t, :, KS - 1], b[:, SEQ:TOK], gatec[:, t, SEQ:TOK], ALU.mult).then_inc(emptied["D"], 1)
                dve.wait_ge(emptied["D"], upto["D"][place[f"sg{2 * DT + t}"] + 1])
                dve.sem_inc(S("up_ready"), 1)
                w = lambda k: vecT[:, 2, 41 + k * DT + t:42 + k * DT + t]
                y = gatec[:, t, 0:SEQ]
                link(ts(y, up[:, t, 0:SEQ], w(0), None, ALU.mult))
                for k in range(1, KS):
                    link(stt(y, up[:, t, k:k + SEQ], w(k), y, ALU.mult, ALU.add))
                ts(uptmp[:, t, :, 0], upS[:, t, :, 0], w(0), None, ALU.mult).then_inc(S("tap0"), 1)
                dve.wait_ge(S("tap0"), t + 1)
                link(stt(uptmp[:, t, :, 1], upS[:, t, :, 1], w(1), uptmp[:, t, :, 0], ALU.mult, ALU.add))
                link(stt(gatec[:, t, SEQ:TOK], upS[:, t, :, 2], w(2), uptmp[:, t, :, 1], ALU.mult, ALU.add))
                tt(gatec[:, t, :], gatec[:, t, :], gateb[:, t, :], ALU.mult).then_inc(S("sconv_y"), 1)
            mixed(1, "so")
            moe(1)
            dve.wait_ge(S("rstd_ready"), 5)
            for t in range(DT):
                stt(hT[:, t, :], xT[:, t, :], vecT[:, 2, 4 * DT + t:4 * DT + t + 1], rstd[:, :], ALU.mult, ALU.mult) \
                    .then_inc(S("h_tiles"), 1)


_INS = ["x_prompt", "x_sample", "state_gdn_S", "state_gdn_conv", "state_sconv", "c_prompt", "c_sample",
        "norm_mix_g", "norm_ffn_g", "norm_final_g", "w_ada", "b_ada", "gdn_w_in", "gdn_conv_w", "gdn_A_log",
        "gdn_dt_bias", "gdn_norm_g", "gdn_w_out", "sc_w_in", "sc_conv_w", "sc_w_out", "moe_w_group",
        "moe_b_group", "moe_w_router", "moe_b_router", "moe_w_gate", "moe_w_up", "moe_w_down"]


def kernel(**inputs):
    import numpy as _np
    import concourse.bacc as _bacc
    from concourse import mybir as _mybir
    from concourse.bass_utils import run_bass_kernel_spmd as _run

    nc = _bacc.Bacc("TRN2", target_bir_lowering=False, num_devices=1)
    arrays, aps = {}, {}
    for name in _INS:
        a = _np.ascontiguousarray(inputs[name])
        arrays[f"in_{name}_dram"] = a
        aps[name] = nc.dram_tensor(f"in_{name}_dram", a.shape, _mybir.dt.from_np(a.dtype), kind="ExternalInput").ap()
    S_, cv_, sc_ = inputs["state_gdn_S"].shape, inputs["state_gdn_conv"].shape, inputs["state_sconv"].shape
    B = inputs["x_prompt"].shape[0]
    shapes = [inputs["x_prompt"].shape, inputs["x_sample"].shape, (S_[0], B) + S_[2:], (cv_[0], B) + cv_[2:],
              (sc_[0], B) + sc_[2:], S_, cv_, sc_]
    outs = [nc.dram_tensor(f"out_{i}_dram", tuple(s), _mybir.dt.float32, kind="ExternalOutput").ap()
            for i, s in enumerate(shapes)]
    hybrid_step(nc, aps, outs)
    r = _run(nc, [arrays], core_ids=[0])
    return tuple(r.results[0][f"out_{i}_dram"] for i in range(len(shapes)))
```

```python
from contextlib import ExitStack

import concourse.bass as bass
from concourse import mybir

F32 = mybir.dt.float32
I32 = mybir.dt.int32
U32 = mybir.dt.uint32
ALU = mybir.AluOpType
ACT = mybir.ActivationFunctionType
AX = mybir.AxisListType

P = 128


def hybrid_step(nc, A, O):
    (y_prompt, y_sample, S_prompt_out, conv_prompt_out, sconv_prompt_out,
     S_sample_out, conv_sample_out, sconv_sample_out) = O
    SEQ, D = A["x_prompt"].shape[1:]
    NB = A["x_sample"].shape[0]
    DT = D // P
    H = A["state_gdn_S"].shape[2]
    QT = A["gdn_conv_w"].shape[2] // P
    NCH = SEQ // P
    TOK = SEQ + NB
    MODS = 1 + NB
    KC = A["gdn_conv_w"].shape[1]
    KS = A["sc_conv_w"].shape[1]
    NG = A["moe_w_group"].shape[2]
    NE = A["moe_w_router"].shape[2]
    PG = NE // NG
    FF = A["moe_w_gate"].shape[3]
    ADA = 6 * D // 512
    CAP = P
    HALF = CAP // 2
    MAXPASS = -(-TOK // CAP)
    EPS = 1e-6
    NM = NCH * H
    NQ = NM // 4
    LEVELS = P.bit_length() - 1
    PART = {"sh_m": 0, "sc_m": 1, "gt_m": 2, "sh_f": 3, "sc_f": 4, "gt_f": 5}

    with ExitStack() as ctx:
        def sb(name, shape, dt=F32):
            return ctx.enter_context(nc.sbuf_tensor(name, shape, dt))

        sems = {}

        def S(name):
            if name not in sems:
                sems[name] = ctx.enter_context(nc.semaphore(name))
            return sems[name]

        class Link:

            def __init__(self, eng, name):
                self.eng, self.sem, self.n = eng, S(name), 0

            def __call__(self, ins):
                self.n += 1
                ins.then_inc(self.sem, 1)
                self.eng.wait_ge(self.sem, self.n)

        xT = sb("xT", [P, DT, TOK])
        hT = sb("hT", [P, DT, TOK])
        ident = sb("ident", [P, P])
        ones = sb("ones", [P, P])
        causal = sb("causal", [P, P])
        strict = sb("strict", [P, P])
        slot_iota = sb("slot_iota", [P, P])
        vecT = sb("vecT", [P, 3, P])
        cT = sb("cT", [P, DT, 32])
        mT = sb("mT", [P, 2, 6 * DT, MODS])
        gain = sb("gain", [P, DT, MODS])
        w_route = sb("w_route", [P, 2, DT, NG + NE])
        b_route = sb("b_route", [P, 2, NG + NE])
        w_ba = sb("w_ba", [P, DT, 40])
        decay_w = sb("decay_w", [P, 4])
        epsc = sb("epsc", [P, 4])
        rstd = sb("rstd", [P, TOK])
        sc_state = sb("sc_state", [P, DT, 2 * NB])
        x_new = sb("x_new", [P, DT, NB])
        passes = sb("passes", [P, 2], I32)
        small_i = sb("small_i", [P, 2, MAXPASS * NG], I32)
        small_f = sb("small_f", [P, MAXPASS, NG])
        count = sb("count", [P, NG])
        upper = sb("upper", [P, P])
        ada_row = sb("ada_row", [P, 512])
        ada_sum = sb("ada_sum", [P, 4, MODS])
        NSTAT, NRING = 3, 6
        ring_lo = sb("ring_lo", [P, NSTAT, DT * 512])
        ARENA = 28992
        arena = sb("arena", [P, ARENA])
        slots = [ring_lo[:, s, :] for s in range(NSTAT)] + \
                [arena[:, s * 4096:(s + 1) * 4096] for s in range(NRING - NSTAT)]

        class Area:

            def __init__(self, at):
                self.at = at

            def take(self, *dims):
                n = 1
                for d in dims:
                    n *= d
                v = arena[:, self.at:self.at + n]
                self.at += n
                assert self.at <= ARENA, self.at
                if len(dims) == 1:
                    return v
                names = "abcd"[:len(dims)]
                return v.rearrange(f"p ({' '.join(names)}) -> p {' '.join(names)}",
                                   **{k: d for k, d in zip(names[1:], dims[1:])})

        g = Area(0)
        cv = g.take(QT, TOK)
        zs = g.take(H, TOK)
        AT = g.take(NM, P)
        intraT = g.take(NM, P)
        eg = g.take(H, P + NB)
        vb = g.take(NM, P)
        kdec = g.take(NM, P)
        kbg = g.take(H, P)
        vnew = g.take(H, P)
        S1 = g.take(H, P)
        work = g.at
        X = g.take(NM, P)
        PX = g.take(NM, P)
        BT = g.take(NM, P)
        XT = g.take(NM, P)
        g = Area(work)
        pre = g.take(QT, KC - 1 + SEQ)
        preS = g.take(QT, NB, KC)
        g = Area(work)
        decM = g.take(NCH, H, P)
        decB = g.take(NCH, H, P)
        g = Area(work)
        Ss = g.take(NB * H, P)
        wT = AT[:, 0:H, :]
        vnew1 = AT[:, H:NM, :]
        S2 = kbg
        levels = sb("levels", [P, LEVELS, P])
        small_iota = levels[:, 0:NG, :]
        e = Area(QT * TOK + H * TOK)
        x_rows = e.take(NCH, D)
        xs_rows = e.take(D)
        c_rows = e.take(D)
        vec_rows = e.take(3, P)
        sc_rows = e.take(D)
        cs_rows = e.take(QT * P)
        convtmp = e.take(QT, NB, KC)
        assert e.at <= work
        e = Area(QT * TOK + H * TOK)
        sqo = e.take(H, TOK)
        e = Area(work + QT * (KC - 1 + SEQ) + QT * NB * KC)
        sqb = e.take(4, TOK)
        e = Area(work)
        rnb = e.take(2 * H, TOK)
        e = Area(QT * TOK + H * TOK)
        slots += [e.take(DT * 512) for _ in range(2)]
        tail = e.take(QT, 3 + NB)
        e2 = Area(QT * TOK + H * TOK + 2 * NM * P + H * (P + NB) + 2 * NM * P)
        tail_rows = e2.take(QT * P)
        smT = sb("smT", [P, TOK])
        ba = sb("ba", [40, TOK])
        bb = sb("bb", [40, TOK])
        bc = sb("bc", [40, TOK])
        colv = sb("colv", [P, NCH, 40])
        lastg = sb("lastg", [P, H, NCH])
        kd = sb("kd", [P, NCH, H])
        kb1 = sb("kb1", [P, H])
        betaS = sb("betaS", [P, H, NB])
        spare = [v.rearrange("p n c -> p (n c)") for v in (kdec, vnew)]
        fit = NM * P // TOK
        sqx = [spare[t // fit][:, t % fit * TOK:(t % fit + 1) * TOK] for t in range(DT)]
        Rs = vb[:, 0, :].rearrange("p (r c) -> p r c", c=2)
        kS = vb[:, 1, 0:NB * H].rearrange("p (h b) -> p h b", h=H)
        qkS = vb[:, 1, NB * H:2 * NB * H].rearrange("p (h b) -> p h b", h=H)
        verr = vb[:, 2, 0:NB * H].rearrange("p (h b) -> p h b", h=H)
        k_rows = vb[:, 3, :]
        qk_pairs = vb[:, 5:7, :].rearrange("p a c -> p (a c)")[:, 0:2 * NB * H + 32]
        R_rows = kdec
        v_rows = vb[:, 4, :]
        spread = vb[:, 8:16, :].rearrange("p (t r) c -> p t r c", t=2)

        m = Area((NRING - NSTAT) * 4096)
        hg = m.take(DT, NG * CAP)
        hcur = m.take(DT, CAP)
        ycur = m.take(D)
        htok = m.take(3, D)
        Pm = m.take(3, NG, CAP)
        sg = m.take(2, FF)
        hid = m.take(2, FF)
        hidT = m.take(2, 2, CAP)
        PT = m.take(1 + NG, TOK)
        lg = sb("lg", [NG + NE, 3 * P])
        lt = sb("lt", [P, 3, NG + NE])
        r4 = sb("r4", [P, 3, NG])
        oh = sb("oh", [P, 3, NG])
        r8 = sb("r8", [P, 3, 4, PG])
        mx8 = sb("mx8", [P, 3, 8])
        ix8 = sb("ix8", [P, 3, 8], U32)
        ixf = sb("ixf", [P, 3, 8])
        r1 = sb("r1", [P, 8, 3])
        cmb = sb("cmb", [P, NG * PG])
        ccur = sb("ccur", [P, PG])
        c = Area((NRING - NSTAT) * 4096)
        gateb = c.take(DT, TOK)
        gatec = c.take(DT, TOK)
        up = c.take(DT, KS - 1 + SEQ)
        upS = c.take(DT, NB, KS)
        uptmp = c.take(DT, NB, KS)
        tail2 = c.take(DT, 2 + NB)
        tail2_rows = c.take(D)
        c = Area(0)
        y_rows = c.take(NCH, D)
        ys_rows = c.take(D)

        sqh = [hT[:, t, :] for t in range(DT)]
        def ou_matrices(t):
            h, b0 = t % H, 4 * (t // H)
            return h, b0, h * NB + b0

        banks = [ctx.enter_context(nc.psum_tensor(f"bank{i}", [P, 512], F32)) for i in range(8)]

        order = []

        def tiles(*names, by):
            order.extend((n, by) for n in names)

        tiles("c", by="A")
        tiles("xs", "x0", "x1", "x2", "x3", by="D")
        tiles("vec", by="A")
        tiles("cs0", "cs1", "sc", by="D")

        ada_first = [(0, i) for i in range(2 * DT * P // 512)]
        ada_later = [(l, i) for l in range(2) for i in range(ADA) if (l, i) not in ada_first]
        WIN = (QT + H) // 4
        ada_after = [ada_later[len(ada_later) * j // WIN:len(ada_later) * (j + 1) // WIN] for j in range(WIN)]

        def ada_tiles(pieces):
            for n, (l, i) in enumerate(pieces):
                tiles(f"ada{l}_{i}", by="A")
                if n:
                    tiles("adaT%d_%d" % pieces[n - 1], by="D")
            tiles("adaT%d_%d" % pieces[-1], by="D")

        tiles("ss0", by="A")
        ada_tiles(ada_first)
        tiles("ba", by="D")
        for j in range(WIN):
            tiles(*[f"in{i}" for i in range(4 * j, 4 * j + 4)], by="A")
            ada_tiles(ada_after[j])
            if j == QT // 4:
                tiles(*[f"cb{i}" for i in range(QT // 4)], by="A")
                tiles(*[f"l2_{i}" for i in range(2 * H)], by="A")
        tiles("smx", by="D")
        tiles(*[f"gr{h}" for h in range(H)], by="D")
        tiles(*[f"br{h}" for h in range(H)], by="D")
        tiles(*[f"kk{q}" for q in range(NQ)], by="D")
        tiles(*[f"qk{q}" for q in range(NQ)], by="D")
        tiles(*[f"xt{q}" for q in range(NQ)], by="A")
        tiles(*[f"vt{q}" for q in range(NQ)], by="D")
        tiles(*[f"kt{q}" for q in range(NQ)], by="D")
        for L in range(1, LEVELS):
            tiles(*[f"P{L}_{q}" for q in range(NQ)], by="A")
            for q in range(NQ):
                tiles(f"T{L}_{q}", by="D")
                if L < LEVELS - 1:
                    tiles(f"Q{L}_{q}", by="D")
        for q in range(2):
            tiles(f"u0_{q}", by="A")
        for q in range(2):
            tiles(f"s1_{q}", by="D")
        for q in range(2):
            tiles(f"o0_{q}", by="A")
        for q in range(2):
            tiles(f"w_{q}", by="A")
        for q in range(2):
            tiles(f"u1_{q}", by="A")
        for q in range(2):
            tiles(f"o1_{q}", by="A")
        for q in range(2):
            tiles(f"s2_{q}", by="D")
        tiles(*[f"R{u}" for u in range(NB * H // 16)], by="A")
        tiles(*[f"RT{u}" for u in range(NB * H // 16)], by="D")
        tiles("qkS", by="D")
        tiles("rw", by="A")
        tiles(*[f"on{h}" for h in range(H)], by="A")
        OU = NB * H // 4
        ou_after = lambda i: range(min(OU // 2 + 2 * i, OU), min(OU // 2 + 2 * i + 2, OU))
        tiles(*[f"ou{t}" for t in range(OU // 2)], by="D")
        for i in range(DT):
            tiles(f"wo{i}", by="D")
            tiles(*[f"ou{t}" for t in ou_after(i)], by="D")
        for l in range(2):
            if l == 1:
                tiles("ss2", by="A")
                tiles(*[f"sg{i}" for i in range(2 * DT)], by="A")
                tiles(*[f"sg{i}" for i in range(2 * DT, 3 * DT)], by="D")
                tiles(*[f"st{i}" for i in range(DT // 4)], by="A")
                tiles(*[f"so{i}" for i in range(DT)], by="D")
            tiles(f"ss{2 * l + 1}", by="A")
            tiles(f"lg{l}", f"lgT{l}", by="D")
            tiles(*[f"ht{l}_{i}" for i in range(6)], by="A")
            tiles(f"cum{l}", by="D")
        tiles("ss4", by="A")
        tiles(*[f"y{i}" for i in range(6)], by="A")

        place = {n: i for i, (n, _) in enumerate(order)}
        upto = {e: [0] for e in "AD"}
        for _, by in order:
            for e_ in "AD":
                upto[e_].append(upto[e_][-1] + (e_ in by))
        emptied = {"A": S("bank_emptied_by_scalar"), "D": S("bank_emptied_by_vector")}
        bank_full = S("bank_full")

        def bank_of(name):
            return banks[place[name] % 8]

        def claim(pe, name):
            i = place[name]
            if i >= 8:
                for e_ in order[i - 8][1]:
                    pe.wait_ge(emptied[e_], upto[e_][i - 7])
            return banks[i % 8]

        def full(eng, name):
            eng.wait_ge(bank_full, place[name] + 1)
            return bank_of(name)

        wa, wi = A["w_ada"], A["gdn_w_in"]
        col512 = lambda w, c_: w[:, c_ * 512:(c_ + 1) * 512].rearrange("(t p) n -> p t n", p=P)
        stream = [(f"ada{l}", i, col512(wa[l], i)) for l, i in ada_first]
        for j in range(WIN):
            stream += [("win", j, col512(wi[0], j))] + [(f"ada{l}", i, col512(wa[l], i)) for l, i in ada_after[j]]
        stream += [("wout", i, col512(A["gdn_w_out"][0], i)) for i in range(D // 512)]
        early = len(stream)
        stream += [("scin", i, col512(A["sc_w_in"][0], i)) for i in range(3 * D // 512)]
        stream += [("scout", i, col512(A["sc_w_out"][0], i)) for i in range(D // 512)]
        EARLY_SLOTS = [0, 1, 2, NRING, NRING + 1]
        FIRST_SLOT = [NSTAT, NSTAT, (NSTAT + len(stream) - early) % NRING]
        moe_slot = lambda l, f: (f + FIRST_SLOT[2 * l]) % NRING
        where, uses = {}, [0] * len(slots)
        for n, (kind, i, _) in enumerate(stream):
            if kind == "wout":
                s = i
            elif n < early:
                s = EARLY_SLOTS[n % len(EARLY_SLOTS)]
            else:
                s = (n - early + FIRST_SLOT[1]) % NRING
            where[kind, i] = (s, uses[s])
            uses[s] += 1
        release, in_slot = {}, {}
        for n, (kind, i, _) in enumerate(stream):
            if kind.startswith("ada"):
                release[kind, i] = (bank_full, place[f"{kind}_{i}"] + 1)
            else:
                last_tile = {"win": "in", "wout": "wo", "scin": "sg", "scout": "so"}[kind]
                release[kind, i] = (bank_full, place[f"{last_tile}{4 * i + 3}"] + 1)
            in_slot[where[kind, i]] = (kind, i)
        last_early = [max(n for n in range(early) if where[stream[n][0:2]][0] == s) for s in range(NSTAT)]
        filled = [S(f"slot_filled{s}") for s in range(len(slots))]
        moe_filled = [[S(f"moe_filled{l}_{s}") for s in range(NRING)] for l in range(2)]

        def slot_of(pe, kind, i):
            s, u = where[kind, i]
            pe.wait_ge(filled[s], 32 * (u + 1))
            return slots[s].rearrange("p (t n) -> p t n", n=512)

        block = ctx.enter_context(nc.Block())

        @block.sync
        def _(sp):
            def fill(n):
                kind, i, src = stream[n]
                s, u = where[kind, i]
                if u:
                    sp.wait_ge(*release[in_slot[s, u - 1]])
                elif s >= NRING:
                    sp.wait_ge(bank_full, place["sc"] + 1)
                dst = slots[s].rearrange("p (t n) -> p t n", n=512)
                for half in range(2):
                    sp.dma_start(dst[:, 4 * half:4 * half + 4, :], src[:, 4 * half:4 * half + 4, :]) \
                        .then_inc(filled[s], 16)

            sp.dma_start(x_rows, A["x_prompt"][0].rearrange("(n p) d -> p n d", p=P)).then_inc(S("rows_loaded"), 16)
            sp.dma_start(cs_rows[0:NB * (KC - 1), :], A["state_gdn_conv"][0].rearrange("b k c -> (b k) c")).then_inc(S("rows_loaded"), 16)
            sp.dma_start(sc_rows[0:NB * (KS - 1), :], A["state_sconv"][0].rearrange("b k c -> (b k) c")).then_inc(S("rows_loaded"), 16)
            sp.wait_ge(S("rows_loaded"), 13 * 16)
            for n in range(early):
                fill(n)

            def wait_moe_fill(l, groups, f):
                pair, part = divmod(f, 3)
                if part < 2:
                    sp.wait_ge(S(f"gu_full{l}"), groups * PG + 2 * pair + part + 1)
                else:
                    sp.wait_ge(S(f"dn_done{l}"), groups * PG + 2 * pair + 2)

            def moe_fills(l, gi, g_):
                for f in range(12):
                    s = moe_slot(l, f)
                    if f < NRING:
                        wait_moe_fill(l, gi, f + NRING)
                    else:
                        wait_moe_fill(l, gi + 1, f - NRING)
                    pair, part = f // 3, f % 3
                    if part < 2:
                        dst = slots[s].rearrange("p (t n) -> p t n", n=512)
                        e_ = bass.ds(g_ * PG + 2 * pair + part, 1)
                        for half, w in enumerate((A["moe_w_gate"], A["moe_w_up"])):
                            sp.dma_start(dst[:, :, half * FF:(half + 1) * FF],
                                         w[l, e_, :, :].rearrange("e (t p) n -> p (e t) n", p=P)) \
                                .then_inc(moe_filled[l][s], 16)
                    else:
                        dst = slots[s].rearrange("p (e t n) -> p e t n", e=2, t=2)
                        for half in range(2):
                            e_ = bass.ds(g_ * PG + 2 * pair + half, 1)
                            sp.dma_start(dst[:, half, :, :],
                                         A["moe_w_down"][l, e_, :, :].rearrange("e (t p) n -> p (e t) n", p=P)) \
                                .then_inc(moe_filled[l][s], 16)

            for l in range(2):
                if l == 0:
                    for s in range(NSTAT):
                        sp.wait_ge(*release[stream[last_early[s]][0:2]])
                    sp.wait_ge(S("oT_gated"), H)
                else:
                    for s in range(NRING):
                        sp.wait_ge(*release[in_slot[s, uses[s] - 1]])
                sp.sem_inc(S(f"gu_full{l}"), PG)
                sp.sem_inc(S(f"dn_done{l}"), PG)
                with sp.Fori(0, NG) as g_:
                    moe_fills(l, g_, g_)
                sp.wait_ge(S(f"passes_known{l}"), 1)
                n_pass = sp.value_load(passes[0:1, l:l + 1], min_val=1, max_val=MAXPASS)
                with sp.If(n_pass > 1):
                    with sp.Fori(1, n_pass) as p_:
                        with sp.Fori(0, NG) as g_:
                            moe_fills(l, p_ * NG + g_, g_)
                if l == 0:
                    for n in range(early, len(stream)):
                        if n - early < NRING:
                            wait_moe_fill(l, n_pass * NG, n - early + NRING)
                        fill(n)
            for n in range(NCH):
                sp.wait_ge(S("y_ready"), 2 * (n + 1))
                sp.dma_start(y_prompt[0, n * P:(n + 1) * P, :], y_rows[:, n, :]).then_inc(S("y_out"), 16)
            sp.wait_ge(S("y_ready"), 6)
            sp.dma_start(y_sample.rearrange("b s d -> (b s) d"), ys_rows[0:NB, :]).then_inc(S("y_out"), 16)
            sp.wait_ge(S("y_out"), 16 * (NCH + 1))
            sp.wait_ge(S("state_copied"), 32)
            sp.wait_ge(S("state_out"), 48)
            sp.wait_ge(S("conv_rows_out"), 32)
            sp.wait_ge(S("sconv_rows_out"), 32)

        @block.gpsimd
        def _(pool):
            link = Link(pool, "pool_link")
            pool.memset(ident[:, :], 0.0)
            pool.memset(ones[:, :], 1.0)
            pool.memset(causal[:, :], 1.0)
            pool.memset(strict[:, :], 1.0)
            pool.memset(levels[:, :, :], 0.0)
            pool.memset(cT[:, :, :], 0.0)
            pool.memset(epsc[:, 0:1], EPS)
            pool.memset(epsc[:, 1:2], 0.0)
            link(pool.memset(epsc[:, 2:3], 1.0))
            for L in range(LEVELS):
                s = 1 << L
                half = levels[:, L, :].rearrange("p (b h c) -> p b h c", h=2, c=s)[:, :, 1, :]
                last = pool.memset(half, 1.0)
            link(last)
            pool.affine_select(out=ident[:, :], in_=ident[:, :], compare_op=ALU.not_equal, fill=1.0, base=0,
                               pattern=[[-1, P]], channel_multiplier=1)
            pool.affine_select(out=causal[:, :], in_=causal[:, :], compare_op=ALU.is_ge, fill=0.0, base=0,
                               pattern=[[1, P]], channel_multiplier=-1)
            pool.affine_select(out=strict[:, :], in_=strict[:, :], compare_op=ALU.is_gt, fill=0.0, base=0,
                               pattern=[[1, P]], channel_multiplier=-1)
            pool.iota(slot_iota[:, :], pattern=[[1, P]], base=0, channel_multiplier=0,
                      allow_small_or_imprecise_dtypes=True)
            for L in range(LEVELS):
                s = 1 << L
                half = levels[:, L, :].rearrange("p (b h c) -> p b h c", h=2, c=s)[:, :, 1, :]
                last = pool.affine_select(out=half, in_=half, compare_op=ALU.is_ge, fill=0.0, base=0,
                                          pattern=[[-2 * s, P // (2 * s)], [0, s]], channel_multiplier=1)
            pool.memset(upper[:, 0:HALF], 0.0)
            last = pool.memset(upper[:, HALF:], float(HALF))
            link(last)
            for L in range(LEVELS):
                s = 1 << L
                half = levels[:, L, :].rearrange("p (b h c) -> p b h c", h=2, c=s)[:, :, 1, :]
                last = pool.affine_select(out=half, in_=half, compare_op=ALU.is_ge, fill=0.0, base=s - 1,
                                          pattern=[[2 * s, P // (2 * s)], [0, s]], channel_multiplier=-1)
            last.then_inc(S("consts"), 1)
            pool.memset(pre[:, :, 0:KC - 1], 0.0).then_inc(S("pre_zeroed"), 1)
            pool.wait_ge(S("pre_ready"), QT)
            pool.tensor_copy(tail[:, :, 0:KC - 1], pre[:, :, SEQ:SEQ + KC - 1])
            pool.tensor_copy(tail[:, :, KC - 1:], preS[:, :, :, KC - 1]).then_inc(S("tail_ready"), 1)
            pool.wait_ge(S("cv_ready"), QT + 1)
            for i in range(0, 2 * H, 2):
                if i >= 4:
                    pool.wait_ge(bank_full, place[f"l2_{i - 4}"] + 1)
                pool.tensor_tensor(sqb[:, i % 4, :], cv[:, i, :], cv[:, i, :], ALU.mult).then_inc(S("sq_even"), 1)
            for h in range(H):
                pool.wait_ge(S("dec_exp"), h + 1)
                pool.tensor_tensor(decM[:, :, h, :], decM[:, :, h, :],
                                   causal[:, :].unsqueeze(1).broadcast_to([P, NCH, P]), ALU.mult) \
                    .then_inc(S("dec_masked"), 1)
            for L in range(LEVELS):
                for q in range(NQ):
                    if L == 0:
                        pool.wait_ge(S("AT_raw"), q + 1)
                    elif L >= 2:
                        pool.wait_ge(bank_full, place[f"P{L - 1}_{q}"] + 1)
                    else:
                        pool.wait_ge(S("XT_ready"), q + 1)
                    pool.tensor_tensor(BT[:, 4 * q:4 * q + 4, :], AT[:, 4 * q:4 * q + 4, :],
                                       levels[:, L, :].unsqueeze(1).broadcast_to([P, 4, P]), ALU.mult) \
                        .then_inc(S("BT_ready"), 1)
            pool.wait_ge(S("oT_ready"), 4)
            pool.wait_ge(bank_full, place["s2_1"] + 1)
            for h in range(H):
                pool.tensor_tensor(sqo[:, h, 0:SEQ], hT[:, h, 0:SEQ], hT[:, h, 0:SEQ], ALU.mult).then_inc(S("osq_ready"), 1)
            pool.wait_ge(bank_full, place["u1_1"] + 1)
            pool.wait_ge(S("osq_ready"), H)
            pool.memset(k_rows[NB * H:96, :], 0.0)
            link(pool.memset(spread[NB * H:96, :, :, :], 0.0))
            pool.wait_ge(S("rows_ready"), 2)
            for t in range(OU):
                if t >= 2:
                    pool.wait_ge(bank_full, place[f"ou{t - 2}"] + 1)
                r = ou_matrices(t)[2]
                pool.tensor_tensor(spread[0:NB * H, t % 2, :, :],
                                   v_rows[0:NB * H, :].unsqueeze(1).broadcast_to([NB * H, 4, P]),
                                   ident[0:NB * H, r:r + 4].unsqueeze(2).broadcast_to([NB * H, 4, P]),
                                   ALU.mult).then_inc(S("spread_ready"), 1)
            pool.wait_ge(S("state_out"), 48)
            pool.memset(htok[:, 2, :], 0.0)
            pool.memset(Pm[:, 2, :, :], 0.0).then_inc(S("pads_zeroed"), 1)
            pool.wait_ge(S("up_ready"), DT)
            pool.tensor_copy(tail2[:, :, 0:KS - 1], up[:, :, SEQ:SEQ + KS - 1])
            pool.tensor_copy(tail2[:, :, KS - 1:], upS[:, :, :, KS - 1]).then_inc(S("tail2_ready"), 1)

        @block.scalar
        def _(act):
            link = Link(act, "act_link")
            ld = S("rows_loaded")
            act.dma_start(c_rows[0:1, :], A["c_prompt"]).then_inc(ld, 16)
            act.dma_start(c_rows[1:1 + NB, :], A["c_sample"]).then_inc(ld, 16)
            act.dma_start(vec_rows[0:96, 0, :], A["b_ada"].rearrange("l (t p) -> (l t) p", p=P)).then_inc(ld, 16)
            act.dma_start(vec_rows[0:96, 1, :], A["gdn_conv_w"].rearrange("o k (t p) -> (o k t) p", p=P)).then_inc(ld, 16)
            act.dma_start(vec_rows[0:16, 2, :], A["norm_mix_g"].rearrange("l (t p) -> (l t) p", p=P)).then_inc(ld, 16)
            act.dma_start(vec_rows[16:32, 2, :], A["norm_ffn_g"].rearrange("l (t p) -> (l t) p", p=P)).then_inc(ld, 16)
            act.dma_start(vec_rows[32:40, 2, :], A["norm_final_g"].rearrange("(t p) -> t p", p=P)).then_inc(ld, 16)
            act.dma_start(vec_rows[40:41, 2, :], A["gdn_norm_g"]).then_inc(ld, 16)
            act.dma_start(vec_rows[41:65, 2, :], A["sc_conv_w"].rearrange("o k (t p) -> (o k t) p", p=P)).then_inc(ld, 16)
            act.dma_start(xs_rows[0:NB, :], A["x_sample"].rearrange("b s d -> (b s) d")).then_inc(ld, 16)
            wl = S("small_weights")
            with nc.allow_non_contiguous_dma(reason="narrow weights, once"):
                act.dma_start(decay_w[32:40, 0:1], A["gdn_A_log"].rearrange("o h -> h o")).then_inc(wl, 16)
                act.dma_start(decay_w[32:40, 1:2], A["gdn_dt_bias"].rearrange("o h -> h o")).then_inc(wl, 16)
                act.wait_ge(S("w_ba_zeroed"), 1)
                narrow = A["gdn_w_in"][0].rearrange("(t p) n -> p t n", p=P)
                act.dma_start(w_ba[:, :, 0:H], narrow[:, :, 4 * D:4 * D + H]).then_inc(wl, 16)
                act.dma_start(w_ba[:, :, 32:32 + H], narrow[:, :, 4 * D + H:4 * D + 2 * H]).then_inc(wl, 16)
                for l in range(2):
                    act.dma_start(w_route[:, l, :, 0:NG], A["moe_w_group"][l].rearrange("(t p) n -> p t n", p=P)).then_inc(wl, 16)
                    act.dma_start(w_route[:, l, :, NG:], A["moe_w_router"][l].rearrange("(t p) n -> p t n", p=P)).then_inc(wl, 16)
                    act.dma_start(b_route[:, l, 0:NG], A["moe_b_group"][l:l + 1, :].to_broadcast([P, NG])).then_inc(wl, 16)
                    act.dma_start(b_route[:, l, NG:], A["moe_b_router"][l:l + 1, :].to_broadcast([P, NE])).then_inc(wl, 16)
            act.dma_start(conv_sample_out[0, :, 0:KC - 2, :], A["state_gdn_conv"][0, :, 1:KC - 1, :]).then_inc(S("state_copied"), 16)
            act.dma_start(sconv_sample_out[0, :, 0:KS - 2, :], A["state_sconv"][0, :, 1:KS - 1, :]).then_inc(S("state_copied"), 16)

            b = full(act, "c")
            act.wait_ge(S("consts"), 1)
            act.activation(cT[:, :, 0:MODS], b[:, 0:DT * MODS].rearrange("p (t c) -> p t c", c=MODS), ACT.Silu) \
                .then_inc(emptied["A"], 1)
            b = full(act, "vec")
            act.activation(vecT[:, 0, 0:96], b[:, 0:96], ACT.Copy)
            act.activation(vecT[:, 1, 0:96], b[:, P:P + 96], ACT.Copy)
            act.activation(vecT[:, 2, 0:65], b[:, 2 * P:2 * P + 65], ACT.Copy).then_inc(emptied["A"], 1)

            def ada(pieces):
                for l, i in pieces:
                    b = full(act, f"ada{l}_{i}")
                    n = (ada_first + ada_later).index((l, i))
                    if n:
                        full(act, "adaT%d_%d" % (ada_first + ada_later)[n - 1])
                    act.activation(ada_row[:, :], b[:, :], ACT.Copy).then_inc(emptied["A"], 1)

            def norm(k, ready, n, squares=sqh):
                for t in range(DT):
                    act.wait_ge(ready, n(t))
                    act.activation(squares[t], xT[:, t, :], ACT.Square).then_inc(S("sq_x"), 1)
                b = full(act, f"ss{k}")
                act.activation(rstd[:, :], b[:, 0:TOK], ACT.Ln, bias=epsc[:, 0:1], scale=1.0 / D).then_inc(emptied["A"], 1)
                act.wait_ge(emptied["A"], upto["A"][place[f"ss{k}"] + 1])
                act.activation(rstd[:, :], rstd[:, :], ACT.Exp, scale=-0.5).then_inc(S("rstd_ready"), 1)

            def shift_tiles(k):
                shift = mT[:, k // 2, PART["sh_m" if k % 2 == 0 else "sh_f"] * DT:, :]
                for t in range(DT):
                    act.wait_ge(S("h_scaled"), k * DT + t + 1)
                    act.activation(hT[:, t, 0:SEQ], hT[:, t, 0:SEQ], ACT.Identity, bias=shift[:, t, 0:1]) \
                        .then_inc(S("h_tiles"), 1)

            norm(0, emptied["D"], lambda t: upto["D"][place["x3"] + 1])
            ada(ada_first)
            shift_tiles(0)

            act.wait_ge(emptied["D"], upto["D"][place["ba"] + 1])
            act.activation(bb[0:8, :], ba[0:8, :], ACT.Exp, scale=-1.0).then_inc(S("beta_exp"), 1)
            act.activation(decay_w[32:40, 2:3], decay_w[32:40, 0:1], ACT.Exp).then_inc(S("beta_exp"), 1)
            act.wait_ge(S("abs_a"), 1)
            link(act.activation(bb[32:40, :], bb[32:40, :], ACT.Exp, scale=-1.0))
            act.activation(bb[32:40, :], bb[32:40, :], ACT.Ln, bias=epsc[32:40, 2:3]).then_inc(S("softplus_ln"), 1)

            for i in range(QT + H):
                if i < QT:
                    b = full(act, f"in{i}")
                    act.activation(pre[:, i, KC - 1:], b[:, 0:SEQ], ACT.Copy)
                    act.activation(preS[:, i, :, KC - 1], b[:, SEQ:TOK], ACT.Copy).then_inc(emptied["A"], 1)
                    act.wait_ge(emptied["A"], upto["A"][place[f"in{i}"] + 1])
                    act.sem_inc(S("pre_ready"), 1)
                elif i < QT + H:
                    b = full(act, f"in{i}")
                    act.activation(zs[:, i - QT, :], b[:, 0:TOK], ACT.Silu).then_inc(emptied["A"], 1)
                if 2 <= i < QT + 2:
                    act.wait_ge(S("conv_done"), i - 1)
                    act.activation(cv[:, i - 2, 0:SEQ], cv[:, i - 2, 0:SEQ], ACT.Silu).then_inc(S("cv_ready"), 1)
                if i == QT + 2:
                    act.wait_ge(S("conv_done"), QT + 1)
                    act.activation(cv[:, :, SEQ:TOK], cv[:, :, SEQ:TOK], ACT.Silu).then_inc(S("cv_ready"), 1)
                if i % 4 == 3:
                    ada(ada_after[i // 4])
                if i == QT + 3:
                    for j in range(QT // 4):
                        b = full(act, f"cb{j}")
                        act.activation(tail_rows[0:3 + NB, j * 512:(j + 1) * 512], b[0:3 + NB, :], ACT.Copy).then_inc(emptied["A"], 1)
                    act.wait_ge(emptied["A"], upto["A"][place[f"cb{QT // 4 - 1}"] + 1])
                    act.dma_start(conv_prompt_out[0, 0], tail_rows[0:3, :]).then_inc(S("conv_rows_out"), 16)
                    act.dma_start(conv_sample_out[0, :, KC - 2, :], tail_rows[3:3 + NB, :]).then_inc(S("conv_rows_out"), 16)

                    act.wait_ge(S("tail_ready"), 1)
                    for j in range(2 * H):
                        b = full(act, f"l2_{j}")
                        act.activation(rnb[:, j, :], b[:, 0:TOK], ACT.Ln, bias=epsc[:, 0:1]).then_inc(emptied["A"], 1)
                    act.wait_ge(emptied["A"], upto["A"][place[f"l2_{2 * H - 1}"] + 1])
                    for j in range(0, 2 * H, H):
                        act.activation(rnb[:, j:j + H, :], rnb[:, j:j + H, :], ACT.Exp, scale=-0.5).then_inc(S("qk_rn"), 1)
            for h in range(H):
                act.wait_ge(S("dec_raw"), h + 1)
                act.activation(eg[:, h, :], eg[:, h, :], ACT.Exp)
                act.activation(decM[:, :, h, :], decM[:, :, h, :], ACT.Exp).then_inc(S("dec_exp"), 1)
            act.wait_ge(S("kd_raw"), 1)
            act.activation(kd[:, :, :], kd[:, :, :], ACT.Exp).then_inc(S("kd_exp"), 1)
            act.activation(kb1[:, :], colv[:, 1, 32:32 + H], ACT.Exp).then_inc(S("kd_exp"), 1)

            act.wait_ge(S("decays_used"), 1)
            for q in range(NQ):
                b = full(act, f"xt{q}")
                act.activation(X[:, 4 * q:4 * q + 4, :], b[:, :].rearrange("p (a c) -> p a c", a=4), ACT.Copy).then_inc(emptied["A"], 1)
            for L in range(1, LEVELS):
                for q in range(NQ):
                    b = full(act, f"P{L}_{q}")
                    act.activation(PX[:, 4 * q:4 * q + 4, :], b[:, :].rearrange("p (a c) -> p a c", a=4), ACT.Copy).then_inc(emptied["A"], 1)

            def four(dst, name):
                b = full(act, name)
                return act.activation(dst, b[:, :].rearrange("p (a c) -> p a c", a=4), ACT.Copy).then_inc(emptied["A"], 1)

            act.wait_ge(bank_full, place[f"T{LEVELS - 1}_{NQ - 1}"] + 1)
            S_in = A["state_gdn_S"][0].rearrange("b h k v -> k (b h) v")
            cut = 3 * NM
            act.dma_start(Ss[:, 0:cut, :], S_in[:, 0:cut, :]).then_inc(S("first_states_in"), 16)
            act.wait_ge(S("conv_rows_out"), 32)
            for q in range(2):
                four(vnew[:, 4 * q:4 * q + 4, :], f"u0_{q}")
            for q in range(2):
                four(hT[:, 4 * q:4 * q + 4, 0:P], f"o0_{q}")
            act.wait_ge(emptied["A"], upto["A"][place["o0_1"] + 1])
            act.sem_inc(S("oT_ready"), 1)
            for q in range(2):
                four(wT[:, 4 * q:4 * q + 4, :], f"w_{q}")
            for q in range(2):
                four(vnew1[:, 4 * q:4 * q + 4, :], f"u1_{q}")
            act.dma_start(Ss[:, cut:, :], S_in[:, cut:, :]).then_inc(S("last_states_in"), 16)
            for q in range(2):
                four(hT[:, 4 * q:4 * q + 4, P:SEQ], f"o1_{q}")
            act.wait_ge(emptied["A"], upto["A"][place["o1_1"] + 1])
            act.sem_inc(S("oT_ready"), 3)

            act.wait_ge(S("S2_ready"), 1)
            act.dma_start(S_prompt_out[0, 0].rearrange("h k v -> k h v"), S2).then_inc(S("state_out"), 16)
            for u in range(NB * H // 16):
                four(R_rows[:, 4 * u:4 * u + 4, :], f"R{u}")
            b = full(act, "rw")
            act.activation(k_rows[0:NB * H, :], b[0:NB * H, 0:P], ACT.Copy).then_inc(S("rows_ready"), 1)
            act.activation(v_rows[0:NB * H, :], b[0:NB * H, P:2 * P], ACT.Copy).then_inc(emptied["A"], 1)
            act.wait_ge(emptied["A"], upto["A"][place["rw"] + 1])
            act.sem_inc(S("rows_ready"), 1)
            for h in range(H):
                b = full(act, f"on{h}")
                act.activation(sqo[:, h, :], b[:, 0:TOK], ACT.Ln, bias=epsc[:, 0:1], scale=1.0 / P).then_inc(emptied["A"], 1)
            act.wait_ge(emptied["A"], upto["A"][place[f"on{H - 1}"] + 1])
            for i in range(2):
                act.activation(sqo[:, i * H // 2:(i + 1) * H // 2, :], sqo[:, i * H // 2:(i + 1) * H // 2, :], ACT.Exp, scale=-0.5) \
                    .then_inc(S("o_rn"), H // 2)
            def states_out(i):
                half = NB * H // 2
                act.wait_ge(S("states_new"), OU // 2 * (i + 1))
                act.dma_start(S_sample_out[0].rearrange("b h k v -> k (b h) v")[:, i * half:(i + 1) * half, :],
                              Ss[:, i * half:(i + 1) * half, :]).then_inc(S("state_out"), 16)

            states_out(0)
            states_out(1)

            def moe(l):
                norm(2 * l + 1, S("x_mixed"), lambda t: l * DT + t + 1, squares=sqx if l == 0 else sqh)
                shift_tiles(2 * l + 1)
                act.wait_ge(S(f"gexp_raw{l}"), 1)
                act.activation(r4[:, :, :], r4[:, :, :], ACT.Exp).then_inc(S(f"gexp{l}"), 1)
                act.wait_ge(S(f"e2_raw{l}"), 1)
                act.activation(r1[:, 2, :], r1[:, 2, :], ACT.Exp).then_inc(S(f"e2_exp{l}"), 1)
                act.wait_ge(S("state_out"), 48)
                act.wait_ge(S("pads_zeroed"), 1)
                for i in range(6):
                    n, j = i // 2, i % 2
                    rows = P if n < 2 else NB
                    b = full(act, f"ht{l}_{i}")
                    act.activation(htok[0:rows, n, j * 512:(j + 1) * 512], b[0:rows, :], ACT.Copy).then_inc(emptied["A"], 1)
                act.wait_ge(S(f"passes_known{l}"), 1)
                n_pass = act.value_load(passes[0:1, l:l + 1], min_val=1, max_val=MAXPASS)
                act.sem_inc(S(f"y_emptied{l}"), 1)
                with act.Fori(0, n_pass) as p_:
                    for g_ in range(NG):
                        act.wait_ge(S(f"PT_full{l}"), p_ * NG + g_ + 1)
                        act.activation(PT[:, 1 + g_, :], banks[g_][:, 0:TOK], ACT.Copy).then_inc(S(f"PT_ready{l}"), 1)
                    for k in range(DT):
                        act.wait_ge(S(f"gathered{l}"), p_ * DT + k + 1)
                        act.activation(hg[:, k, :], banks[(5 + k) % 8][:, :], ACT.Copy).then_inc(S(f"hg_ready{l}"), 1)

                    def output_rows(gi):
                        act.wait_ge(S(f"dn_done{l}"), gi * PG + PG)
                        act.activation(ycur[:, 0:512], banks[4][:, :], ACT.Copy)
                        act.activation(ycur[:, 512:1024], banks[5][:, :], ACT.Copy).then_inc(S(f"y_emptied{l}"), 1)

                    with act.Fori(0, NG) as g_:
                        gi = p_ * NG + g_

                        def experts(c_):
                            for u in range(PG // c_ + 1):
                                if u < PG // c_:
                                    act.wait_ge(S(f"gu_full{l}"), gi * PG + (u + 1) * c_ + PG)
                                    if u >= 2:
                                        act.wait_ge(S(f"hid_done{l}"), gi * PG + (u - 1) * c_ + PG)
                                    act.activation(sg[:, u % 2, :], banks[u % 2][:, 0:FF], ACT.Silu) \
                                        .then_inc(S(f"sg_ready{l}"), c_)
                                if u >= 1:
                                    v = u - 1
                                    act.wait_ge(S(f"tr_full{l}"), gi * PG + (v + 1) * c_)
                                    if v >= 2:
                                        act.wait_ge(S(f"dn_done{l}"), gi * PG + (v - 1) * c_ + PG)
                                    act.activation(hidT[:, v % 2, :, :],
                                                   banks[2 + v % 2][:, 0:2 * P].rearrange("p (a c) -> p a c", a=2),
                                                   ACT.Copy).then_inc(S(f"hidT_ready{l}"), c_)

                        with act.If(g_ > 0):
                            output_rows(gi)
                        is_small = act.value_load(small_i[0:1, l, bass.ds(gi, 1)], min_val=0, max_val=1)
                        with act.If(is_small > 0):
                            experts(2)
                        with act.Else():
                            experts(1)
                    output_rows((p_ + 1) * NG)
                return n_pass

            np0 = moe(0)
            norm(2, S("x_moe0"), lambda t: np0 * (NG * DT) + DT + t + 1)
            shift_tiles(2)
            for i in range(2 * DT):
                b = full(act, f"sg{i}")
                dst = gateb[:, i, :] if i < DT else gatec[:, i - DT, :]
                act.activation(dst, b[:, 0:TOK], ACT.Copy).then_inc(emptied["A"], 1)
            for i in range(DT // 4):
                b = full(act, f"st{i}")
                act.activation(tail2_rows[0:2 + NB, i * 512:(i + 1) * 512], b[0:2 + NB, :], ACT.Copy).then_inc(emptied["A"], 1)
            act.wait_ge(emptied["A"], upto["A"][place[f"st{DT // 4 - 1}"] + 1])
            act.dma_start(sconv_prompt_out[0, 0], tail2_rows[0:2, :]).then_inc(S("sconv_rows_out"), 16)
            act.dma_start(sconv_sample_out[0, :, KS - 2, :], tail2_rows[2:2 + NB, :]).then_inc(S("sconv_rows_out"), 16)
            act.wait_ge(S("sconv_rows_out"), 32)
            np1 = moe(1)
            norm(4, S("x_moe1"), lambda t: np1 * (NG * DT) + DT + t + 1)
            for i in range(6):
                n, j = i // 2, i % 2
                b = full(act, f"y{i}")
                dst = y_rows[:, n, j * 512:(j + 1) * 512] if n < 2 else ys_rows[0:NB, j * 512:(j + 1) * 512]
                act.activation(dst, b[0:(P if n < 2 else NB), :], ACT.Copy).then_inc(S("y_ready"), 1)

        @block.tensor
        def _(pe):
            pe.wait_ge(S("consts"), 1)
            pe.wait_ge(S("rows_loaded"), 13 * 16)
            b = claim(pe, "c")
            for t in range(DT):
                last = pe.transpose(b[:, t * MODS:(t + 1) * MODS], c_rows[0:MODS, t * P:(t + 1) * P], ident[0:MODS, 0:MODS])
            last.then_inc(bank_full, 1)
            b = claim(pe, "xs")
            for t in range(DT):
                last = pe.transpose(b[:, t * NB:(t + 1) * NB], xs_rows[0:NB, t * P:(t + 1) * P], ident[0:NB, 0:NB])
            last.then_inc(bank_full, 1)
            for i in range(4):
                n, j = i // 2, i % 2
                b = claim(pe, f"x{i}")
                for t in range(4):
                    last = pe.transpose(b[:, t * P:(t + 1) * P], x_rows[:, n, (4 * j + t) * P:(4 * j + t + 1) * P], ident[:, :])
                last.then_inc(bank_full, 1)
            b = claim(pe, "vec")
            pe.transpose(b[:, 0:96], vec_rows[0:96, 0, :], ident[0:96, 0:96])
            pe.transpose(b[:, P:P + 96], vec_rows[0:96, 1, :], ident[0:96, 0:96])
            pe.transpose(b[:, 2 * P:2 * P + 65], vec_rows[0:65, 2, :], ident[0:65, 0:65]).then_inc(bank_full, 1)
            R = NB * (KC - 1)
            for name, lo, hi in (("cs0", 0, 16), ("cs1", 16, QT)):
                b = claim(pe, name)
                for t in range(lo, hi):
                    last = pe.transpose(b[:, (t - lo) * R:(t - lo + 1) * R], cs_rows[0:R, t * P:(t + 1) * P], ident[0:R, 0:R])
                last.then_inc(bank_full, 1)
            b = claim(pe, "sc")
            R = NB * (KS - 1)
            for t in range(DT):
                last = pe.transpose(b[:, t * R:(t + 1) * R], sc_rows[0:R, t * P:(t + 1) * P], ident[0:R, 0:R])
            last.then_inc(bank_full, 1)

            def ada(pieces):
                def turn(l, i):
                    b = claim(pe, f"adaT{l}_{i}")
                    pe.wait_ge(emptied["A"], upto["A"][place[f"ada{l}_{i}"] + 1])
                    for c_ in range(4):
                        last = pe.transpose(b[:, c_ * P:(c_ + 1) * P], ada_row[:, c_ * P:(c_ + 1) * P], ident[:, :])
                    last.then_inc(bank_full, 1)

                for n, (l, i) in enumerate(pieces):
                    w = slot_of(pe, f"ada{l}", i)
                    b = claim(pe, f"ada{l}_{i}")
                    for k in range(DT // 4):
                        for j in range(4):
                            last = pe.matmul(b[32 * j:32 * j + 32, :], cT[:, 4 * k + j, :], w[:, 4 * k + j, :],
                                             start=(k == 0), stop=(k == DT // 4 - 1), skip_group_check=True)
                    last.then_inc(bank_full, 1)
                    if n:
                        turn(*pieces[n - 1])
                turn(*pieces[-1])

            def norm(k, squares=sqh):
                b = claim(pe, f"ss{k}")
                for t in range(DT):
                    pe.wait_ge(S("sq_x"), k * DT + t + 1)
                    last = pe.matmul(b[:, 0:TOK], ones[:, :], squares[t], start=(t == 0), stop=(t == DT - 1))
                last.then_inc(bank_full, 1)

            def h_tile(k, t):
                if t == 0:
                    pe.wait_ge(S("h_samples"), k + 1)
                pe.wait_ge(S("h_tiles"), k * DT + t + 1)

            def conv_rows_and_norms():
                pe.wait_ge(S("tail_ready"), 1)
                for i in range(QT // 4):
                    b = claim(pe, f"cb{i}")
                    for t in range(4):
                        last = pe.transpose(b[0:3 + NB, t * P:(t + 1) * P], tail[:, 4 * i + t, :], ident[:, :])
                    last.then_inc(bank_full, 1)
                for i in range(2 * H):
                    b = claim(pe, f"l2_{i}")
                    pe.wait_ge(S("sq_odd" if i % 2 else "sq_even"), i // 2 + 1)
                    pe.matmul(b[:, 0:TOK], ones[:, :], sqb[:, i % 4, :], start=True, stop=True).then_inc(bank_full, 1)

            def project(kind, names, x, ready=None, between=None):
                for i, name in enumerate(names):
                    c_, j = i // 4, i % 4
                    if j == 0:
                        w = slot_of(pe, kind, c_)
                    b = claim(pe, name)
                    for k in range(DT):
                        if i == 0 and ready:
                            ready(k)
                        last = pe.matmul(b[:, 0:TOK], w[:, k, j * P:(j + 1) * P], x[:, k, :],
                                         start=(k == 0), stop=(k == DT - 1))
                    last.then_inc(bank_full, 1)
                    if between:
                        between(i)
                    if kind == "win" and j == 3:
                        ada(ada_after[c_])
                        if c_ == QT // 4:
                            conv_rows_and_norms()

            norm(0)
            pe.wait_ge(emptied["A"], upto["A"][place["c"] + 1])
            ada(ada_first)
            pe.wait_ge(S("small_weights"), 12 * 16)
            b = claim(pe, "ba")
            for k in range(DT):
                h_tile(0, k)
                last = pe.matmul(b[0:40, 0:TOK], w_ba[:, k, :], hT[:, k, :], start=(k == 0), stop=(k == DT - 1))
            last.then_inc(bank_full, 1)
            project("win", [f"in{i}" for i in range(QT + H)], hT)
            b = claim(pe, "smx")
            pe.wait_ge(S("smT_ready"), 1)
            for n in range(NCH):
                last = pe.transpose(b[:, n * 40:(n + 1) * 40], smT[0:40, n * P:(n + 1) * P], ident[0:40, 0:40])
            last.then_inc(bank_full, 1)
            for h in range(H):
                b = claim(pe, f"gr{h}")
                pe.matmul(b[:, 0:TOK], ident[:, 32 + h:33 + h].to_broadcast([P, P]), smT[:, :], start=True, stop=True) \
                    .then_inc(bank_full, 1)
            for h in range(H):
                b = claim(pe, f"br{h}")
                pe.matmul(b[:, 0:TOK], ident[:, h:h + 1].to_broadcast([P, P]), smT[:, :], start=True, stop=True) \
                    .then_inc(bank_full, 1)
            pe.wait_ge(S("qk_normed"), 2 * H)
            for name, other in (("kk", H), ("qk", 0)):
                for q in range(NQ):
                    b = claim(pe, f"{name}{q}")
                    for a in range(4):
                        n, h = divmod(4 * q + a, H)
                        last = pe.matmul(b[:, a * P:(a + 1) * P], cv[:, H + h, n * P:(n + 1) * P],
                                         cv[:, other + h, n * P:(n + 1) * P], start=True, stop=True)
                    last.then_inc(bank_full, 1)
            for q in range(NQ):
                b = claim(pe, f"xt{q}")
                pe.wait_ge(S("XT_ready"), q + 1)
                for a in range(4):
                    last = pe.transpose(b[:, a * P:(a + 1) * P], XT[:, 4 * q + a, :], ident[:, :])
                last.then_inc(bank_full, 1)
            for name, base in (("vt", 2 * H), ("kt", H)):
                for q in range(NQ):
                    b = claim(pe, f"{name}{q}")
                    for a in range(4):
                        n, h = divmod(4 * q + a, H)
                        last = pe.transpose(b[:, a * P:(a + 1) * P], cv[:, base + h, n * P:(n + 1) * P], ident[:, :])
                    last.then_inc(bank_full, 1)
            for L in range(1, LEVELS):
                for q in range(NQ):
                    b = claim(pe, f"P{L}_{q}")
                    pe.wait_ge(S("BT_ready"), L * NQ + q + 1)
                    if L == 1:
                        pe.wait_ge(emptied["A"], upto["A"][place[f"xt{q}"] + 1])
                    else:
                        pe.wait_ge(emptied["D"], upto["D"][place[f"Q{L - 1}_{q}"] + 1])
                    for a in range(4):
                        last = pe.matmul(b[:, a * P:(a + 1) * P], BT[:, 4 * q + a, :], X[:, 4 * q + a, :], start=True, stop=True)
                    last.then_inc(bank_full, 1)
                for q in range(NQ):
                    b = claim(pe, f"T{L}_{q}")
                    pe.wait_ge(emptied["A"], upto["A"][place[f"P{L}_{q}"] + 1])
                    for a in range(4):
                        last = pe.matmul(b[:, a * P:(a + 1) * P], PX[:, 4 * q + a, :], XT[:, 4 * q + a, :], start=True, stop=True)
                    last.then_inc(bank_full, 1)
                    if L < LEVELS - 1:
                        b = claim(pe, f"Q{L}_{q}")
                        for a in range(4):
                            last = pe.matmul(b[:, a * P:(a + 1) * P], XT[:, 4 * q + a, :], PX[:, 4 * q + a, :], start=True, stop=True)
                        last.then_inc(bank_full, 1)

            def four(name, terms):
                b = claim(pe, name)
                q = int(name[-1])
                for a in range(4):
                    h = 4 * q + a
                    ts = terms(h)
                    for i, (l_, r_) in enumerate(ts):
                        last = pe.matmul(b[:, a * P:(a + 1) * P], l_, r_, start=(i == 0), stop=(i == len(ts) - 1))
                last.then_inc(bank_full, 1)

            def got(e_, name):
                pe.wait_ge(emptied[e_], upto[e_][place[name] + 1])

            got("D", f"T{LEVELS - 1}_{NQ - 1}")
            for q in range(2):
                four(f"u0_{q}", lambda h: [(XT[:, h, :], vb[:, h, :])])
            for q in range(2):
                got("A", f"u0_{q}")
                four(f"s1_{q}", lambda h: [(kdec[:, h, :], vnew[:, h, :])])
            for q in range(2):
                four(f"o0_{q}", lambda h: [(vnew[:, h, :], intraT[:, h, :])])
            for q in range(2):
                four(f"w_{q}", lambda h: [(kbg[:, h, :], XT[:, H + h, :])])
            for q in range(2):
                got("A", f"w_{q}")
                got("D", f"s1_{q}")
                four(f"u1_{q}", lambda h: [(XT[:, H + h, :], vb[:, H + h, :]), (wT[:, h, :], S1[:, h, :])])
            pe.wait_ge(S("qg_ready"), 1)
            for q in range(2):
                got("A", f"u1_{q}")
                four(f"o1_{q}", lambda h: [(vnew1[:, h, :], intraT[:, H + h, :]), (S1[:, h, :], cv[:, h, P:SEQ])])
            for q in range(2):
                four(f"s2_{q}", lambda h: [(kdec[:, H + h, :], vnew1[:, h, :])])
            pe.wait_ge(S("pairs_ready"), 1)
            for u in range(NB * H // 16):
                b = claim(pe, f"R{u}")
                if u == 0:
                    pe.wait_ge(S("first_states_in"), 16)
                if u == 3 * NM // 16:
                    pe.wait_ge(S("last_states_in"), 16)
                for i in range(4):
                    for j in range(4):
                        m = 16 * u + 4 * i + j
                        last = pe.matmul(b[32 * j:32 * j + 32, i * P:(i + 1) * P], qk_pairs[:, 2 * m:2 * m + 32], Ss[:, m, :],
                                         start=True, stop=True, skip_group_check=True)
                last.then_inc(bank_full, 1)
            for u in range(NB * H // 16):
                b = claim(pe, f"RT{u}")
                got("A", f"R{u}")
                for i in range(4):
                    last = pe.transpose(b[:, i * P:(i + 1) * P], R_rows[:, 4 * u + i, :], ident[:, :])
                last.then_inc(bank_full, 1)
            b = claim(pe, "qkS")
            pe.wait_ge(S("qk_prod"), 1)
            pe.matmul(b[:, 0:NB * H], ones[:, :], qkS.rearrange("p h b -> p (h b)"), start=True, stop=True).then_inc(bank_full, 1)
            b = claim(pe, "rw")
            pe.wait_ge(S("verr_ready"), 1)
            pe.transpose(b[0:NB * H, 0:P], kS.rearrange("p h b -> p (h b)"), ident[:, :])
            pe.transpose(b[0:NB * H, P:2 * P], verr.rearrange("p h b -> p (h b)"), ident[:, :]).then_inc(bank_full, 1)
            pe.wait_ge(S("rows_ready"), 2)
            for h in range(H):
                b = claim(pe, f"on{h}")
                pe.wait_ge(S("osq_ready"), h + 1)
                if h == 0:
                    pe.wait_ge(S("osq_samples"), 1)
                pe.matmul(b[:, 0:TOK], ones[:, :], sqo[:, h, :], start=True, stop=True).then_inc(bank_full, 1)

            def update(t):
                b = claim(pe, f"ou{t}")
                pe.wait_ge(S("spread_ready"), t + 1)
                pe.matmul(b[:, :], k_rows[0:96, :], spread[0:96, t % 2, :, :].rearrange("p r c -> p (r c)"),
                          start=True, stop=True).then_inc(bank_full, 1)

            for t in range(OU // 2):
                update(t)
            pe.wait_ge(S("oT_gated"), H)
            project("wout", [f"wo{i}" for i in range(DT)], hT, between=lambda i: [update(t) for t in ou_after(i)])

            def moe(l):
                norm(2 * l + 1, squares=sqx if l == 0 else sqh)
                b = claim(pe, f"lg{l}")
                for k in range(DT):
                    h_tile(2 * l + 1, k)
                    last = pe.matmul(b[0:NG + NE, 0:TOK], w_route[:, l, k, :], hT[:, k, :], start=(k == 0), stop=(k == DT - 1))
                last.then_inc(bank_full, 1)
                b = claim(pe, f"lgT{l}")
                pe.wait_ge(emptied["D"], upto["D"][place[f"lg{l}"] + 1])
                for n in range(3):
                    last = pe.transpose(b[:, n * (NG + NE):(n + 1) * (NG + NE)], lg[:, n * P:(n + 1) * P],
                                        ident[0:NG + NE, 0:NG + NE])
                last.then_inc(bank_full, 1)
                for i in range(6):
                    n, j = i // 2, i % 2
                    b = claim(pe, f"ht{l}_{i}")
                    rows = P if n < 2 else NB
                    for t in range(4):
                        last = pe.transpose(b[0:rows, t * P:(t + 1) * P], hT[:, 4 * j + t, n * P:n * P + rows], ident[:, :])
                    last.then_inc(bank_full, 1)
                b = claim(pe, f"cum{l}")
                pe.wait_ge(S(f"oh_ready{l}"), 1)
                for n in range(4):
                    for n2 in range(min(n, 2) + 1):
                        rows = P if n2 < 2 else NB
                        diag = n2 == n
                        last = pe.matmul(b[:, n * NG:(n + 1) * NG], (strict if diag else ones)[0:rows, :],
                                         oh[0:rows, n2, :], start=(n2 == 0), stop=(n2 == min(n, 2)))
                last.then_inc(bank_full, 1)
                got("A", f"ht{l}_5")
                got("D", f"cum{l}")
                pe.wait_ge(S(f"passes_known{l}"), 1)
                n_pass = pe.value_load(passes[0:1, l:l + 1], min_val=1, max_val=MAXPASS)
                with pe.Fori(0, n_pass) as p_:
                    pe.wait_ge(S(f"Pm_ready{l}"), p_ + 1)
                    for g_ in range(NG):
                        for n in range(3):
                            rows = P if n < 2 else NB
                            last = pe.transpose(banks[g_][:, n * P:n * P + rows], Pm[0:rows, n, g_, :], ident[0:rows, 0:rows])
                        last.then_inc(S(f"PT_full{l}"), 1)
                    for g_ in range(NG):
                        for n in range(3):
                            rows = P if n < 2 else NB
                            last = pe.matmul(banks[4][:, g_ * PG:(g_ + 1) * PG], Pm[0:rows, n, g_, :], r8[0:rows, n, 0, :],
                                             start=(n == 0), stop=(n == 2))
                    last.then_inc(S(f"cmb_full{l}"), 1)
                    for k in range(DT):
                        bk = (5 + k) % 8
                        if bk < 4:
                            pe.wait_ge(S(f"PT_ready{l}"), p_ * NG + bk + 1)
                        if bk == 4:
                            pe.wait_ge(S(f"cmb_ready{l}"), p_ + 1)
                        for n in range(3):
                            last = pe.matmul(banks[bk][:, :], htok[:, n, k * P:(k + 1) * P],
                                             Pm[:, n, :, :].rearrange("p g c -> p (g c)"), start=(n == 0), stop=(n == 2))
                        last.then_inc(S(f"gathered{l}"), 1)

                    def scatter(gi, at):
                        pe.wait_ge(S(f"y_emptied{l}"), gi + 1)
                        for t in range(DT):
                            pe.wait_ge(S(f"samples_gated{l}"), gi * DT + DT - 1 + t)
                            pe.matmul(banks[6 + t % 2][:, 0:TOK].unsqueeze(1), ycur[:, t * P:(t + 1) * P],
                                      PT[:, bass.ds(at, 1), :], start=True, stop=True).then_inc(S(f"scattered{l}"), 1)

                    with pe.Fori(0, NG) as g_:
                        gi = p_ * NG + g_
                        pe.wait_ge(S(f"hcur_ready{l}"), gi + 1)

                        def filled_by(f):
                            s = moe_slot(l, f)
                            pe.wait_ge(moe_filled[l][s], (gi * 2 + f // NRING + 1) * 32)
                            return slots[s]

                        def experts(c_):
                            M = CAP // c_

                            def turn(u):
                                pe.wait_ge(S(f"hid_done{l}"), gi * PG + (u + 1) * c_ + PG)
                                if u >= 2:
                                    pe.wait_ge(S(f"hidT_ready{l}"), gi * PG + (u - 1) * c_)
                                for f in range(2):
                                    last = pe.transpose(banks[2 + u % 2][:, f * P:(f + 1) * P],
                                                        hid[:, u % 2, f * P:(f + 1) * P], ident[:, :])
                                last.then_inc(S(f"tr_full{l}"), c_)

                            def gate_up(u):
                                w = [filled_by(3 * (j // 2) + j % 2).rearrange("p (t n) -> p t n", n=512)
                                     for j in range(u * c_, (u + 1) * c_)]
                                if u >= 2:
                                    pe.wait_ge(S(f"hid_done{l}"), gi * PG + (u - 1) * c_ + PG)
                                for k in range(DT):
                                    if k == DT // 2 and u == 0:
                                        with pe.If(g_ > 0):
                                            scatter(gi, g_)
                                    if k == DT // 2 and u >= 1:
                                        turn(u - 1)
                                    for x in range(c_):
                                        last = pe.matmul(banks[u % 2][x * M:(x + 1) * M, :], hcur[:, k, x * M:(x + 1) * M],
                                                         w[x][:, k, :], start=(k == 0), stop=(k == DT - 1),
                                                         skip_group_check=True)
                                last.then_inc(S(f"gu_full{l}"), c_)

                            def down(u):
                                w = filled_by(3 * (u * c_ // 2) + 2).rearrange("p (e t n) -> p e t n", e=2, t=2)
                                pe.wait_ge(S(f"hidT_ready{l}"), gi * PG + (u + 1) * c_)
                                for f in range(2):
                                    for d in range(2):
                                        for x in range(c_):
                                            last = pe.matmul(banks[4 + d][x * M:(x + 1) * M, :],
                                                             hidT[:, u % 2, f, x * M:(x + 1) * M],
                                                             w[:, (u * c_ + x) % 2, f, d * 512:(d + 1) * 512],
                                                             start=(u == 0 and f == 0), stop=(u == PG // c_ - 1 and f == 1),
                                                             skip_group_check=True)
                                last.then_inc(S(f"dn_done{l}"), c_)

                            for u in range(PG // c_):
                                gate_up(u)
                                if u == 1:
                                    pe.wait_ge(S(f"y_emptied{l}"), gi + 1)
                                if u >= 1:
                                    down(u - 1)
                            turn(PG // c_ - 1)
                            down(PG // c_ - 1)

                        is_small = pe.value_load(small_i[0:1, l, bass.ds(gi, 1)], min_val=0, max_val=1)
                        with pe.If(is_small > 0):
                            experts(2)
                        with pe.Else():
                            experts(1)
                    scatter((p_ + 1) * NG, NG)
                return n_pass

            np0 = moe(0)
            if place["ss2"] % 8 >= 6:
                pe.wait_ge(S("samples_gated0"), np0 * (NG * DT) + 2 * DT)
            norm(2)
            project("scin", [f"sg{i}" for i in range(3 * DT)], hT, ready=lambda k: h_tile(2, k))
            pe.wait_ge(S("tail2_ready"), 1)
            for i in range(DT // 4):
                b = claim(pe, f"st{i}")
                for t in range(4):
                    last = pe.transpose(b[0:2 + NB, t * P:(t + 1) * P], tail2[:, 4 * i + t, :], ident[:, :])
                last.then_inc(bank_full, 1)
            pe.wait_ge(S("sconv_y"), DT)
            project("scout", [f"so{i}" for i in range(DT)], gatec)
            np1 = moe(1)
            if place["ss4"] % 8 >= 6:
                pe.wait_ge(S("samples_gated1"), np1 * (NG * DT) + 2 * DT)
            norm(4)
            for i in range(6):
                n, j = i // 2, i % 2
                b = claim(pe, f"y{i}")
                rows = P if n < 2 else NB
                for t in range(4):
                    if n == 0:
                        pe.wait_ge(S("h_tiles"), 4 * DT + 4 * j + t + 1)
                    last = pe.transpose(b[0:rows, t * P:(t + 1) * P], hT[:, 4 * j + t, n * P:n * P + rows], ident[:, :])
                last.then_inc(bank_full, 1)

        @block.vector
        def _(dve):
            link = Link(dve, "dve_link")
            stt, tt, ts = dve.scalar_tensor_tensor, dve.tensor_tensor, dve.tensor_scalar
            dve.memset(w_ba[:, :, :], 0.0).then_inc(S("w_ba_zeroed"), 1)
            dve.memset(smT[:, :], 0.0)
            link(dve.memset(lg[:, :], 0.0))
            b = full(dve, "xs")
            dve.tensor_copy(xT[:, :, SEQ:TOK], b[:, 0:DT * NB].rearrange("p (t c) -> p t c", c=NB)).then_inc(emptied["D"], 1)
            for i in range(4):
                n, j = i // 2, i % 2
                b = full(dve, f"x{i}")
                dve.tensor_copy(xT[:, 4 * j:4 * j + 4, n * P:(n + 1) * P], b[:, :].rearrange("p (t c) -> p t c", t=4)) \
                    .then_inc(emptied["D"], 1)
            for name, lo, hi in (("cs0", 0, 16), ("cs1", 16, QT)):
                b = full(dve, name)
                for t in range(lo, hi):
                    last = dve.tensor_copy(preS[:, t, :, 0:KC - 1],
                                           b[:, (t - lo) * NB * (KC - 1):(t - lo + 1) * NB * (KC - 1)].rearrange("p (b k) -> p b k", b=NB))
                last.then_inc(emptied["D"], 1)
            b = full(dve, "sc")
            dve.tensor_copy(sc_state[:, :, :], b[:, 0:DT * NB * (KS - 1)].rearrange("p (t r) -> p t r", t=DT)).then_inc(emptied["D"], 1)

            def ada(pieces):
                for l, i in pieces:
                    b = full(dve, f"adaT{l}_{i}")
                    v = b[:, :].rearrange("p (t j r) -> p t r j", t=4, j=4)[:, :, 0:MODS, :]
                    link(dve.tensor_reduce(ada_sum[:, :, :], v, AX.X, ALU.add))
                    bias = vecT[:, 0, l * 6 * DT + 4 * i:l * 6 * DT + 4 * i + 4].unsqueeze(2).broadcast_to([P, 4, MODS])
                    tt(mT[:, l, 4 * i:4 * i + 4, :], ada_sum[:, :, :], bias, ALU.add).then_inc(emptied["D"], 1)
                    dve.wait_ge(emptied["D"], upto["D"][place[f"adaT{l}_{i}"] + 1])

            def mod(l, part):
                t = PART[part] * DT
                return mT[:, l, t:t + DT, :]

            def norm(k, l, which):
                at = (l * DT if which == "m" else 2 * DT + l * DT)
                dve.wait_ge(emptied["A"], upto["A"][place["vec"] + 1])
                gv = vecT[:, 2, at:at + DT].unsqueeze(2).broadcast_to([P, DT, MODS])
                link(stt(gain[:, :, :], mod(l, "sc_" + which), 1.0, gv, ALU.add, ALU.mult))
                dve.wait_ge(S("rstd_ready"), k + 1)
                hS = hT[:, :, SEQ:TOK]
                link(tt(hS, xT[:, :, SEQ:TOK], rstd[:, SEQ:TOK].unsqueeze(1).broadcast_to([P, DT, NB]), ALU.mult))
                link(tt(hS, hS, gain[:, :, 1:MODS], ALU.mult))
                tt(hS, hS, mod(l, "sh_" + which)[:, :, 1:MODS], ALU.add).then_inc(S("h_samples"), 1)
                for t in range(DT):
                    stt(hT[:, t, 0:SEQ], xT[:, t, 0:SEQ], gain[:, t, 0:1], rstd[:, 0:SEQ], ALU.mult, ALU.mult) \
                        .then_inc(S("h_scaled"), 1)

            def residual(l, part, t, b, x_new_free=None):
                gt = mod(l, part)
                stt(xT[:, t, 0:SEQ], b[:, 0:SEQ], gt[:, t, 0:1], xT[:, t, 0:SEQ], ALU.mult, ALU.add)
                if x_new_free:
                    x_new_free()
                return tt(x_new[:, t, :], b[:, SEQ:TOK], gt[:, t, 1:MODS], ALU.mult)

            def residual_samples(t):
                return tt(xT[:, t, SEQ:TOK], xT[:, t, SEQ:TOK], x_new[:, t, :], ALU.add)

            dve.wait_ge(emptied["A"], upto["A"][place["vec"] + 1])
            ada(ada_first)
            norm(0, 0, "m")
            b = full(dve, "ba")
            dve.tensor_copy(ba[:, :], b[0:40, 0:TOK]).then_inc(emptied["D"], 1)
            dve.wait_ge(emptied["D"], upto["D"][place["ba"] + 1])

            link(ts(bc[32:40, :], ba[32:40, :], decay_w[32:40, 1:2], None, ALU.add))
            dve.wait_ge(S("beta_exp"), 2)
            link(ts(bb[32:40, :], bc[32:40, :], -1.0, None, ALU.mult))
            tt(bb[32:40, :], bb[32:40, :], bc[32:40, :], ALU.max).then_inc(S("abs_a"), 1)
            link(ts(bb[0:8, :], bb[0:8, :], 1.0, None, ALU.add))
            link(dve.reciprocal(smT[0:8, :], bb[0:8, :]))
            dve.wait_ge(S("softplus_ln"), 1)
            link(stt(bc[32:40, :], bc[32:40, :], 0.0, bb[32:40, :], ALU.max, ALU.add))
            link(ts(bc[32:40, :], bc[32:40, :], decay_w[32:40, 2:3], -1.0, ALU.mult, ALU.mult))
            for n in range(NCH):
                dve.tensor_tensor_scan(smT[32:40, n * P:(n + 1) * P], ones[32:40, :], bc[32:40, n * P:(n + 1) * P],
                                       0.0, ALU.mult, ALU.add)
            dve.tensor_copy(smT[32:40, SEQ:TOK], bc[32:40, SEQ:TOK]).then_inc(S("smT_ready"), 1)
            dve.wait_ge(S("pre_zeroed"), 1)
            for i in range(QT):
                if i and i % 4 == 0:
                    ada(ada_after[i // 4 - 1])
                dve.wait_ge(S("pre_ready"), i + 1)
                w = lambda k: vecT[:, 1, k * QT + i:k * QT + i + 1]
                link(ts(cv[:, i, 0:SEQ], pre[:, i, 0:SEQ], w(0), None, ALU.mult))
                for k in range(1, KC - 1):
                    link(stt(cv[:, i, 0:SEQ], pre[:, i, k:k + SEQ], w(k), cv[:, i, 0:SEQ], ALU.mult, ALU.add))
                stt(cv[:, i, 0:SEQ], pre[:, i, KC - 1:KC - 1 + SEQ], w(KC - 1), cv[:, i, 0:SEQ], ALU.mult, ALU.add) \
                    .then_inc(S("conv_done"), 1)
            for k in range(KC):
                wk = vecT[:, 1, k * QT:(k + 1) * QT].unsqueeze(2).broadcast_to([P, QT, NB])
                last = tt(convtmp[:, :, :, k], preS[:, :, :, k], wk, ALU.mult)
            link(last)
            link(tt(convtmp[:, :, :, 0], convtmp[:, :, :, 0], convtmp[:, :, :, 1], ALU.add))
            link(tt(convtmp[:, :, :, 0], convtmp[:, :, :, 0], convtmp[:, :, :, 2], ALU.add))
            tt(cv[:, :, SEQ:TOK], convtmp[:, :, :, 0], convtmp[:, :, :, 3], ALU.add).then_inc(S("conv_done"), 1)
            for j in range(QT // 4 - 1, QT // 4 + 1):
                ada(ada_after[j])
            dve.wait_ge(S("cv_ready"), QT + 1)
            for i in range(1, 2 * H, 2):
                if i >= 4:
                    dve.wait_ge(bank_full, place[f"l2_{i - 4}"] + 1)
                tt(sqb[:, i % 4, :], cv[:, i, :], cv[:, i, :], ALU.mult).then_inc(S("sq_odd"), 1)

            for i in range(2 * H):
                dve.wait_ge(S("qk_rn"), i // H + 1)
                stt(cv[:, i, :], cv[:, i, :], float(P) ** -0.5 if i < H else 1.0, rnb[:, i, :], ALU.mult, ALU.mult) \
                    .then_inc(S("qk_normed"), 1)
            dve.wait_ge(S("qk_normed"), 2 * H)
            for j in range(QT // 4 + 1, WIN):
                ada(ada_after[j])
            b = full(dve, "smx")
            dve.tensor_copy(colv[:, :, :], b[:, 0:NCH * 40].rearrange("p (n c) -> p n c", n=NCH)).then_inc(emptied["D"], 1)
            dve.wait_ge(emptied["D"], upto["D"][place["smx"] + 1])
            dve.wait_ge(S("conv_done"), QT + 1)
            dve.wait_ge(S("tail_ready"), 1)
            for h in range(H):
                b = full(dve, f"gr{h}")
                for n in range(NCH):
                    ts(decM[:, n, h, :], b[:, n * P:(n + 1) * P], colv[:, n, 32 + h:33 + h], 0.0, ALU.subtract, ALU.min)
                dve.tensor_copy(eg[:, h, :], b[:, P:TOK])
                dve.tensor_copy(lastg[:, h, :], b[:, P - 1:SEQ:P]).then_inc(emptied["D"], 1)
                dve.wait_ge(emptied["D"], upto["D"][place[f"gr{h}"] + 1])
                dve.sem_inc(S("dec_raw"), 1)
            for h in range(H):
                b = full(dve, f"br{h}")
                dve.wait_ge(S("dec_masked"), h + 1)
                tt(decB[:, :, h, :], decM[:, :, h, :], b[:, 0:SEQ].rearrange("p (n c) -> p n c", n=NCH), ALU.mult)
                dve.tensor_copy(betaS[:, h, :], b[:, SEQ:TOK]).then_inc(emptied["D"], 1)
            tt(kd[:, :, :], lastg[:, :, :].rearrange("p h n -> p n h"), colv[:, :, 32:32 + H], ALU.subtract).then_inc(S("kd_raw"), 1)
            flat = lambda v: v.rearrange("p n h c -> p (n h) c")
            b4 = lambda b_: b_[:, :].rearrange("p (a c) -> p a c", a=4)
            dve.wait_ge(emptied["D"], upto["D"][place[f"br{H - 1}"] + 1])
            for q in range(NQ):
                b = full(dve, f"kk{q}")
                tt(AT[:, 4 * q:4 * q + 4, :], b4(b), flat(decB)[:, 4 * q:4 * q + 4, :], ALU.mult).then_inc(emptied["D"], 1)
                dve.wait_ge(emptied["D"], upto["D"][place[f"kk{q}"] + 1])
                dve.sem_inc(S("AT_raw"), 1)
            for q in range(NQ):
                b = full(dve, f"qk{q}")
                tt(intraT[:, 4 * q:4 * q + 4, :], b4(b), flat(decM)[:, 4 * q:4 * q + 4, :], ALU.mult).then_inc(emptied["D"], 1)
            dve.wait_ge(emptied["D"], upto["D"][place[f"qk{NQ - 1}"] + 1])
            dve.sem_inc(S("decays_used"), 1)
            for q in range(NQ):
                dve.wait_ge(S("BT_ready"), q + 1)
                tt(XT[:, 4 * q:4 * q + 4, :], ident[:, :].unsqueeze(1).broadcast_to([P, 4, P]), BT[:, 4 * q:4 * q + 4, :], ALU.subtract) \
                    .then_inc(S("XT_ready"), 1)
            beta_col = lambda q: colv[:, (4 * q) // H, (4 * q) % H:(4 * q) % H + 4].unsqueeze(2).broadcast_to([P, 4, P])
            for q in range(NQ):
                b = full(dve, f"vt{q}")
                tt(vb[:, 4 * q:4 * q + 4, :], b4(b), beta_col(q), ALU.mult).then_inc(emptied["D"], 1)
            dve.wait_ge(S("kd_exp"), 2)
            link(stt(kb1[:, :], kb1[:, :], -1.0, colv[:, 1, 0:H], ALU.mult, ALU.mult))
            kdf = kd[:, :, :].rearrange("p n h -> p (n h)")
            dve.wait_ge(S("conv_rows_out"), 32)
            for q in range(NQ):
                b = full(dve, f"kt{q}")
                last = tt(kdec[:, 4 * q:4 * q + 4, :], b4(b), kdf[:, 4 * q:4 * q + 4].unsqueeze(2).broadcast_to([P, 4, P]), ALU.mult)
                if 4 * q >= H:
                    last = tt(kbg[:, 4 * q - H:4 * q - H + 4, :], b4(b),
                              kb1[:, 4 * q - H:4 * q - H + 4].unsqueeze(2).broadcast_to([P, 4, P]), ALU.mult)
                last.then_inc(emptied["D"], 1)
            dve.wait_ge(S("XT_ready"), NQ)
            for L in range(1, LEVELS):
                for q in range(NQ):
                    b = full(dve, f"T{L}_{q}")
                    if L < LEVELS - 1:
                        b2 = full(dve, f"Q{L}_{q}")
                    if L > 1:
                        dve.wait_ge(emptied["D"], upto["D"][place[f"T{L}_{q}"]])
                    v = XT[:, 4 * q:4 * q + 4, :]
                    tt(v, v, b4(b), ALU.subtract).then_inc(emptied["D"], 1)
                    if L < LEVELS - 1:
                        v = X[:, 4 * q:4 * q + 4, :]
                        tt(v, v, b4(b2), ALU.subtract).then_inc(emptied["D"], 1)
            for q in range(2):
                b = full(dve, f"s1_{q}")
                dve.tensor_copy(S1[:, 4 * q:4 * q + 4, :], b4(b)).then_inc(emptied["D"], 1)
            dve.wait_ge(emptied["D"], upto["D"][place["s1_1"] + 1])
            tt(cv[:, 0:H, P:SEQ], cv[:, 0:H, P:SEQ], eg[:, :, 0:P], ALU.mult).then_inc(S("qg_ready"), 1)
            pairs = qk_pairs[:, 0:2 * NB * H].rearrange("p (b h c) -> p b h c", b=NB, h=H)
            for c_ in range(2):
                dve.tensor_copy(pairs[:, :, :, c_], cv[:, c_ * H:(c_ + 1) * H, SEQ:TOK].rearrange("p h b -> p b h"))
            dve.memset(qk_pairs[:, 2 * NB * H:], 0.0).then_inc(S("pairs_ready"), 1)
            for q in range(2):
                b = full(dve, f"s2_{q}")
                for a in range(4):
                    h = 4 * q + a
                    last = stt(S2[:, h, :], S1[:, h, :], eg[:, h, P - 1:P], b[:, a * P:(a + 1) * P], ALU.mult, ALU.add)
                last.then_inc(emptied["D"], 1)
            dve.wait_ge(emptied["D"], upto["D"][place["s2_1"] + 1])
            dve.sem_inc(S("S2_ready"), 1)

            qv = cv[:, 0:H, SEQ:TOK]
            g_o = vecT[:, 2, 40:41]
            kv = cv[:, H:2 * H, SEQ:TOK]
            dve.tensor_copy(kS, kv)
            tt(qkS, qv, kv, ALU.mult).then_inc(S("qk_prod"), 1)
            for h in range(H):
                dve.wait_ge(S("osq_ready"), h + 1)
                stt(hT[:, h, 0:SEQ], hT[:, h, 0:SEQ], g_o, zs[:, h, 0:SEQ], ALU.mult, ALU.mult)
            egs = eg[:, :, P:P + NB]
            Rv = Rs.rearrange("p (h b) c -> p h b c", h=H)
            for u in range(NB * H // 16):
                b = full(dve, f"RT{u}")
                bv = b[:, :].rearrange("p (s h r) -> p h s r", s=2, h=H)
                for c_ in range(2):
                    last = tt(Rv[:, :, 2 * u:2 * u + 2, c_], bv[:, :, :, c_], egs[:, :, 2 * u:2 * u + 2], ALU.mult)
                last.then_inc(emptied["D"], 1)
            dve.wait_ge(emptied["D"], upto["D"][place[f"RT{NB * H // 16 - 1}"] + 1])
            link(tt(verr, cv[:, 2 * H:3 * H, SEQ:TOK], Rv[:, :, :, 1], ALU.subtract))
            tt(verr, verr, betaS[:, :, :], ALU.mult).then_inc(S("verr_ready"), 1)
            dve.wait_ge(S("verr_ready"), 1)
            b = full(dve, "qkS")
            tt(qkS, b[:, 0:NB * H].rearrange("p (h b) -> p h b", h=H), verr, ALU.mult).then_inc(emptied["D"], 1)
            dve.wait_ge(emptied["D"], upto["D"][place["qkS"] + 1])
            hS = hT[:, :, SEQ:TOK]
            link(tt(hS, Rv[:, :, :, 0], qkS, ALU.add))
            tt(sqo[:, :, SEQ:TOK], hS, hS, ALU.mult).then_inc(S("osq_samples"), 1)
            dve.wait_ge(S("osq_samples"), 1)
            stt(hS, hS, g_o, zs[:, :, SEQ:TOK], ALU.mult, ALU.mult).then_inc(S("out_scaled"), 1)
            SsV = Ss.rearrange("p (b h) c -> p b h c", h=H)

            def update(t):
                h, b0, _ = ou_matrices(t)
                b = full(dve, f"ou{t}")
                for a in range(4):
                    v = SsV[:, b0 + a, h, :]
                    last = stt(v, v, eg[:, h, P + b0 + a:P + b0 + a + 1], b[:, a * P:(a + 1) * P], ALU.mult, ALU.add)
                last.then_inc(emptied["D"], 1)
                dve.wait_ge(emptied["D"], upto["D"][place[f"ou{t}"] + 1])
                dve.sem_inc(S("states_new"), 1)

            for t in range(OU // 2 - 2):
                update(t)
            dve.wait_ge(S("out_scaled"), 1)
            for h in range(H):
                dve.wait_ge(S("o_rn"), h + 1)
                tt(hT[:, h, :], hT[:, h, :], sqo[:, h, :], ALU.mult).then_inc(S("oT_gated"), 1)
            for t in range(OU // 2 - 2, OU // 2):
                update(t)

            def mixed(l, names, between=None):
                for t in range(DT):
                    b = full(dve, f"{names}{t}")
                    residual(l, "gt_m", t, b).then_inc(emptied["D"], 1)
                    if t:
                        dve.wait_ge(emptied["D"], upto["D"][place[f"{names}{t - 1}"] + 1])
                        residual_samples(t - 1).then_inc(S("x_mixed"), 1)
                    if between and t < DT - 1:
                        between(t)
                dve.wait_ge(emptied["D"], upto["D"][place[f"{names}{DT - 1}"] + 1])
                residual_samples(DT - 1).then_inc(S("x_mixed"), 1)
                if between:
                    between(DT - 1)

            def moe(l):
                norm(2 * l + 1, l, "f")
                b = full(dve, f"lg{l}")
                dve.tensor_copy(lg[:, 0:TOK], b[0:NG + NE, 0:TOK]).then_inc(emptied["D"], 1)
                b = full(dve, f"lgT{l}")
                v = b[:, 0:3 * (NG + NE)].rearrange("p (n c) -> p n c", n=3)
                tt(lt[:, :, :], v, b_route[:, l, :].unsqueeze(1).broadcast_to([P, 3, NG + NE]), ALU.add).then_inc(emptied["D"], 1)
                dve.wait_ge(emptied["D"], upto["D"][place[f"lgT{l}"] + 1])
                gl = lt[:, :, 0:NG]
                link(dve.tensor_reduce(r1[:, 0, :], gl, AX.X, ALU.max))
                gmax = r1[:, 0, :].unsqueeze(2).broadcast_to([P, 3, NG])
                tt(r4[:, :, :], gl, gmax, ALU.subtract).then_inc(S(f"gexp_raw{l}"), 1)
                link(tt(oh[:, :, :], gl, gmax, ALU.is_ge))
                link(dve.tensor_copy(r1[:, 1, :], oh[:, :, 0]))
                for q in range(1, NG):
                    link(tt(r1[:, 3, :], r1[:, 1, :], oh[:, :, q], ALU.max))
                    link(tt(oh[:, :, q], oh[:, :, q], r1[:, 1, :], ALU.is_gt))
                    link(dve.tensor_copy(r1[:, 1, :], r1[:, 3, :]))
                dve.sem_inc(S(f"oh_ready{l}"), 1)
                ev = lt[:, :, NG:].rearrange("p n (g e) -> p n g e", g=NG)
                for n in range(3):
                    last = tt(r8[:, n, :, :], ev[:, n, :, :], oh[:, n, :].unsqueeze(2).broadcast_to([P, NG, PG]), ALU.mult)
                link(last)
                link(tt(r8[:, :, 0, :], r8[:, :, 0, :], r8[:, :, 1, :], ALU.add))
                link(tt(r8[:, :, 2, :], r8[:, :, 2, :], r8[:, :, 3, :], ALU.add))
                link(tt(r8[:, :, 0, :], r8[:, :, 0, :], r8[:, :, 2, :], ALU.add))
                for n in range(3):
                    last = dve.max(mx8[:, n, :], r8[:, n, 0, :])
                link(last)
                for n in range(3):
                    last = dve.max_index(ix8[:, n, :], mx8[:, n, :], r8[:, n, 0, :])
                link(last)
                link(dve.tensor_copy(ixf[:, :, :], ix8[:, :, :]))
                tt(r1[:, 2, :], mx8[:, :, 1], mx8[:, :, 0], ALU.subtract).then_inc(S(f"e2_raw{l}"), 1)
                dve.wait_ge(S(f"gexp{l}"), 1)
                link(dve.tensor_reduce(r1[:, 4, :], r4[:, :, :], AX.X, ALU.add))
                dve.wait_ge(S(f"e2_exp{l}"), 1)
                link(ts(r1[:, 5, :], r1[:, 2, :], 1.0, None, ALU.add))
                link(tt(r1[:, 5, :], r1[:, 5, :], r1[:, 4, :], ALU.mult))
                link(dve.reciprocal(r1[:, 5, :], r1[:, 5, :]))
                link(tt(r1[:, 6, :], r1[:, 5, :], r1[:, 2, :], ALU.mult))
                io = slot_iota[:, 0:PG].unsqueeze(1).broadcast_to([P, 3, PG])
                for c_, w_ in ((0, 5), (1, 6)):
                    link(tt(r8[:, :, 2 + c_, :], io, ixf[:, :, c_:c_ + 1].broadcast_to([P, 3, PG]), ALU.is_equal))
                    link(tt(r8[:, :, 2 + c_, :], r8[:, :, 2 + c_, :], r1[:, w_, :].unsqueeze(2).broadcast_to([P, 3, PG]), ALU.mult))
                link(tt(r8[:, :, 0, :], r8[:, :, 2, :], r8[:, :, 3, :], ALU.add))
                b = full(dve, f"cum{l}")
                link(tt(r4[:, :, :], b[:, 0:3 * NG].rearrange("p (n g) -> p n g", n=3), oh[:, :, :], ALU.mult))
                link(dve.tensor_reduce(r1[:, 7, :], r4[:, :, :], AX.X, ALU.add))
                link(dve.tensor_reduce(r1[:, 0, 0:1], b[:, 3 * NG:4 * NG], AX.X, ALU.max))
                link(ts(r1[:, 0, 1:2], r1[:, 0, 0:1], float(CAP), 1.0, ALU.is_gt, ALU.add))
                link(ts(r1[:, 0, 2:3], r1[:, 0, 0:1], float(2 * CAP), None, ALU.is_gt))
                for p_ in range(MAXPASS):
                    last = ts(small_f[:, p_, :], b[:, 3 * NG:4 * NG], float(CAP * p_ + HALF), None, ALU.is_le)
                link(last)
                dve.tensor_copy(small_i[:, l, :], small_f[:, :, :].rearrange("p n g -> p (n g)"))
                dve.tensor_copy(count[:, :], b[:, 3 * NG:4 * NG])
                tt(r1[:, 0, 1:2], r1[:, 0, 1:2], r1[:, 0, 2:3], ALU.add).then_inc(emptied["D"], 1)
                dve.wait_ge(emptied["D"], upto["D"][place[f"cum{l}"] + 1])
                dve.tensor_copy(passes[:, l:l + 1], r1[:, 0, 1:2]).then_inc(S(f"passes_known{l}"), 1)
                dve.wait_ge(S(f"passes_known{l}"), 1)
                n_pass = dve.value_load(passes[0:1, l:l + 1], min_val=1, max_val=MAXPASS)
                dve.wait_ge(S("state_out"), 48)
                dve.wait_ge(S("pads_zeroed"), 1)
                dve.sem_inc(S(f"hid_done{l}"), PG)
                dve.sem_inc(S(f"scattered{l}"), DT)
                dve.sem_inc(S(f"x_moe{l}"), 2 * DT)
                dve.sem_inc(S(f"samples_gated{l}"), 2 * DT)
                with dve.Fori(0, n_pass) as p_:
                    ts(small_f[:, 0, :], count[:, :], float(HALF), -1.0, ALU.is_le, ALU.mult).then_inc(S(f"small_sign{l}"), 1)
                    dve.wait_ge(S(f"small_sign{l}"), p_ + 1)
                    for g_ in range(NG):
                        last = stt(small_iota[:, g_, :], upper[:, :], small_f[:, 0, g_:g_ + 1], slot_iota[:, :], ALU.mult, ALU.add)
                    last.then_inc(S(f"slots_numbered{l}"), 1)
                    dve.wait_ge(S(f"slots_numbered{l}"), p_ + 1)
                    for n in range(3):
                        rows = P if n < 2 else NB
                        for g_ in range(NG):
                            last = ts(Pm[0:rows, n, g_, :], small_iota[0:rows, g_, :], r1[0:rows, 7, n:n + 1],
                                      oh[0:rows, n, g_:g_ + 1], ALU.is_equal, ALU.mult)
                    last.then_inc(S(f"Pm_ready{l}"), 1)
                    dve.wait_ge(S(f"cmb_full{l}"), p_ + 1)
                    dve.tensor_copy(cmb[:, :], banks[4][:, 0:NG * PG]).then_inc(S(f"cmb_ready{l}"), 1)
                    dve.wait_ge(S(f"hg_ready{l}"), (p_ + 1) * DT)
                    ts(count[:, :], count[:, :], float(CAP), None, ALU.subtract)
                    ts(r1[:, 7, :], r1[:, 7, :], float(CAP), None, ALU.subtract)

                    def add_group(gi):
                        for t in range(DT):
                            dve.wait_ge(S(f"scattered{l}"), gi * DT + t + 1)
                            x_new_free = (lambda: dve.wait_ge(S(f"x_moe{l}"), gi * DT + DT)) if t == 0 else None
                            residual(l, "gt_f", t, banks[6 + t % 2], x_new_free).then_inc(S(f"samples_gated{l}"), 1)
                            if t:
                                dve.wait_ge(S(f"samples_gated{l}"), gi * DT + DT + t)
                                residual_samples(t - 1).then_inc(S(f"x_moe{l}"), 1)
                        dve.wait_ge(S(f"samples_gated{l}"), gi * DT + 2 * DT)
                        residual_samples(DT - 1).then_inc(S(f"x_moe{l}"), 1)

                    with dve.Fori(0, NG) as g_:
                        gi = p_ * NG + g_
                        dve.wait_ge(S(f"gu_full{l}"), gi * PG + PG)
                        dve.tensor_copy(hcur, hg[:, :, bass.ds(g_ * CAP, CAP)]).then_inc(S(f"hcur_ready{l}"), 1)
                        with dve.If(g_ > 0):
                            add_group(gi)

                        def experts(c_):
                            for u in range(PG // c_):
                                dve.wait_ge(S(f"sg_ready{l}"), gi * PG + (u + 1) * c_)
                                if u >= 2:
                                    dve.wait_ge(S(f"tr_full{l}"), gi * PG + (u - 1) * c_)
                                stt(hid[:, u % 2, :], banks[u % 2][:, FF:2 * FF], ccur[:, u:u + 1], sg[:, u % 2, :],
                                    ALU.mult, ALU.mult).then_inc(S(f"hid_done{l}"), c_)

                        dve.wait_ge(S(f"hid_done{l}"), gi * PG + PG)
                        is_small = dve.value_load(small_i[0:1, l, bass.ds(gi, 1)], min_val=0, max_val=1)
                        with dve.If(is_small > 0):
                            cp = cmb[:, bass.ds(g_ * PG, PG)].rearrange("p (u x) -> p u x", x=2)
                            dve.tensor_copy(ccur[0:HALF, 0:PG // 2], cp[0:HALF, :, 0])
                            dve.tensor_copy(ccur[HALF:CAP, 0:PG // 2], cp[HALF:CAP, :, 1]).then_inc(S(f"ccur_ready{l}"), 1)
                            dve.wait_ge(S(f"ccur_ready{l}"), gi + 1)
                            experts(2)
                        with dve.Else():
                            dve.tensor_copy(ccur[:, :], cmb[:, bass.ds(g_ * PG, PG)]).then_inc(S(f"ccur_ready{l}"), 1)
                            dve.wait_ge(S(f"ccur_ready{l}"), gi + 1)
                            experts(1)
                    add_group((p_ + 1) * NG)

            mixed(0, "wo", between=lambda i: [update(t) for t in ou_after(i)])
            moe(0)
            norm(2, 1, "m")
            dve.memset(up[:, :, 0:KS - 1], 0.0)
            dve.tensor_copy(upS[:, :, :, 0:KS - 1], sc_state[:, :, :].rearrange("p t (b k) -> p t b k", b=NB))
            for t in range(DT):
                b = full(dve, f"sg{2 * DT + t}")
                tt(up[:, t, KS - 1:], b[:, 0:SEQ], gatec[:, t, 0:SEQ], ALU.mult)
                tt(upS[:, t, :, KS - 1], b[:, SEQ:TOK], gatec[:, t, SEQ:TOK], ALU.mult).then_inc(emptied["D"], 1)
                dve.wait_ge(emptied["D"], upto["D"][place[f"sg{2 * DT + t}"] + 1])
                dve.sem_inc(S("up_ready"), 1)
                w = lambda k: vecT[:, 2, 41 + k * DT + t:42 + k * DT + t]
                y = gatec[:, t, 0:SEQ]
                link(ts(y, up[:, t, 0:SEQ], w(0), None, ALU.mult))
                for k in range(1, KS):
                    link(stt(y, up[:, t, k:k + SEQ], w(k), y, ALU.mult, ALU.add))
                ts(uptmp[:, t, :, 0], upS[:, t, :, 0], w(0), None, ALU.mult).then_inc(S("first_tap"), 1)
                dve.wait_ge(S("first_tap"), t + 1)
                link(stt(uptmp[:, t, :, 1], upS[:, t, :, 1], w(1), uptmp[:, t, :, 0], ALU.mult, ALU.add))
                link(stt(gatec[:, t, SEQ:TOK], upS[:, t, :, 2], w(2), uptmp[:, t, :, 1], ALU.mult, ALU.add))
                tt(gatec[:, t, :], gatec[:, t, :], gateb[:, t, :], ALU.mult).then_inc(S("sconv_y"), 1)
            mixed(1, "so")
            moe(1)
            dve.wait_ge(S("rstd_ready"), 5)
            for t in range(DT):
                stt(hT[:, t, :], xT[:, t, :], vecT[:, 2, 4 * DT + t:4 * DT + t + 1], rstd[:, :], ALU.mult, ALU.mult) \
                    .then_inc(S("h_tiles"), 1)


_INS = ["x_prompt", "x_sample", "state_gdn_S", "state_gdn_conv", "state_sconv", "c_prompt", "c_sample",
        "norm_mix_g", "norm_ffn_g", "norm_final_g", "w_ada", "b_ada", "gdn_w_in", "gdn_conv_w", "gdn_A_log",
        "gdn_dt_bias", "gdn_norm_g", "gdn_w_out", "sc_w_in", "sc_conv_w", "sc_w_out", "moe_w_group",
        "moe_b_group", "moe_w_router", "moe_b_router", "moe_w_gate", "moe_w_up", "moe_w_down"]


def kernel(**inputs):
    import numpy as _np
    import concourse.bacc as _bacc
    from concourse import mybir as _mybir
    from concourse.bass_utils import run_bass_kernel_spmd as _run

    nc = _bacc.Bacc("TRN2", target_bir_lowering=False, num_devices=1)
    arrays, aps = {}, {}
    for name in _INS:
        a = _np.ascontiguousarray(inputs[name])
        arrays[f"in_{name}_dram"] = a
        aps[name] = nc.dram_tensor(f"in_{name}_dram", a.shape, _mybir.dt.from_np(a.dtype), kind="ExternalInput").ap()
    S_, cv_, sc_ = inputs["state_gdn_S"].shape, inputs["state_gdn_conv"].shape, inputs["state_sconv"].shape
    B = inputs["x_prompt"].shape[0]
    shapes = [inputs["x_prompt"].shape, inputs["x_sample"].shape, (S_[0], B) + S_[2:], (cv_[0], B) + cv_[2:],
              (sc_[0], B) + sc_[2:], S_, cv_, sc_]
    outs = [nc.dram_tensor(f"out_{i}_dram", tuple(s), _mybir.dt.float32, kind="ExternalOutput").ap()
            for i, s in enumerate(shapes)]
    hybrid_step(nc, aps, outs)
    r = _run(nc, [arrays], core_ids=[0])
    return tuple(r.results[0][f"out_{i}_dram"] for i in range(len(shapes)))
```
